# Optimizing a Trainium2 kernel written in Bass

```python
import jax, jax.numpy as jnp
from jax import lax
import numpy as np

D_MODEL = 1024
BATCH = 1
SEQ = 1024
DEPTH = 1
DEC_BATCH = 8
DEC_SEQ = 1
PAST_LEN = 8192
PAGE_SIZE = 128

CONV_W = D_MODEL // 2
CONV_K = 3
GLA_HEADS = 4
GLA_V = D_MODEL // 2
GLA_K = GLA_V // 2
GLA_DK = GLA_K // GLA_HEADS
GLA_DV = GLA_V // GLA_HEADS
GLA_RANK = 16
GLA_TAU = 16.0
GLA_CHUNK = 64
MIX_W = CONV_W + GLA_V
IN_COLS = 3 * CONV_W + 2 * GLA_K + 2 * GLA_V + GLA_RANK
IN_SPLITS = (CONV_W, 2 * CONV_W, 3 * CONV_W, 3 * CONV_W + GLA_K, 3 * CONV_W + 2 * GLA_K,
             3 * CONV_W + 2 * GLA_K + GLA_V, 3 * CONV_W + 2 * GLA_K + 2 * GLA_V)
N_MEM = 256
MEM_HEADS = 4
MEM_DH = D_MODEL // MEM_HEADS
N_GROUPS = 4
EXP_PER_GROUP = 4
N_EXPERTS = N_GROUPS * EXP_PER_GROUP
TOP_K_INNER = 2
EXPERT_FF = 256
EPS = 1e-6

kernel_name = "hymba_conv_gla_hiermoe_step"

def rmsnorm(x, g):
    xf = x.astype(jnp.float32)
    y = xf * lax.rsqrt(jnp.mean(xf * xf, axis=-1, keepdims=True) + EPS)
    return (y * g.astype(jnp.float32)).astype(x.dtype)

def short_conv(u, buf, w):
    full = jnp.concatenate([buf.astype(u.dtype), u], axis=1)
    T = u.shape[1]
    y = full[:, 0:T] * w[0]
    for j in range(1, CONV_K):
        y = y + full[:, j:j + T] * w[j]
    return y, full[:, -(CONV_K - 1):]

def gla_chunked(q, k, v, log_a, s0):
    Bn, T, H, dk = q.shape
    dv = v.shape[-1]
    c = min(GLA_CHUNK, T)
    pad = (-T) % c
    Tp = T + pad
    n = Tp // c

    def blocks(a):
        a = jnp.pad(a.astype(jnp.float32), ((0, 0), (0, pad), (0, 0), (0, 0)))
        return a.reshape(Bn, n, c, H, a.shape[-1]).transpose(0, 3, 1, 2, 4)

    qf = blocks(q) * (dk ** -0.5)
    kf, vf, la = blocks(k), blocks(v), blocks(log_a)
    b = jnp.cumsum(la, axis=3)
    b_mid = b[:, :, :, c // 2:c // 2 + 1, :]
    q_i = qf * jnp.exp(b - b_mid)
    k_i = kf * jnp.exp(b_mid - b)
    A = jnp.einsum('bhnid,bhnjd->bhnij', q_i, k_i)
    causal = jnp.tril(jnp.ones((c, c), dtype=bool))
    A = jnp.where(causal, A, 0.0)
    o_intra = jnp.einsum('bhnij,bhnjv->bhniv', A, vf)
    b_last = b[:, :, :, -1, :]
    k_dec = kf * jnp.exp(b_last[:, :, :, None, :] - b)
    dS = jnp.einsum('bhncd,bhncv->bhndv', k_dec, vf)
    decay = jnp.exp(b_last)

    def step(S, inp):
        dS_n, dec_n = inp
        return dec_n[..., None] * S + dS_n, S

    s_final, s_prev = lax.scan(step, s0.astype(jnp.float32),
                               (jnp.moveaxis(dS, 2, 0), jnp.moveaxis(decay, 2, 0)))
    s_prev = jnp.moveaxis(s_prev, 0, 2)
    o_inter = jnp.einsum('bhncd,bhndv->bhncv', qf * jnp.exp(b), s_prev)
    o = (o_intra + o_inter).transpose(0, 2, 3, 1, 4).reshape(Bn, Tp, H, dv)[:, :T]
    return o, s_final

def token_mixer(h, conv_buf, s0, w_in, conv_w, gate_up, gate_b, gla_g, w_out):
    Bn, T, _ = h.shape
    proj = h @ w_in
    cb, cc, ch, q, k, v, g, lr = jnp.split(proj, IN_SPLITS, axis=-1)
    uc, new_buf = short_conv(cc * ch, conv_buf, conv_w)
    y_conv = cb * uc
    log_a = jax.nn.log_sigmoid((lr @ gate_up + gate_b).astype(jnp.float32)) / GLA_TAU
    o, s_new = gla_chunked(q.reshape(Bn, T, GLA_HEADS, GLA_DK), k.reshape(Bn, T, GLA_HEADS, GLA_DK),
                           v.reshape(Bn, T, GLA_HEADS, GLA_DV), log_a.reshape(Bn, T, GLA_HEADS, GLA_DK), s0)
    o = rmsnorm(o, gla_g.reshape(GLA_HEADS, GLA_DV)).reshape(Bn, T, GLA_V)
    y_gla = (o * jax.nn.silu(g.astype(jnp.float32))).astype(h.dtype)
    y = jnp.concatenate([y_conv, y_gla], axis=-1) @ w_out
    return y, new_buf, s_new

def mem_kv(mem, w_k, w_v):
    Bn = mem.shape[0]
    mk = (mem @ w_k).reshape(Bn, N_MEM, MEM_HEADS, MEM_DH)
    mv = (mem @ w_v).reshape(Bn, N_MEM, MEM_HEADS, MEM_DH)
    return mk, mv

def mem_attend(h, mk, mv, w_q, w_o):
    Bn, T, _ = h.shape
    q = (h @ w_q).reshape(Bn, T, MEM_HEADS, MEM_DH)
    s = jnp.einsum('bthd,bmhd->bhtm', q, mk.astype(q.dtype)).astype(jnp.float32) * (MEM_DH ** -0.5)
    p = jax.nn.softmax(s, axis=-1).astype(h.dtype)
    o = jnp.einsum('bhtm,bmhd->bthd', p, mv.astype(h.dtype)).reshape(Bn, T, D_MODEL)
    return o @ w_o

def hier_moe(h, r_g, r_gb, r_e, r_eb, w_gate, w_up, w_down):
    shp = h.shape
    xt = h.reshape(-1, D_MODEL)
    g_logits = (xt @ r_g).astype(jnp.float32) + r_gb.astype(jnp.float32)
    g_prob = jax.nn.softmax(g_logits, axis=-1)
    g_idx = jnp.argmax(g_logits, axis=-1)
    g_w = jnp.take_along_axis(g_prob, g_idx[:, None], axis=1)[:, 0]
    e_logits = jnp.einsum('nd,gde->nge', xt, r_e).astype(jnp.float32) + r_eb.astype(jnp.float32)
    e_sel = jnp.take_along_axis(e_logits, g_idx[:, None, None], axis=1)[:, 0]
    top_v, top_i = lax.top_k(e_sel, TOP_K_INNER)
    top_w = jax.nn.softmax(top_v, axis=-1) * g_w[:, None]
    expert_id = g_idx[:, None] * EXP_PER_GROUP + top_i
    combine = jnp.sum(jax.nn.one_hot(expert_id, N_EXPERTS, dtype=jnp.float32) * top_w[..., None], axis=1)
    hid = jax.nn.silu(jnp.einsum('nd,edf->nef', xt, w_gate)) * jnp.einsum('nd,edf->nef', xt, w_up)
    hid = hid * combine.astype(hid.dtype)[..., None]
    y = jnp.einsum('nef,efd->nd', hid, w_down)
    return y.reshape(shp)

def layer(x, conv_buf, s0, mk, mv, nm, wi, cw, gu, gb, gn, wo, nmem, wq, wom, nf, rg, rgb, re, reb, wg, wu, wd):
    y, new_buf, s_new = token_mixer(rmsnorm(x, nm), conv_buf, s0, wi, cw, gu, gb, gn, wo)
    x = x + y
    x = x + mem_attend(rmsnorm(x, nmem), mk, mv, wq, wom)
    x = x + hier_moe(rmsnorm(x, nf), rg, rgb, re, reb, wg, wu, wd)
    return x, new_buf, s_new

def setup_inputs(seed: int = 0) -> dict:
    key = jax.random.key(seed)
    ks = jax.random.split(key, 32)
    f32 = jnp.float32

    def nrm(k, shape, scale):
        return jax.random.normal(k, shape, f32) * scale

    def gain(k, shape):
        return 1.0 + 0.02 * jax.random.normal(k, shape, f32)

    return {
        "x_prompt": nrm(ks[0], (BATCH, SEQ, D_MODEL), 1.0),
        "x_sample": nrm(ks[1], (DEC_BATCH, DEC_SEQ, D_MODEL), 1.0),
        "state_conv": nrm(ks[2], (DEPTH, DEC_BATCH, CONV_K - 1, CONV_W), 1.0),
        "state_gla": nrm(ks[3], (DEPTH, DEC_BATCH, GLA_HEADS, GLA_DK, GLA_DV), 1.0),
        "cache_mem_k": nrm(ks[4], (DEPTH, DEC_BATCH, N_MEM, MEM_HEADS, MEM_DH), 1.0),
        "cache_mem_v": nrm(ks[5], (DEPTH, DEC_BATCH, N_MEM, MEM_HEADS, MEM_DH), 1.0),
        "mem_prompt": nrm(ks[6], (BATCH, N_MEM, D_MODEL), 1.0),
        "norm_mix": gain(ks[7], (DEPTH, D_MODEL)),
        "w_in": nrm(ks[8], (DEPTH, D_MODEL, IN_COLS), D_MODEL ** -0.5),
        "conv_w": nrm(ks[9], (DEPTH, CONV_K, CONV_W), CONV_K ** -0.5),
        "gla_gate_up": nrm(ks[10], (DEPTH, GLA_RANK, GLA_K), GLA_RANK ** -0.5),
        "gla_gate_b": nrm(ks[11], (DEPTH, GLA_K), 0.1),
        "gla_out_norm": gain(ks[12], (DEPTH, GLA_V)),
        "w_out": nrm(ks[13], (DEPTH, MIX_W, D_MODEL), MIX_W ** -0.5),
        "norm_mem": gain(ks[14], (DEPTH, D_MODEL)),
        "w_q": nrm(ks[15], (DEPTH, D_MODEL, D_MODEL), D_MODEL ** -0.5),
        "w_k": nrm(ks[16], (DEPTH, D_MODEL, D_MODEL), D_MODEL ** -0.5),
        "w_v": nrm(ks[17], (DEPTH, D_MODEL, D_MODEL), D_MODEL ** -0.5),
        "w_o": nrm(ks[18], (DEPTH, D_MODEL, D_MODEL), D_MODEL ** -0.5),
        "norm_ffn": gain(ks[19], (DEPTH, D_MODEL)),
        "router_group": nrm(ks[20], (DEPTH, D_MODEL, N_GROUPS), D_MODEL ** -0.5),
        "router_group_b": nrm(ks[21], (DEPTH, N_GROUPS), 0.01),
        "router_expert": nrm(ks[22], (DEPTH, N_GROUPS, D_MODEL, EXP_PER_GROUP), D_MODEL ** -0.5),
        "router_expert_b": nrm(ks[23], (DEPTH, N_GROUPS, EXP_PER_GROUP), 0.01),
        "w_gate": nrm(ks[24], (DEPTH, N_EXPERTS, D_MODEL, EXPERT_FF), D_MODEL ** -0.5),
        "w_up": nrm(ks[25], (DEPTH, N_EXPERTS, D_MODEL, EXPERT_FF), D_MODEL ** -0.5),
        "w_down": nrm(ks[26], (DEPTH, N_EXPERTS, EXPERT_FF, D_MODEL), EXPERT_FF ** -0.5),
        "norm_final": gain(ks[27], (D_MODEL,)),
    }

def reference(x_prompt, x_sample, state_conv, state_gla, cache_mem_k, cache_mem_v, mem_prompt,
              norm_mix, w_in, conv_w, gla_gate_up, gla_gate_b, gla_out_norm, w_out,
              norm_mem, w_q, w_k, w_v, w_o, norm_ffn, router_group, router_group_b,
              router_expert, router_expert_b, w_gate, w_up, w_down, norm_final):
    xp, xs = x_prompt, x_sample
    conv_p, gla_p, mk_p, mv_p, conv_s, gla_s = [], [], [], [], [], []
    for l in range(DEPTH):
        wl = (norm_mix[l], w_in[l], conv_w[l], gla_gate_up[l], gla_gate_b[l], gla_out_norm[l], w_out[l],
              norm_mem[l], w_q[l], w_o[l], norm_ffn[l], router_group[l], router_group_b[l],
              router_expert[l], router_expert_b[l], w_gate[l], w_up[l], w_down[l])
        mk, mv = mem_kv(mem_prompt, w_k[l], w_v[l])
        buf0 = jnp.zeros((xp.shape[0], CONV_K - 1, CONV_W), xp.dtype)
        s00 = jnp.zeros((xp.shape[0], GLA_HEADS, GLA_DK, GLA_DV), jnp.float32)
        xp, nb, ns = layer(xp, buf0, s00, mk, mv, *wl)
        conv_p.append(nb)
        gla_p.append(ns)
        mk_p.append(mk)
        mv_p.append(mv)
        xs, nb, ns = layer(xs, state_conv[l], state_gla[l].astype(jnp.float32),
                           cache_mem_k[l], cache_mem_v[l], *wl)
        conv_s.append(nb)
        gla_s.append(ns)
    y_prompt = rmsnorm(xp, norm_final)
    y_sample = rmsnorm(xs, norm_final)
    return (y_prompt, y_sample, jnp.stack(conv_p), jnp.stack(gla_p), jnp.stack(mk_p), jnp.stack(mv_p),
            jnp.stack(conv_s), jnp.stack(gla_s))


_drawn_inputs = setup_inputs


def setup_inputs(seed=0):
    import zlib

    import numpy as np

    out = dict(_drawn_inputs(seed))
    spreads = {}
    factors = {'gla_out_norm': 3.994,
     'norm_mem': 8.0,
     'router_group_b': 55.706,
     'router_expert_b': 36.369,
     'norm_final': 9.638,
     'norm_ffn': 4.306}
    for name, (base, spread) in spreads.items():
        noise = np.random.default_rng([zlib.crc32(name.encode()), seed]).standard_normal(out[name].shape)
        drawn = base * np.exp(spread * noise) if base else spread * noise
        out[name] = __import__('jax').numpy.asarray(drawn.astype(out[name].dtype))
    for name, factor in factors.items():
        out[name] = (out[name] * factor).astype(out[name].dtype)
    return out
```

```python
from contextlib import ExitStack

import concourse.bass as bass
from concourse import mybir

F32 = mybir.dt.float32
F32R = mybir.dt.float32r
BF16 = mybir.dt.bfloat16
I32 = mybir.dt.int32
U32 = mybir.dt.uint32
ALU = mybir.AluOpType
ACT = mybir.ActivationFunctionType
AX = mybir.AxisListType

P = 128


def build(nc, x_prompt, x_sample, state_conv, state_gla, cache_mem_k, cache_mem_v, mem_prompt,
          norm_mix, w_in, conv_w, gla_gate_up, gla_gate_b, gla_out_norm, w_out,
          norm_mem, w_q, w_k, w_v, w_o, norm_ffn, router_group, router_group_b,
          router_expert, router_expert_b, w_gate, w_up, w_down, norm_final,
          y_prompt, y_sample, new_conv_p, new_gla_p, new_mk, new_mv, new_conv_s, new_gla_s):
    D = x_prompt.shape[2]
    KB = D // P
    SEQ = x_prompt.shape[1]
    DB = x_sample.shape[0]
    NT = SEQ // P
    TILES = NT + 1
    COLS = SEQ + DB
    NCH = 3
    CH = COLS // NCH
    CONV = conv_w.shape[2]
    CB = CONV // P
    HEADS, DK, DV = 4, 64, 128
    QB = HEADS * DK // P
    VB = HEADS * DV // P
    CHUNK = 64
    NCK = SEQ // CHUNK
    MEM = mem_prompt.shape[1]
    MB = MEM // P
    MH, DH = 4, D // 4
    NG, EG = 4, 4
    NE = NG * EG
    FF = w_gate.shape[3]
    EPS = 1e-6
    STEPS = 2 * COLS // P + NE
    NSLOT = STEPS * P
    LEAST = COLS // P
    PAD = 1 << 14
    WR = 3
    rows = [P] * NT + [DB]

    win = w_in[0]
    c_q, c_k = 3 * CONV, 3 * CONV + QB * P
    c_v, c_g = c_k + QB * P, c_k + QB * P + VB * P
    c_lr = c_g + VB * P
    blocks, kinds = [], []

    def add(kind, i, w, c0, n=P):
        blocks.append((w, c0, n))
        kinds.append((kind, i))

    for i in range(KB):
        add("memk", i, w_k[0], i * P)
    for i in range(KB):
        add("memv", i, w_v[0], i * P)
    for i in range(CB):
        add("cc", i, win, CONV + i * P)
        add("ch", i, win, 2 * CONV + i * P)
        add("cb", i, win, i * P)
    add("lr", 0, win, c_lr, 16)
    for i in range(QB):
        add("q", i, win, c_q + i * P)
    for i in range(QB):
        add("k", i, win, c_k + i * P)
    for i in range(VB):
        add("v", i, win, c_v + i * P)
    for i in range(VB):
        add("g", i, win, c_g + i * P)
    for i in range(KB):
        add("out", i, w_out[0], i * P)
    for i in range(KB):
        add("mq", i, w_q[0], i * P)
    for i in range(KB):
        add("o", i, w_o[0], i * P)
    NBLK = len(blocks)
    at = {k: n for n, k in enumerate(kinds)}
    Z0 = at[("q", 0)] + 1
    def use(n):
        return n if n < Z0 else n + QB
    def use_z(i):
        return Z0 + i

    order = [("mem", t) for t in range(MB)]
    early = [("norm", t) for t in range(2, TILES)]
    for n in range(2 * KB):
        order.append(("block", n))
        if n >= 2 and n % 2 == 0 and early:
            order.append(early.pop(0))
    order += early + [("memout", 0), ("norm", 0), ("norm", 1)]
    for n in range(2 * KB, at[("g", 0)]):
        order.append(("block", n))
        k, i = kinds[n]
        if k == "cb":
            order.append(("convstate", i))
        if (k, i) == ("q", 0):
            order.append(("gate", 0))
        if (k, i) == ("k", QB - 1):
            order.append(("prep", 0))
            order.append(("prep", 1))
        if k == "v":
            order.append(("vT", i))
    gla_at = 0
    for i in range(VB):
        order.append(("block", at[("g", i)]))
        for _ in range(NT // VB):
            order.append(("gla", gla_at))
            gla_at += 1
    order += [("glasample", 0), ("ysplit", 0)]
    for i in range(KB):
        order.append(("block", at[("out", i)]))
    order += [("norm", TILES + t) for t in range(TILES)]
    for i in range(KB):
        order.append(("block", at[("mq", i)]))
    order += [("sq", 0)]
    order += [("att", t) for t in range(NT // 2)]
    order += [("smax", 0), ("pv", 0), ("sprob", 0)]
    order += [("att", NT // 2 + t) for t in range(NT // 2)]
    order += [("sout", 0), ("pv", 1)]
    PER = DB // (NT // 2)
    for i in range(KB):
        order.append(("block", at[("o", i)]))
    order += [("norm", 2 * TILES + t) for t in range(TILES)]
    norm_seq = [i for k, i in order if k == "norm"]
    nseq = {i: j for j, i in enumerate(norm_seq)}

    ctx = ExitStack()
    with ctx:
        def sb(name, shape, dt=F32):
            return ctx.enter_context(nc.sbuf_tensor(name, shape, dt))

        def pb(name, shape, dt=F32):
            return ctx.enter_context(nc.psum_tensor(name, shape, dt))

        def sem(name):
            return ctx.enter_context(nc.semaphore(name))

        def dram(name, shape, dt=F32):
            return nc.dram_tensor(name, shape, dt, kind="Internal").ap()

        d_yc = dram("d_yc", [CB, P, COLS])
        d_mkT = dram("d_mkT", [P, KB * MEM])
        d_x1 = dram("d_x1", [COLS, D])
        d_x2 = dram("d_x2", [COLS, D])
        d_h3 = dram("d_h3", [COLS, D])
        d_y = dram("d_y", [2 * COLS, D])
        d_list = dram("d_list", [NSLOT, 1], I32)

        act_hi = sb("act_hi", [P, KB, COLS], F32R)
        act_lo = sb("act_lo", [P, KB, COLS], F32R)
        w_hi = sb("w_hi", [P, 2, KB, P], F32R)
        w_lo = sb("w_lo", [P, 2, KB, P], F32R)
        RAW = 3
        sizes = dict(feat=KB * COLS, vtm=TILES * VB * P, qk=2 * QB * COLS, zb=QB * COLS, tmp=4 * (COLS + 2),
                     qe=QB * SEQ, raw=RAW * KB * P, S=4 * QB * DV)
        base, tot = {}, 0
        for k, n in sizes.items():
            base[k] = tot
            tot += n
        arena = sb("arena", [P, tot])

        def region(k, off=0, n=None, parts=P):
            n = sizes[k] - off if n is None else n
            assert off + n <= sizes[k], (k, off, n)
            return arena[0:parts, base[k] + off:base[k] + off + n]

        ident = sb("ident", [P, P])
        ones = sb("ones", [P, P])
        tri = sb("tri", [P, P])
        cmask = sb("cmask", [P, P])
        smask = sb("smask", [P, SEQ], BF16)
        cw = sb("cw", [P, CB, 3])
        gateb = sb("gateb", [P, QB])
        glag = sb("glag", [P, VB])
        gup = sb("gup", [16, QB * P])
        rw = sb("rw", [P, KB, 20])
        rb = sb("rb", [P, 20])
        stT = sb("stT", [P, CB, 2 * DB])
        epsb = sb("epsb", [P, 1])
        sst = sb("sst", [DB * MH, 4])
        smx = sb("smx", [P, 2, 4, MH])
        ksc = sb("ksc", [P, MB, DB * MH])
        pTs = sb("pTs", [P, MB, DB * MH])
        sps = sb("sps", [DB * MH, MEM])
        ssum = sb("ssum", [P, 3 * TILES + TILES, 4])
        dec = sb("dec", [P, QB, NCK])
        adec = sb("adec", [P, QB, DB])
        L = sb("L", [P, TILES, 20])

        raw = region("raw").rearrange("p (s k n) -> p s k n", s=RAW, k=KB)
        feat = region("feat").rearrange("p (k n) -> p k n", k=KB)
        vtm = region("vtm").rearrange("p (t n) -> p t n", t=TILES)
        qT = region("qk", 0, QB * COLS).rearrange("p (k n) -> p k n", k=QB)
        kT = region("qk", QB * COLS).rearrange("p (k n) -> p k n", k=QB)
        zT = region("zb").rearrange("p (k n) -> p k n", k=QB)
        qe = region("qe").rearrange("p (k n) -> p k n", k=QB)
        S = region("S").rearrange("p (s k v) -> p s k v", s=4, k=QB)
        gain = region("qe", 0, D)
        TW = COLS + 2
        tmp = [region("tmp", i * TW, TW) for i in range(4)]
        xb = [region("tmp", i * TW, D) for i in range(2)]
        hb = [region("tmp", (2 + i) * TW, D) for i in range(2)]
        lrT = region("qk", 3 * COLS, COLS, 16)
        TW = COLS + 2
        S0 = region("qe").rearrange("p (k b v) -> p k b v", k=QB, b=DB)
        KV = region("zb", 0, QB * DB * DV).rearrange("p (k b v) -> p k b v", k=QB, b=DB)
        sel_g = region("tmp", 3 * (COLS + 2), DB * P, DB).rearrange("q (b p) -> q b p", b=DB)
        sel_a = region("qe", D, DB * P, DB).rearrange("q (b p) -> q b p", b=DB)
        qs = region("S", 0, D, DB)
        cache = [region("tmp", i * MB * D, MB * D).rearrange("p (m d) -> p m d", m=MB) for i in range(2)]
        mkT = region("vtm", 0, KB * MEM).rearrange("p (k m) -> p k m", k=KB)
        mv_sb = region("vtm", KB * MEM, MB * D).rearrange("p (m d) -> p m d", m=MB)
        kprod = region("vtm", KB * MEM + MB * D, DH)
        HT = SEQ // 2
        Am = [region("tmp", i * HEADS * P, HEADS * P).rearrange("p (q k n) -> p q k n", q=2, k=QB) for i in range(2)]
        gsq = region("tmp", TW, HEADS * P)
        grt = region("tmp", TW + HEADS * P, HEADS * P)
        kdt = [region("tmp", 2 * TW + i * QB * P, QB * P) for i in range(2)]
        pT = region("qk", 0, MH * MB * HT).rearrange("p (e n) -> p e n", e=MH * MB)
        pr = [region("zb", i * MH * MEM, MH * MEM).rearrange("p (h m) -> p h m", h=MH) for i in range(2)]
        h3T = [region("zb", i * D, D).rearrange("p (k n) -> p k n", k=KB) for i in range(2)]

        G = [pb("G0", [P, 3, 512]), pb("G1", [P, 3, 512])]
        T = pb("T", [P, 2, 512])
        lower4 = T[:, :, 0:QB * P].rearrange("p q (k n) -> p q k n", k=QB)
        fwd = [T[:, :, :], G[0][:, 1:3, :]]
        back = G[1][:, 1:3, :]

        names = """const_in ident_rdy ones_rdy masks_rdy raw_in0 raw_in1 raw_in2 hi_done split_done big_done free0 free1
        x_in0 x_in1 gain_in h_done sq_done ms_done rt_done fwd_done nhi_done nlo_done x_out0 x_out1 h_out0 h_out1 back_done res_done
        mem_in mk_spill mem_tm_tr mem_tm_ev mem_out
        st_in st_tr st_ev y_sp us_tr us_ev cs_out z_abs z_ln la_done
        p_d1 p_d2 p_e p_m p_x prep_done v_tr vt_ev
        a_mm a_kd a_cp a_kdt a_ds a_S a_o a_oev a_sq a_ms a_rt a_norm
        gs_in gs_bc gs_kv gs_a gs_sn gs_o gs_oev gs_sq gs_ms gs_rt gs_out yc_in yg_done ys_hi ys_lo
        mk_in mv_in s_mm s_mx s_e s_p s_tr s_pT s_pv s_pvhi s_pvlo
        kc_in0 kc_in1 vc_in0 vc_in1 q_tr q_ev q_bc q_sc q_t2 q_mx q_ex q_pn q_t3 q_pT q_o q_ohi q_olo
        r_mm r_L r_ge r_gexp r_d r_dexp r_M r_rank r_slot r_tab iota_rdy l_init l_st l_sc l_in l_f l_tr l_ids
        wt_in0 wt_in1 wt_in2 wt_rdy moe_done xg_in0 xg_in1 tx_done hT_rdy gu_done sg_done hid_done ht_done hidT_rdy y_rdy y_out0 y_out1 xg_z
        c_gain c_in0 c_in1 c_y c_sq c_ms c_rt c_h c_out0 c_out1 a_ch d_ch g_ch""".split()
        s = {n: sem(n) for n in names}
        raw_in = [s["raw_in0"], s["raw_in1"], s["raw_in2"]]
        free = [s["free0"], s["free1"]]
        x_in = [s["x_in0"], s["x_in1"]]
        N_CONST = 0

        x_out = [s["x_out0"], s["x_out1"]]
        h_out = [s["h_out0"], s["h_out1"]]

        def wait_x_out(eng, j):
            eng.wait_ge(x_out[j % 2], 16 * len([i for i in range(TILES, j + 1) if i % 2 == j % 2]))

        def wait_h_out(eng, j):
            eng.wait_ge(h_out[j % 2], 16 * len([i for i in range(2 * TILES, j + 1) if i % 2 == j % 2]))

        def spare(t):
            return G[use(at[("g", t // (NT // VB))]) % 2]

        def wait_read(eng, n):
            eng.wait_ge(free[use(n) % 2], use(n) // 2 + 1)

        def wait_free(eng, n):
            u = use(n)
            for v in (u, u - 1):
                eng.wait_ge(free[v % 2], v // 2 + 1)

        links = {}

        def chain(eng, sm):
            count = [0]

            def link(ins):
                count[0] += 1
                ins.then_inc(sm, 1)
                eng.wait_ge(sm, count[0])
            return link

        def group(n):
            return G[use(n) % 2]

        def chunks(ap):
            return ap.rearrange("p (c n) -> p c n", c=NCH)

        xrows = [x_prompt[0, t * P:(t + 1) * P, :] for t in range(NT)] + [x_sample[:, 0, :]]
        yrows = [y_prompt[0, t * P:(t + 1) * P, :] for t in range(NT)] + [y_sample[:, 0, :]]

        def drows(d, t):
            return d[t * P:t * P + rows[t], :]

        const_loads = [
            (gateb[:, :], gla_gate_b[0].rearrange("(k p) -> p k", p=P)),
            (glag[:, :], gla_out_norm[0].rearrange("(k p) -> p k", p=P)),
            (gup[:, :], gla_gate_up[0]),
            (rw[:, :, 0:NG], router_group[0].rearrange("(k p) g -> p k g", p=P)),
            (rb[:, 0:NG], router_group_b[0].partition_broadcast(P)),
            (rb[:, NG:NG + NE], router_expert_b[0].rearrange("g e -> (g e)").partition_broadcast(P)),
        ] + [(rw[:, :, NG + g * EG:NG + (g + 1) * EG], router_expert[0, g].rearrange("(k p) e -> p k e", p=P)) for g in range(NG)] + [
            (cw[:, :, j], conv_w[0, j].rearrange("(k p) -> p k", p=P)) for j in range(3)]
        N_CONST = 16 * len(const_loads)
        memx = region("vtm", 0, MB * D).rearrange("p (m d) -> p m d", m=MB)
        mkT_w = region("vtm", MB * D, KB * MEM).rearrange("p (k m) -> p k m", k=KB)
        mvT_w = region("qk", 0, KB * MEM).rearrange("p (k m) -> p k m", k=KB)
        mtm = [region("qk", KB * MEM, MB * D).rearrange("p (m d) -> p m d", m=MB),
               region("feat", 0, MB * D).rearrange("p (m d) -> p m d", m=MB)]
        strow = region("feat", MB * D, CONV, 2 * DB)
        csrow = region("feat", MB * D + CONV, CONV, 2 + DB)

        WSZ = KB * 2 * FF + (FF // P) * D
        o = WR * WSZ
        def take(n):
            nonlocal_o[0] += n
            return arena[:, nonlocal_o[0] - n:nonlocal_o[0]]
        nonlocal_o = [o]
        xg = [take(D) for _ in range(2)]
        hT = [take(D).rearrange("p (k n) -> p k n", k=KB) for _ in range(2)]
        sg = [take(FF) for _ in range(2)]
        hid = [take(FF) for _ in range(2)]
        hidT = [take(FF).rearrange("p (k n) -> p k n", k=FF // P) for _ in range(2)]
        yb = [take(D) for _ in range(2)]
        NTE = TILES * NE
        def t3(ap, a):
            return ap.rearrange("p (a b) -> p a b", a=a)
        M = t3(take(NTE), TILES)
        OH1 = t3(take(NTE), TILES)
        OH2 = t3(take(NTE), TILES)
        prod = t3(take(NTE), TILES)
        slotA = t3(take(NTE), TILES)
        totE = take(NTE)
        incE = take(NTE)
        tmask = take(NTE)
        cmp_ = t3(take(STEPS * NE), STEPS)
        ohg, oh1, oh2 = (t3(take(TILES * NG), TILES) for _ in range(3))
        esel, e2, ww, ee = (t3(take(TILES * EG), TILES) for _ in range(4))
        cj = take(NG)
        valid, gmx, wmx, gsm, m1, m2, dlt, wt1, wt2, slf = (take(TILES) for _ in range(10))
        tcnt, tend, tbase, one16 = (take(NE) for _ in range(4))
        stepf, est, em3, ec = (take(STEPS) for _ in range(4))
        lf = take(P)
        assert nonlocal_o[0] <= tot, (nonlocal_o, tot)
        slot = sb("slot", [P, 2, TILES], I32)
        rid = sb("rid", [P, TILES, 2], I32)
        stepi = sb("stepi", [P, STEPS], I32)
        tci = sb("tci", [P, NE], I32)
        tab_off = sb("tab_off", [P, STEPS], I32)
        tab_need = sb("tab_need", [P, STEPS], I32)
        tab_end = sb("tab_end", [P, NE], I32)
        tab_last = sb("tab_last", [P, 2], I32)
        tab_pairs = sb("tab_pairs", [P, 1], I32)
        lrow = sb("lrow", [STEPS, P], I32)
        ridx = sb("ridx", [P, STEPS], I32)
        tidx = sb("tidx", [P, STEPS], I32)
        wcol = sb("wcol", [P, 2, TILES])
        cst = sb("cst", [P, TILES, 4])
        GU = [G[0][:, 0, :], G[1][:, 0, :]]
        XT = T
        HTp = G[0][:, 1, 0:FF].rearrange("p (k n) -> p k n", k=FF // P)
        Y = G[1][:, 1:3, :]
        cy = [arena[:, i * 2 * D:(i + 1) * 2 * D].rearrange("p (r d) -> p r d", r=2) for i in range(2)]
        cx = [arena[:, (4 + i) * D:(5 + i) * D] for i in range(2)]
        cg = arena[:, 6 * D:7 * D]
        co = [arena[:, (7 + i) * D:(8 + i) * D] for i in range(2)]
        wt_in = [s["wt_in0"], s["wt_in1"], s["wt_in2"]]

        def step_pairs(eng):
            return eng.value_load(tab_pairs[0:1, 0:1], min_val=0, max_val=STEPS // 2 - LEAST) + LEAST

        def sp_moe(sp):
            def load_expert(e):
                wv = arena[:, (e % WR) * WSZ:(e % WR + 1) * WSZ]
                gu = wv[:, 0:KB * 2 * FF].rearrange("p (k a f) -> p k a f", k=KB, a=2)
                sp.dma_start(gu[:, :, 0, :], w_gate[0, e].rearrange("(k p) f -> p k f", p=P)).then_inc(wt_in[e % WR], 16)
                sp.dma_start(gu[:, :, 1, :], w_up[0, e].rearrange("(k p) f -> p k f", p=P)).then_inc(wt_in[e % WR], 16)
                sp.dma_start(wv[:, KB * 2 * FF:].rearrange("p (k d) -> p k d", k=FF // P),
                             w_down[0, e].rearrange("(k p) d -> p k d", p=P)).then_inc(wt_in[e % WR], 16)

            def arrived(e):
                sp.wait_ge(wt_in[e % WR], 48 * (e // WR + 1))
                sp.sem_inc(s["wt_rdy"], 1)

            sp.wait_ge(s["l_st"], 1)
            sp.dma_start(d_list.rearrange("(a b) o -> a (b o)", a=STEPS), lrow[:, :]).then_inc(s["l_init"], 16)
            sp.wait_ge(s["r_mm"], TILES)
            sp.wait_ge(s["r_L"], TILES)
            for e in range(WR):
                load_expert(e)
            sp.wait_ge(s["l_sc"], 16 * 2 * TILES)
            sp.dma_start(lrow[:, :], d_list.rearrange("(a b) o -> a (b o)", a=STEPS)).then_inc(s["l_in"], 16)
            sp.wait_ge(s["r_tab"], 1)
            arrived(0)
            for e in range(NE):
                if e + 1 < NE:
                    arrived(e + 1)
                if e + WR < NE:
                    end = sp.value_load(tab_end[0:1, e:e + 1], min_val=1, max_val=STEPS + 1)
                    sp.wait_ge(s["moe_done"], end)
                    load_expert(e + WR)
            steps_done = sp.value_load(tab_last[0:1, 0:1], min_val=2 * LEAST + 1, max_val=STEPS + 1)
            rows_out = sp.value_load(tab_last[0:1, 1:2], min_val=16 * LEAST, max_val=8 * STEPS)
            sp.wait_ge(s["moe_done"], steps_done)
            sp.wait_ge(s["y_out0"], rows_out)
            sp.wait_ge(s["y_out1"], rows_out)
            for t in (3 * TILES - 1, 3 * TILES - 2):
                wait_x_out(sp, t)
            sp.dma_start(cg, norm_final.partition_broadcast(P)).then_inc(s["c_gain"], 16)
            for t in range(TILES + 2):
                if t < TILES:
                    r = rows[t]
                    if t >= 2:
                        sp.wait_ge(s["c_h"], t - 1)
                    sp.dma_start(cy[t % 2][0:r], d_y[2 * t * P:2 * (t * P + r), :].rearrange("(p r) d -> p r d", r=2)).then_inc(s[f"c_in{t % 2}"], 16)
                    sp.dma_start(cx[t % 2][0:r, :], drows(d_x2, t)).then_inc(s[f"c_in{t % 2}"], 16)
                if t >= 2:
                    sp.wait_ge(s["c_h"], t - 1)
                    sp.dma_start(yrows[t - 2], co[t % 2][0:rows[t - 2], :]).then_inc(s[f"c_out{t % 2}"], 16)
            sp.wait_ge(s["c_out0"], 16 * len(range(0, TILES, 2)))
            sp.wait_ge(s["c_out1"], 16 * len(range(1, TILES, 2)))

        def pool_moe(pool):
            pool.iota(stepi[:, :], pattern=[[1, STEPS]], base=0, channel_multiplier=0)
            pool.iota(rid[:, :, :], pattern=[[2 * P, TILES], [1, 2]], base=0, channel_multiplier=2).then_inc(s["iota_rdy"], 1)
            pool.wait_ge(s["iota_rdy"], 1)
            pool.wait_ge(s["l_init"], 16)
            pool.wait_ge(s["r_slot"], 1)
            for t in range(TILES):
                for c in range(2):
                    r = rows[t]
                    pool.indirect_dma_start(out=d_list, out_offset=bass.IndirectOffsetOnAxis(ap=slot[0:r, c, t:t + 1].bitcast(U32), axis=0),
                                            in_=rid[0:r, t, c:c + 1], in_offset=None, bounds_check=NSLOT - 1,
                                            oob_is_err=False).then_inc(s["l_sc"], 16)
            pool.wait_ge(s["l_ids"], 1)
            wait_h_out(pool, 3 * TILES - 1)
            wait_h_out(pool, 3 * TILES - 2)
            pool.wait_ge(s["xg_z"], 1)

            def gather(t):
                if t >= 2:
                    pool.wait_ge(s["tx_done"], t - 1)
                pool.indirect_dma_start(out=xg[t % 2], out_offset=None, in_=d_h3,
                                        in_offset=bass.IndirectOffsetOnAxis(ap=tidx[:, t:t + 1].bitcast(U32), axis=0),
                                        bounds_check=COLS - 1, oob_is_err=False).then_inc(s[f"xg_in{t % 2}"], 16)

            def scatter(t):
                pool.wait_ge(s["y_rdy"], t + 1)
                pool.indirect_dma_start(out=d_y, out_offset=bass.IndirectOffsetOnAxis(ap=ridx[:, t:t + 1].bitcast(U32), axis=0),
                                        in_=yb[t % 2], in_offset=None, bounds_check=2 * COLS - 1,
                                        oob_is_err=False).then_inc(s[f"y_out{t % 2}"], 16)
            pairs = step_pairs(pool)
            gather(0)
            gather(1)
            gather(2)
            gather(3)
            for i in range(STEPS // 2):
                with pool.If(pairs > i):
                    scatter(2 * i)
                if 2 * i + 4 < STEPS:
                    with pool.If(pairs > i + 2):
                        gather(2 * i + 4)
                with pool.If(pairs > i):
                    scatter(2 * i + 1)
                if 2 * i + 4 < STEPS:
                    with pool.If(pairs > i + 2):
                        gather(2 * i + 5)

        def pe_moe(pe):
            pe.wait_ge(s["r_M"], 1)
            pe.matmul(T[:, 0, 0:NTE], tri[:, :], M.rearrange("p a b -> p (a b)"), start=True, stop=True)
            pe.matmul(T[:, 1, 0:NTE], ones[:, :], M.rearrange("p a b -> p (a b)"), start=True, stop=True).then_inc(s["r_rank"], 1)
            pe.wait_ge(s["l_f"], 1)
            pe.transpose(G[0][:, 2, 0:STEPS], lf[0:STEPS, :], ident[0:STEPS, 0:STEPS]).then_inc(s["l_tr"], 1)
            pe.wait_ge(s["r_tab"], 1)
            pe.nop().then_inc(s["moe_done"], 1)

            def transpose_rows(b, n_in, hT_used):
                pe.wait_ge(s[f"xg_in{b}"], n_in)
                pe.wait_ge(s["hT_rdy"], hT_used)
                for k in range(KB):
                    ins = pe.transpose(XT[:, k // 4, (k % 4) * P:(k % 4 + 1) * P], xg[b][:, k * P:(k + 1) * P], ident[:, :])
                ins.then_inc(s["tx_done"], 1)

            def gate_up(b, step, rdy):
                off = pe.value_load(tab_off[0:1, step], min_val=0, max_val=(WR - 1) * WSZ)
                need = pe.value_load(tab_need[0:1, step], min_val=1, max_val=NE)
                pe.wait_ge(s["wt_rdy"], need)
                pe.wait_ge(s["hT_rdy"], rdy)
                for k in range(KB):
                    ins = pe.matmul(GU[b], hT[b][:, k, :], arena[:, bass.ds(off + k * 2 * FF, 2 * FF)],
                                    start=(k == 0), stop=(k == KB - 1))
                ins.then_inc(s["gu_done"], 1)

            def hid_transpose(b, n):
                pe.wait_ge(s["hid_done"], n)
                for k in range(FF // P):
                    ins = pe.transpose(HTp[:, k, :], hid[b][:, k * P:(k + 1) * P], ident[:, :])
                ins.then_inc(s["ht_done"], 1)

            def down(b, step, n, y_used):
                off = pe.value_load(tab_off[0:1, step], min_val=0, max_val=(WR - 1) * WSZ)
                pe.wait_ge(s["hidT_rdy"], n)
                if y_used is not None:
                    pe.wait_ge(s["y_rdy"], y_used)
                for c in range(D // 512):
                    for k in range(FF // P):
                        ins = pe.matmul(Y[:, c, :], hidT[b][:, k, :],
                                        arena[:, bass.ds(off + KB * 2 * FF + k * D + c * 512, 512)],
                                        start=(k == 0), stop=(k == FF // P - 1))
                ins.then_inc(s["moe_done"], 1)

            pe.wait_ge(s["xg_in0"], 16)
            for k in range(KB):
                ins = pe.transpose(XT[:, k // 4, (k % 4) * P:(k % 4 + 1) * P], xg[0][:, k * P:(k + 1) * P], ident[:, :])
            ins.then_inc(s["tx_done"], 1)
            gate_up(0, slice(0, 1), 1)
            transpose_rows(1, 16, 1)
            hid_transpose(0, 1)
            for t in (1, 2):
                gate_up(t % 2, slice(t, t + 1), t + 1)
                transpose_rows(1 - t % 2, 32, t + 1)
                down(1 - t % 2, slice(t - 1, t), t, t - 1 if t > 1 else None)
                hid_transpose(t % 2, t + 1)
            pairs = step_pairs(pe)
            with pe.Fori(1, STEPS // 2 - 1) as it:
                with pe.If(it < pairs - 1):
                    for b in (1, 0):
                        t = 2 * it + (2 - b)
                        gate_up(b, bass.ds(t, 1), t + 1)
                        transpose_rows(1 - b, 16 * (it + 2), t + 1)
                        down(1 - b, bass.ds(t - 1, 1), t, t - 1)
                        hid_transpose(b, t + 1)
            t = 2 * pairs - 1
            gate_up(1, bass.ds(t, 1), t + 1)
            down(0, bass.ds(t - 1, 1), t, t - 1)
            hid_transpose(1, t + 1)
            down(1, bass.ds(t, 1), t + 1, t)

        def act_moe(act):
            act.wait_ge(s["r_ge"], 1)
            act.activation(ee, ee, ACT.Exp).then_inc(s["r_gexp"], 1)
            act.wait_ge(s["r_d"], 1)
            act.activation(dlt, dlt, ACT.Exp).then_inc(s["r_dexp"], 1)

            def rows_in(b, n):
                act.wait_ge(s["tx_done"], n)
                act.copy(hT[b], XT[:, :, :].rearrange("p a (k n) -> p (a k) n", n=P)).then_inc(s["hT_rdy"], 1)

            def gate(b, n):
                act.wait_ge(s["gu_done"], n)
                act.activation(sg[b], GU[b][:, 0:FF], ACT.Silu).then_inc(s["sg_done"], 1)

            def hidden(b, n):
                act.wait_ge(s["ht_done"], n)
                act.copy(hidT[b], HTp).then_inc(s["hidT_rdy"], 1)

            rows_in(0, 1)
            act.wait_ge(s["r_tab"], 1)
            pairs = step_pairs(act)
            with act.Fori(0, STEPS // 2 - 1) as it:
                with act.If(it < pairs - 1):
                    for b in (0, 1):
                        t = 2 * it + b
                        gate(b, t + 1)
                        rows_in(1 - b, t + 2)
                        hidden(b, t + 1)
            last = 2 * pairs
            gate(0, last - 1)
            rows_in(1, last)
            hidden(0, last - 1)
            gate(1, last)
            hidden(1, last)
            for t in range(TILES):
                r = rows[t]
                act.wait_ge(s["c_y"], t + 1)
                if t >= 2:
                    act.wait_ge(s[f"c_out{t % 2}"], 16 * (t // 2))
                act.activation(co[t % 2][0:r, :], cx[t % 2][0:r, :], ACT.Square, accum_out=cst[0:r, t, 0:1]).then_inc(s["c_sq"], 1)
                act.wait_ge(s["c_ms"], t + 1)
                act.activation(cst[0:r, t, 2:3], cst[0:r, t, 1:2], ACT.Sqrt).then_inc(s["c_rt"], 1)

        def dve_moe(dve):
            link = links["dve"]
            v = nc.vector
            def bc(ap, shape):
                return ap.to_broadcast(shape)
            dve.wait_ge(s["iota_rdy"], 1)
            v.memset(lrow[:, :], PAD).then_inc(s["l_st"], 1)
            dve.wait_ge(s["r_L"], TILES)
            for j in range(NG):
                link(v.memset(cj[:, j:j + 1], float(NG - j)))
            link(v.memset(valid, 1.0))
            link(v.memset(valid[:, NT:TILES], 0.0))
            link(v.memset(valid[0:DB, NT:TILES], 1.0))
            link(v.memset(tmask, 1.0))
            link(v.memset(t3(tmask, NE)[:, :, 0:1], 0.0))
            link(v.memset(one16, 1.0))
            link(v.tensor_copy(stepf, stepi[:, :]))
            link(v.tensor_tensor(L[:, :, :], L[:, :, :], bc(rb[:, :].unsqueeze(1), [P, TILES, 20]), ALU.add))
            gl = L[:, :, 0:NG]
            el = L[:, :, NG:20].rearrange("p t (g e) -> p t g e", g=NG)

            def first_max(vals, mx, oh):
                link(v.reduce_max(mx, vals, AX.X))
                link(v.tensor_tensor(oh, vals, bc(mx.unsqueeze(2), [P, TILES, NG]), ALU.is_equal))
                link(v.tensor_tensor(ww, oh, bc(cj.unsqueeze(1), [P, TILES, NG]), ALU.mult))
                link(v.reduce_max(wmx, ww, AX.X))
                link(v.tensor_tensor(oh, ww, bc(wmx.unsqueeze(2), [P, TILES, NG]), ALU.is_equal))

            first_max(gl, gmx, ohg)
            v.tensor_tensor(ee, gl, bc(gmx.unsqueeze(2), [P, TILES, NG]), ALU.subtract).then_inc(s["r_ge"], 1)
            p4 = prod.rearrange("p t (g e) -> p t g e", g=NG)
            for g in range(NG):
                link(v.tensor_tensor(p4[:, :, g, :], el[:, :, g, :], bc(ohg[:, :, g:g + 1], [P, TILES, EG]), ALU.mult))
            link(v.reduce_sum(esel, p4.rearrange("p t g e -> p t e g"), AX.X))
            first_max(esel, m1, oh1)
            link(v.scalar_tensor_tensor(e2, oh1, -1e30, esel, ALU.mult, ALU.add))
            first_max(e2, m2, oh2)
            v.tensor_tensor(dlt, m2, m1, ALU.subtract).then_inc(s["r_d"], 1)
            for oh, OH in ((oh1, OH1), (oh2, OH2)):
                o4 = OH.rearrange("p t (g e) -> p t g e", g=NG)
                for g in range(NG):
                    link(v.tensor_tensor(o4[:, :, g, :], oh, bc(ohg[:, :, g:g + 1], [P, TILES, EG]), ALU.mult))
                link(v.tensor_tensor(OH, OH, bc(valid.unsqueeze(2), [P, TILES, NE]), ALU.mult))
            v.tensor_tensor(M, OH1, OH2, ALU.add).then_inc(s["r_M"], 1)
            dve.wait_ge(s["r_gexp"], 1)
            link(v.reduce_sum(gsm, ee, AX.X))
            dve.wait_ge(s["r_dexp"], 1)
            link(v.tensor_scalar(wt1, dlt, 1.0, None, ALU.add))
            link(v.tensor_tensor(wt1, wt1, gsm, ALU.mult))
            link(v.reciprocal(wcol[:, 0, :], wt1))
            link(v.tensor_tensor(wcol[:, 1, :], wcol[:, 0, :], dlt, ALU.mult))
            dve.wait_ge(s["r_rank"], 1)
            link(v.tensor_copy(t3(totE, NE), T[:, 1, 0:NTE].rearrange("p (t e) -> p e t", t=TILES)))
            link(v.tensor_tensor_scan(incE, tmask, totE, 0.0, ALU.mult, ALU.add))
            ends = t3(incE, NE)[:, :, TILES - 1:TILES].rearrange("p e o -> p (e o)")
            link(v.tensor_scalar(tci[:, :], ends, float(P - 1), None, ALU.add))
            link(v.tensor_single_scalar(tci[:, :], tci[:, :], 7, ALU.logical_shift_right))
            link(v.tensor_copy(tcnt, tci[:, :]))
            link(v.tensor_tensor_scan(tend, one16, tcnt, 0.0, ALU.mult, ALU.add))
            link(v.tensor_tensor(tbase, tend, tcnt, ALU.subtract))
            link(v.tensor_scalar(tbase, tbase, float(P), None, ALU.mult))
            link(v.tensor_tensor(incE, incE, totE, ALU.subtract))
            link(v.tensor_tensor(slotA, T[:, 0, 0:NTE].rearrange("p (t e) -> p t e", t=TILES),
                                 incE.rearrange("p (e t) -> p t e", t=TILES), ALU.add))
            link(v.tensor_tensor(slotA, slotA, bc(tbase.unsqueeze(1), [P, TILES, NE]), ALU.add))
            for c, OH in enumerate((OH1, OH2)):
                link(v.tensor_tensor(prod, slotA, OH, ALU.mult))
                link(v.reduce_sum(slf, prod, AX.X))
                ins = v.tensor_copy(slot[:, c, :], slf)
                if c == 0:
                    link(ins)
            ins.then_inc(s["r_slot"], 1)
            link(v.tensor_tensor(cmp_, bc(tend.unsqueeze(1), [P, STEPS, NE]), bc(stepf.unsqueeze(2), [P, STEPS, NE]), ALU.is_le))
            link(v.reduce_sum(est, cmp_, AX.X))
            link(v.tensor_scalar(est, est, float(NE - 1), None, ALU.min))
            link(v.tensor_scalar(tab_need[:, :], est, 1.0, None, ALU.add))
            link(v.tensor_copy(em3, est))
            for j in range(WR, NE, WR):
                link(v.tensor_scalar(ec, est, float(j), -float(WR), ALU.is_ge, ALU.mult))
                link(v.tensor_tensor(em3, em3, ec, ALU.add))
            link(v.tensor_scalar(tab_off[:, :], em3, float(WSZ), None, ALU.mult))
            link(v.tensor_scalar(tab_pairs[:, :], tend[:, NE - 1:NE], 1.0, None, ALU.add))
            link(v.tensor_single_scalar(tab_pairs[:, :], tab_pairs[:, :], 1, ALU.logical_shift_right))
            link(v.tensor_scalar(tab_last[:, 0:1], tab_pairs[:, :], 2.0, 1.0, ALU.mult, ALU.add))
            link(v.tensor_scalar(tab_last[:, 1:2], tab_pairs[:, :], 16.0, None, ALU.mult))
            link(v.tensor_scalar(tab_pairs[:, :], tab_pairs[:, :], -float(LEAST), None, ALU.add))
            v.tensor_scalar(tab_end[:, :], tend, 1.0, None, ALU.add).then_inc(s["r_tab"], 1)
            dve.wait_ge(s["r_tab"], 1)
            dve.wait_ge(s["l_in"], 16)
            v.tensor_copy(lf[0:STEPS, :], lrow[:, :]).then_inc(s["l_f"], 1)
            dve.wait_ge(s["l_tr"], 1)
            link(v.tensor_copy(ridx[:, :], G[0][:, 2, 0:STEPS]))
            v.tensor_single_scalar(tidx[:, :], ridx[:, :], 1, ALU.logical_shift_right).then_inc(s["l_ids"], 1)
            link(v.memset(xg[0], 0.0))
            v.memset(xg[1], 0.0).then_inc(s["xg_z"], 1)

            def product(b, n, used):
                dve.wait_ge(s["sg_done"], n)
                if used is not None:
                    dve.wait_ge(s["ht_done"], used)
                v.tensor_tensor(hid[b], GU[b][:, FF:2 * FF], sg[b], ALU.mult).then_inc(s["hid_done"], 1)

            def out_rows(b, n, stored):
                dve.wait_ge(s["moe_done"], n)
                if stored is not None:
                    dve.wait_ge(s[f"y_out{b}"], stored)
                v.tensor_copy(yb[b].rearrange("p (a n) -> p a n", a=2), Y).then_inc(s["y_rdy"], 1)

            product(0, 1, None)
            product(1, 2, None)
            out_rows(0, 2, None)
            product(0, 3, 1)
            out_rows(1, 3, None)
            pairs = step_pairs(dve)
            with dve.Fori(1, STEPS // 2 - 1) as it:
                with dve.If(it < pairs - 1):
                    for b in (1, 0):
                        t = 2 * it + (2 - b)
                        product(b, t + 1, t - 1)
                        out_rows(1 - b, t + 1, 16 * it)
            last = 2 * pairs
            product(1, last, last - 2)
            out_rows(0, last, 16 * (pairs - 1))
            out_rows(1, last + 1, 16 * (pairs - 1))
            for t in range(TILES):
                r = rows[t]
                dve.wait_ge(s[f"c_in{t % 2}"], 32 * (t // 2 + 1))
                x = cx[t % 2][0:r, :]
                link(v.scalar_tensor_tensor(x, cy[t % 2][0:r, 0, :], wcol[0:r, 0, t:t + 1], x, ALU.mult, ALU.add))
                v.scalar_tensor_tensor(x, cy[t % 2][0:r, 1, :], wcol[0:r, 1, t:t + 1], x, ALU.mult, ALU.add).then_inc(s["c_y"], 1)
                dve.wait_ge(s["c_sq"], t + 1)
                v.tensor_scalar(cst[0:r, t, 1:2], cst[0:r, t, 0:1], 1.0 / D, EPS, ALU.mult, ALU.add).then_inc(s["c_ms"], 1)
                dve.wait_ge(s["c_rt"], t + 1)
                link(v.reciprocal(cst[0:r, t, 3:4], cst[0:r, t, 2:3]))
                if t == 0:
                    dve.wait_ge(s["c_gain"], 16)
                v.scalar_tensor_tensor(co[t % 2][0:r, :], x, cst[0:r, t, 3:4], cg[0:r, :], ALU.mult, ALU.mult).then_inc(s["c_h"], 1)

        block = ctx.enter_context(nc.Block())

        @block.sync
        def _(sp):
            link_raw = [0]

            def load_block(n):
                w, c0, width = blocks[n]
                if n >= RAW:
                    sp.wait_ge(s["split_done"], n - RAW + 1)
                sp.dma_start(raw[:, n % RAW, :, 0:width],
                             w[:, c0:c0 + width].rearrange("(k p) n -> p k n", p=P)).then_inc(raw_in[n % RAW], 16)

            def load_x(i):
                j, stage, t = nseq[i], i // TILES, i % TILES
                if j >= 2:
                    sp.wait_ge(s["h_done"], j - 1)
                if stage == 0:
                    src = xrows[t]
                elif stage == 1:
                    src = xrows[t]
                    if t >= 2:
                        wait_x_out(sp, j - 2)
                else:
                    src = drows(d_x1, t)
                    if t == 0:
                        wait_x_out(sp, 2 * TILES - 1)
                        wait_x_out(sp, 2 * TILES - 2)
                    if t >= 2:
                        wait_x_out(sp, j - 2)
                sp.dma_start(xb[j % 2][0:rows[t], :], src).then_inc(x_in[j % 2], 16)

            for m in range(MB):
                sp.dma_start(memx[:, m, :], mem_prompt[0, m * P:(m + 1) * P, :]).then_inc(s["mem_in"], 16)
            for n in range(RAW):
                load_block(n)
            sp.dma_start(gain, norm_mix[0].partition_broadcast(P)).then_inc(s["gain_in"], 16)
            sp.dma_start(strow, state_conv[0].rearrange("b j c -> (b j) c")).then_inc(s["st_in"], 16)
            for i in norm_seq[0:2]:
                load_x(i)
            for dst, src in const_loads:
                sp.dma_start(dst, src, allow_slow_non_contiguous=True).then_inc(s["const_in"], 16)
            sp.dma_start(new_conv_s[0, :, 0, :], state_conv[0, :, 1, :]).then_inc(s["cs_out"], 16)

            nb = RAW
            for what, i in order:
                if what == "block":
                    if nb < NBLK:
                        load_block(nb)
                        nb += 1
                    k, b = kinds[i]
                    if k == "cb":
                        wait_read(sp, i)
                        sp.dma_start(d_yc[b], tmp[2][:, 0:COLS]).then_inc(s["y_sp"], 16)
                elif what == "norm":
                    j, stage, t = nseq[i], i // TILES, i % TILES
                    if stage == 1:
                        sp.wait_ge(s["res_done"], t + 1)
                        sp.dma_start(drows(d_x1, t), xb[j % 2][0:rows[t], :]).then_inc(x_out[j % 2], 16)
                    if stage == 2:
                        sp.wait_ge(s["res_done"], TILES + t + 1)
                        sp.dma_start(drows(d_x2, t), xb[j % 2][0:rows[t], :]).then_inc(x_out[j % 2], 16)
                        sp.wait_ge(s["h_done"], j + 1)
                        sp.dma_start(drows(d_h3, t), hb[j % 2][0:rows[t], :]).then_inc(h_out[j % 2], 16)
                    if j + 2 < len(norm_seq) and norm_seq[j + 2] // TILES == stage:
                        load_x(norm_seq[j + 2])
                elif what == "memout":
                    sp.wait_ge(s["mem_tm_ev"], 2 * MB)
                    for o, (dst, r) in enumerate(((new_mk, mtm[0]), (new_mv, mtm[1]))):
                        for m in range(MB):
                            sp.dma_start(dst[0, 0, m * P:(m + 1) * P].rearrange("m h d -> m (h d)"),
                                         r[:, m, :]).then_inc(s["mem_out"], 16)
                    sp.dma_start(d_mkT, region("vtm", MB * D, KB * MEM)).then_inc(s["mk_spill"], 16)
                elif what == "convstate" and i == CB - 1:
                    sp.wait_ge(s["us_ev"], CB)
                    sp.dma_start(new_conv_p[0, 0], csrow[0:2, :]).then_inc(s["cs_out"], 16)
                    sp.dma_start(new_conv_s[0, :, 1, :], csrow[2:2 + DB, :]).then_inc(s["cs_out"], 16)
                elif what == "glasample":
                    sp.wait_ge(s["a_norm"], NT)
                    for k in range(QB):
                        sp.dma_start(S0[:, k, :, :], state_gla[0, :, 2 * k:2 * k + 2].rearrange("b h d v -> (h d) b v")).then_inc(s["gs_in"], 16)
                    sp.wait_ge(s["a_S"], NT)
                    for k in range(QB):
                        sp.dma_start(new_gla_p[0, 0, 2 * k:2 * k + 2].rearrange("h d v -> (h d) v"), S[:, NCK % 4, k, :]).then_inc(s["gs_out"], 16)
                    sp.wait_ge(s["gs_sn"], 1)
                    for k in range(QB):
                        sp.dma_start(new_gla_s[0, :, 2 * k:2 * k + 2].rearrange("b h d v -> (h d) b v"), S0[:, k, :, :]).then_inc(s["gs_out"], 16)
                elif what == "ysplit":
                    sp.wait_ge(s["yg_done"], 1)
                    sp.wait_ge(s["y_sp"], 16 * CB)
                    sp.dma_start(feat[:, VB:VB + CB, :], d_yc.rearrange("k p n -> p k n")).then_inc(s["yc_in"], 16)
                    sp.wait_ge(s["gs_o"], 1)
                    sp.wait_ge(s["gs_out"], 16 * 2 * QB)
                    sp.dma_start(gain, norm_mem[0].partition_broadcast(P)).then_inc(s["gain_in"], 16)
                    load_x(norm_seq[TILES])
                    load_x(norm_seq[TILES + 1])
                elif what == "sq":
                    sp.wait_ge(s["gs_bc"], DB)
                    sp.wait_ge(s["mk_spill"], 16)
                    sp.wait_ge(s["mem_out"], 16 * 2 * MB)
                    sp.dma_start(region("vtm", 0, KB * MEM), d_mkT).then_inc(s["mk_in"], 16)
                    for m in range(MB):
                        sp.dma_start(mv_sb[:, m, :], new_mv[0, 0, m * P:(m + 1) * P].rearrange("m h d -> m (h d)")).then_inc(s["mv_in"], 16)
                    sp.wait_ge(s["h_done"], 2 * TILES)
                    wait_x_out(sp, 2 * TILES - 1)
                    wait_x_out(sp, 2 * TILES - 2)
                    sp.wait_ge(s["fwd_done"], MB + 2 * TILES)
                    for b in range(DB):
                        if b >= 2:
                            sp.wait_ge(s["q_sc"], 2 * b - 2)
                        sp.dma_start(cache[b % 2], cache_mem_k[0, b].rearrange("(m p) h d -> p m (h d)", p=P)).then_inc(s[f"kc_in{b % 2}"], 16)
                    for b in range(DB):
                        sp.wait_ge(s["q_sc"], 2 * DB - (2 if b == 0 else 0))
                        if b >= 2:
                            sp.wait_ge(s["q_o"], b - 1)
                        sp.dma_start(cache[b % 2], cache_mem_v[0, b].rearrange("(m p) h d -> p m (h d)", p=P)).then_inc(s[f"vc_in{b % 2}"], 16)
                elif what == "pv" and i == 1:
                    sp.wait_ge(s["q_o"], DB)
                    sp.wait_ge(s["h_done"], 2 * TILES)
                    sp.wait_ge(s["q_bc"], 2 * DB)
                    sp.dma_start(gain, norm_ffn[0].partition_broadcast(P)).then_inc(s["gain_in"], 16)
                    load_x(norm_seq[2 * TILES])
                    load_x(norm_seq[2 * TILES + 1])
            sp_moe(sp)
            sp.wait_ge(s["cs_out"], 16 * 3)
            sp.wait_ge(s["gs_out"], 16 * 2 * QB)
            sp.wait_ge(s["mem_out"], 16 * 2 * MB)
            sp.wait_ge(s["y_sp"], 16 * CB)
            wait_x_out(sp, 3 * TILES - 1)
            wait_x_out(sp, 3 * TILES - 2)
            wait_h_out(sp, 3 * TILES - 1)
            wait_h_out(sp, 3 * TILES - 2)
            sp.wait_ge(s["mk_spill"], 16)

        @block.gpsimd
        def _(pool):
            link = chain(pool, s["g_ch"])
            link(pool.memset(ident[:, :], 0.0))
            pool.affine_select(out=ident[:, :], in_=ident[:, :], compare_op=ALU.not_equal, fill=1.0, base=0,
                               pattern=[[-1, P]], channel_multiplier=1).then_inc(s["ident_rdy"], 1)
            pool.memset(ones[:, :], 1.0).then_inc(s["ones_rdy"], 1)
            link(pool.memset(tri[:, :], 1.0))
            link(pool.memset(cmask[:, :], 1.0))
            link(pool.affine_select(out=tri[:, :], in_=tri[:, :], compare_op=ALU.is_gt, fill=0.0, base=0,
                                    pattern=[[1, P]], channel_multiplier=-1))
            link(pool.affine_select(out=cmask[:, :], in_=cmask[:, :], compare_op=ALU.is_ge, fill=0.0, base=0,
                                    pattern=[[1, P]], channel_multiplier=-1))
            link(pool.memset(cmask[0:CHUNK, CHUNK:P], 0.0))
            link(pool.memset(smask[:, :], 1.0))
            link(pool.memset(smask[:, :].rearrange("p (n c) -> p n c", c=CHUNK)[:, :, 0:1], 0.0))
            pool.memset(L[:, :, :], 0.0).then_inc(s["masks_rdy"], 1)
            pool_moe(pool)

        @block.tensor
        def _(pe):
            def mm3(out, a_hi, a_lo, b_hi, b_lo, first, last):
                pe.matmul(out, a_hi, b_hi, start=first, stop=False)
                pe.matmul(out, a_hi, b_lo, start=False, stop=False)
                return pe.matmul(out, a_lo, b_hi, start=False, stop=last)

            def stream(n):
                kind, b = kinds[n]
                u, slot, width = use(n), n % 2, blocks[n][2]
                pe.wait_ge(s["split_done"], n + 1)
                if u >= 2:
                    pe.wait_ge(free[u % 2], u // 2)
                spans = [(0, MEM)] if kind in ("memk", "memv") else [(c * CH, CH) for c in range(NCH)]
                ins = None
                for k in range(KB):
                    for c, (c0, cn) in enumerate(spans):
                        ins = mm3(G[u % 2][0:width, c, 0:cn], w_hi[:, slot, k, 0:width], w_lo[:, slot, k, 0:width],
                                  act_hi[:, k, c0:c0 + cn], act_lo[:, k, c0:c0 + cn], k == 0, k == KB - 1)
                ins.then_inc(s["big_done"], 1)

            def forward(f, src, r):
                if f >= 2:
                    pe.wait_ge(s["nlo_done"], f - 1)
                for k in range(KB):
                    ins = pe.transpose(fwd[f % 2][:, k // 4, (k % 4) * P:(k % 4) * P + r],
                                       src[0:r, k * P:(k + 1) * P], ident[0:r, 0:r])
                ins.then_inc(s["fwd_done"], 1)

            def backward(t):
                r = rows[t]
                for k in range(KB):
                    ins = pe.transpose(back[0:r, k // 4, (k % 4) * P:(k % 4) * P + P],
                                       feat[:, k, t * P:t * P + r], ident[:, :])
                ins.then_inc(s["back_done"], 1)

            pe.wait_ge(s["ident_rdy"], 1)
            for what, i in order:
                if what == "mem":
                    if i == 0:
                        pe.wait_ge(s["mem_in"], 16 * MB)
                    forward(i, memx[:, i, :], P)
                elif what == "block":
                    kind, b = kinds[i]
                    if i == 0:
                        pe.wait_ge(s["nlo_done"], MB)
                    if (kind, b) == ("cc", 0):
                        pe.wait_ge(s["nlo_done"], MB + TILES)
                        pe.wait_ge(s["mem_tm_ev"], 2 * MB)
                    if (kind, b) == ("out", 0):
                        pe.wait_ge(s["ys_lo"], KB)
                    if (kind, b) == ("mq", 0):
                        pe.wait_ge(s["nlo_done"], MB + 2 * TILES)
                    if (kind, b) == ("o", 0):
                        pe.wait_ge(s["s_pvlo"], 2 * KB)
                        pe.wait_ge(s["q_olo"], 1)
                    stream(i)
                elif what == "memout":
                    wait_free(pe, 2 * KB - 1)
                    for o, src in enumerate((mkT_w, mvT_w)):
                        for m in range(MB):
                            if o * MB + m >= 1:
                                pe.wait_ge(s["mem_tm_ev"], o * MB + m)
                            for k in range(KB):
                                ins = pe.transpose(back[:, k // 4, (k % 4) * P:(k % 4 + 1) * P],
                                                   src[:, k, m * P:(m + 1) * P], ident[:, :])
                            ins.then_inc(s["mem_tm_tr"], 1)
                elif what == "norm":
                    j, stage, t = nseq[i], i // TILES, i % TILES
                    if stage >= 1:
                        if t == 0:
                            wait_free(pe, at[("out" if stage == 1 else "o", KB - 1)])
                            backward(0)
                        if t + 1 < TILES:
                            pe.wait_ge(s["res_done"], (stage - 1) * TILES + t + 1)
                            backward(t + 1)
                    pe.wait_ge(s["h_done"], j + 1)
                    forward(MB + j, hb[j % 2], rows[t])
                    if stage == 2:
                        pe.wait_ge(s["nlo_done"], MB + j + 1)
                        if t == 0:
                            pe.wait_ge(s["const_in"], N_CONST)
                        if t >= 2:
                            pe.wait_ge(s["r_L"], t - 1)
                        for k in range(KB):
                            ins = pe.matmul(G[t % 2][0:rows[t], 0, 0:20], h3T[j % 2][:, k, 0:rows[t]], rw[:, k, :],
                                            start=(k == 0), stop=(k == KB - 1))
                        ins.then_inc(s["r_mm"], 1)
                elif what == "convstate":
                    if i == 0:
                        pe.wait_ge(s["st_in"], 16)
                        for k in range(CB):
                            ins = pe.transpose(T[:, 1, k * 2 * DB:(k + 1) * 2 * DB], strow[:, k * P:(k + 1) * P],
                                               ident[0:2 * DB, 0:2 * DB])
                        ins.then_inc(s["st_tr"], 1)
                    if i >= 1:
                        pe.wait_ge(s["us_ev"], i)
                    wait_read(pe, at[("ch", i)])
                    pe.transpose(T[0:2 + DB, 0, i * P:(i + 1) * P], tmp[1][:, SEQ:SEQ + 2 + DB],
                                 ident[:, :]).then_inc(s["us_tr"], 1)
                elif what == "gate":
                    wait_read(pe, at[("lr", 0)])
                    pe.wait_ge(s["const_in"], N_CONST)
                    for b in range(QB):
                        u = use_z(b)
                        pe.wait_ge(free[u % 2], u // 2)
                        for c in range(NCH):
                            ins = pe.matmul(G[u % 2][:, c, 0:CH], gup[:, b * P:(b + 1) * P],
                                            lrT[:, c * CH:(c + 1) * CH], start=True, stop=True)
                        ins.then_inc(s["big_done"], 1)
                elif what == "vT":
                    wait_free(pe, at[("v", i)])
                    if i == 0:
                        pe.wait_ge(s["us_ev"], CB)
                        pe.wait_ge(s["st_ev"], 1)
                    else:
                        pe.wait_ge(s["vt_ev"], i)
                    for t in range(NT):
                        ins = pe.transpose(T[:, t // 4, (t % 4) * P:(t % 4 + 1) * P],
                                           feat[:, i, t * P:(t + 1) * P], ident[:, :])
                    ins.then_inc(s["v_tr"], 1)
                    if i == VB - 1:
                        pe.wait_ge(s["vt_ev"], VB)
                        for k in range(VB):
                            ins = pe.transpose(T[0:DB, 0, k * P:(k + 1) * P], feat[:, k, SEQ:COLS], ident[:, :])
                        ins.then_inc(s["v_tr"], 1)
                elif what == "gla":
                    t = i
                    if t == 0:
                        pe.wait_ge(s["prep_done"], 1)
                        pe.wait_ge(s["vt_ev"], VB + 1)
                        pe.wait_ge(s["ones_rdy"], 1)
                    else:
                        pe.wait_ge(s["a_sq"], t)
                    c0 = t * P
                    for q in range(2):
                        for k in range(QB):
                            ins = pe.matmul(T[:, q, k * P:(k + 1) * P], kT[q * DK:(q + 1) * DK, k, c0:c0 + P],
                                            qT[q * DK:(q + 1) * DK, k, c0:c0 + P], start=True, stop=True)
                    ins.then_inc(s["a_mm"], 1)
                    X = spare(t)
                    wait_read(pe, at[("g", t // (NT // VB))])
                    if t >= 1:
                        pe.wait_ge(s["a_rt"], t)
                    for k in range(QB):
                        ins = pe.transpose(X[:, 0, k * P:(k + 1) * P], zT[:, k, c0:c0 + P], ident[:, :])
                    ins.then_inc(s["a_kd"], 1)
                    pe.wait_ge(s["a_kdt"], t + 1)
                    for c in range(2):
                        for h in range(HEADS):
                            r0, k = (h % 2) * DK, h // 2
                            ins = pe.matmul(X[r0:r0 + DK, 1 + c, k * DV:(k + 1) * DV],
                                            kdt[t % 2][c * CHUNK:(c + 1) * CHUNK, h * DK:(h + 1) * DK],
                                            vtm[c * CHUNK:(c + 1) * CHUNK, t, h * DV:(h + 1) * DV],
                                            start=True, stop=True)
                    ins.then_inc(s["a_ds"], 1)
                    pe.wait_ge(s["a_cp"], t + 1)
                    pe.wait_ge(s["a_S"], t + 1)
                    for q in range(2):
                        for k in range(QB):
                            h = 2 * k + q
                            pe.matmul(T[:, q, k * P:(k + 1) * P], vtm[:, t, h * DV:(h + 1) * DV], Am[t % 2][:, q, k, :],
                                      start=True, stop=False)
                            for c in range(2):
                                a0 = k * P + c * CHUNK
                                ins = pe.matmul(T[:, q, a0:a0 + CHUNK], S[q * DK:(q + 1) * DK, (2 * t + c) % 4, k, :],
                                                qe[q * DK:(q + 1) * DK, k, c0 + c * CHUNK:c0 + (c + 1) * CHUNK],
                                                start=False, stop=(c == 1))
                    ins.then_inc(s["a_o"], 1)
                    pe.wait_ge(s["a_sq"], t + 1)
                    pe.matmul(X[:, 0, :], ones[:, :], gsq[:, :], start=True, stop=True).then_inc(s["a_ms"], 1)
                elif what == "glasample":
                    pe.wait_ge(s["gs_a"], 1)
                    for b in range(DB):
                        if b >= 2:
                            pe.wait_ge(s["gs_kv"], b - 1)
                        else:
                            pe.wait_ge(s["a_rt"], NT)
                            pe.wait_ge(s["a_sq"], NT)
                        pe.matmul(T[:, b % 2, :], sel_g[:, b, :], vtm[0:DB, NT, :], start=True,
                                  stop=True).then_inc(s["gs_bc"], 1)
                    pe.wait_ge(s["gs_sn"], 1)
                    for q in range(2):
                        for k in range(QB):
                            for b in range(DB):
                                ins = pe.matmul(T[:, q, k * DB + b:k * DB + b + 1], S0[q * DK:(q + 1) * DK, k, b, :],
                                                qT[q * DK:(q + 1) * DK, k, SEQ + b:SEQ + b + 1], start=True, stop=True)
                    ins.then_inc(s["gs_o"], 1)
                    pe.wait_ge(s["gs_sq"], 1)
                    pe.matmul(spare(NT - 1)[:, 0, 0:HEADS * DB], ones[:, :], gsq[:, 0:HEADS * DB], start=True,
                              stop=True).then_inc(s["gs_ms"], 1)
                elif what == "sq":
                    wait_free(pe, at[("mq", KB - 1)])
                    for k in range(KB):
                        ins = pe.transpose(back[0:DB, k // 4, (k % 4) * P:(k % 4 + 1) * P], feat[:, k, SEQ:COLS], ident[:, :])
                    ins.then_inc(s["q_tr"], 1)
                    pe.wait_ge(s["q_ev"], 2)
                elif what == "smax":
                    pe.wait_ge(s["q_sc"], 2 * DB)
                    pe.wait_ge(s["s_e"], NT // 2)
                    for m in range(MB):
                        ins = pe.transpose(back[0:DB * MH, 0, m * P:(m + 1) * P], ksc[:, m, :], ident[:, :])
                    ins.then_inc(s["q_t2"], 1)
                elif what == "sprob":
                    pe.wait_ge(s["q_pn"], 1)
                    for m in range(MB):
                        ins = pe.transpose(back[:, 1, m * DB * MH:(m + 1) * DB * MH], sps[:, m * P:(m + 1) * P],
                                           ident[0:DB * MH, 0:DB * MH])
                    ins.then_inc(s["q_t3"], 1)
                    pe.wait_ge(s["q_pT"], 1)
                elif what == "sout":
                    pe.wait_ge(s["q_olo"], 1)
                elif what == "att":
                    def key_rows(b):
                        for c in range(2):
                            if b >= 1:
                                pe.wait_ge(s["q_sc"], 2 * b - 1 + c)
                            pe.matmul(G[c][:, 0, :], sel_a[:, b, :], qs[:, c * 512:(c + 1) * 512], start=True,
                                      stop=True).then_inc(s["q_bc"], 1)

                    def values(b):
                        if b == 0:
                            pe.wait_ge(s["s_pvlo"], KB)
                        pe.wait_ge(s[f"vc_in{b % 2}"], 16 * (b // 2 + 1))
                        for k in range(KB):
                            for m in range(MB):
                                e = b * MH + k * P // DH
                                ins = pe.matmul(G[0][:, 0, k * DB + b:k * DB + b + 1], cache[b % 2][:, m, k * P:(k + 1) * P],
                                                pTs[:, m, e:e + 1], start=(m == 0), stop=(m == MB - 1))
                        ins.then_inc(s["q_o"], 1)

                    beside = key_rows if i < NT // 2 else values
                    b0 = i % (NT // 2) * PER

                    def scores(t):
                        if t == 0:
                            pe.wait_ge(s["mk_in"], 16)
                        if t >= 2:
                            pe.wait_ge(s["s_e"], t - 1)
                        pair = (T[:, :, :], back)[t % 2]
                        for h in range(MH):
                            for kk in range(DH // P):
                                k = h * (DH // P) + kk
                                ins = pe.matmul(pair[:, h // 2, (h % 2) * MEM:(h % 2 + 1) * MEM],
                                                feat[:, k, t * P:(t + 1) * P], mkT[:, k, :],
                                                start=(kk == 0), stop=(kk == DH // P - 1))
                        ins.then_inc(s["s_mm"], 1)
                    if i == 0:
                        scores(0)
                    if i + 1 < NT:
                        scores(i + 1)
                    for b in range(b0, b0 + PER // 2):
                        beside(b)
                    pe.wait_ge(s["s_p"], i + 1)
                    if i >= 1:
                        pe.wait_ge(s["s_pT"], i)
                    for e in range(MH * MB):
                        ins = pe.transpose(G[0][:, 1 + e // 4, (e % 4) * P:(e % 4 + 1) * P],
                                           pr[i % 2][:, e // MB, (e % MB) * P:(e % MB + 1) * P], ident[:, :])
                    ins.then_inc(s["s_tr"], 1)
                    for b in range(b0 + PER // 2, b0 + PER):
                        beside(b)
                elif what == "pv":
                    if i == 0:
                        pe.wait_ge(s["mv_in"], 16 * MB)
                    pe.wait_ge(s["s_pT"], (i + 1) * (NT // 2))
                    for k in range(KB):
                        n = i * KB + k
                        if n >= 2:
                            pe.wait_ge(s["s_pvlo"], n - 1)
                        for m in range(MB):
                            ins = pe.matmul(G[k % 2][:, 0, :], mv_sb[:, m, k * P:(k + 1) * P],
                                            pT[:, (k * P // DH) * MB + m, :], start=(m == 0), stop=(m == MB - 1))
                        ins.then_inc(s["s_pv"], 1)
            pe_moe(pe)

        @block.scalar
        def _(act):
            link = chain(act, s["a_ch"])

            def split_hi(n):
                width = blocks[n][2]
                act.wait_ge(raw_in[n % RAW], 16 * (n // RAW + 1))
                if n >= 2:
                    act.wait_ge(s["big_done"], use(n - 2) + 1)
                act.copy(w_hi[:, n % 2, :, 0:width], raw[:, n % RAW, :, 0:width]).then_inc(s["hi_done"], 1)

            def evacuate(n):
                kind, b = kinds[n]
                u = use(n)
                if kind in ("ch", "cb"):
                    return
                act.wait_ge(s["big_done"], u + 1)
                src, dst, scale, fn = G[u % 2][:, :, 0:CH], None, 1.0, None
                if kind == "memk":
                    src, dst = G[u % 2][:, 0, 0:MEM], mkT_w[:, b, :]
                elif kind == "memv":
                    src, dst = G[u % 2][:, 0, 0:MEM], mvT_w[:, b, :]
                elif kind == "cc":
                    if b >= 1:
                        wait_read(act, at[("ch", b - 1)])
                    dst = chunks(tmp[0][:, 0:COLS])
                elif kind == "lr":
                    act.wait_ge(s["mem_out"], 16 * 2 * MB)
                    src, dst = G[u % 2][0:16, :, 0:CH], chunks(lrT)
                elif kind == "q":
                    dst, scale = chunks(qT[:, b, :]), DK ** -0.5
                elif kind == "k":
                    dst = chunks(kT[:, b, :])
                elif kind == "v":
                    if b == 0:
                        act.wait_ge(s["cs_out"], 16 * 3)
                        act.wait_ge(s["mk_spill"], 16)
                    dst = chunks(feat[:, b, :])
                elif kind == "g":
                    dst, fn = chunks(feat[:, VB + b, :]), ACT.Silu
                elif kind == "out":
                    if b == 0:
                        act.wait_ge(s["ys_lo"], KB)
                    dst = chunks(feat[:, b, :])
                else:
                    dst = chunks(feat[:, b, :])
                if fn is not None:
                    ins = act.activation(dst, src, fn)
                elif scale != 1.0:
                    ins = act.activation(dst, src, ACT.Copy, scale=scale)
                else:
                    ins = act.copy(dst, src)
                ins.then_inc(free[u % 2], 1)

            def evac_fwd(f, t, col0, r):
                act.wait_ge(s["fwd_done"], f + 1)
                act.copy(act_hi[:, :, col0:col0 + r], fwd[f % 2].rearrange("p a (k n) -> p (a k) n", n=P)[:, :, 0:r]).then_inc(s["nhi_done"], 1)

            def square(i):
                j, stage, t = nseq[i], i // TILES, i % TILES
                r = rows[t]
                if stage == 0:
                    act.wait_ge(x_in[j % 2], 16 * (j // 2 + 1))
                else:
                    act.wait_ge(s["res_done"], (stage - 1) * TILES + t + 1)
                if j >= 2:
                    act.wait_ge(s["fwd_done"], MB + j - 1)
                if stage == 2 and t >= 2:
                    wait_h_out(act, j - 2)
                act.activation(hb[j % 2][0:r, :], xb[j % 2][0:r, :], ACT.Square,
                               accum_out=ssum[0:r, j, 0:1]).then_inc(s["sq_done"], 1)

            def late(i):
                j, stage, t = nseq[i], i // TILES, i % TILES
                f, r = MB + j, rows[t]
                if stage == 2:
                    act.wait_ge(s["fwd_done"], f + 1)
                    if t >= 2:
                        act.wait_ge(s["r_mm"], t - 1)
                    act.copy(h3T[j % 2][:, :, 0:r], fwd[f % 2].rearrange("p a (k n) -> p (a k) n", n=P)[:, :, 0:r]).then_inc(s["nlo_done"], 1)
                    act.wait_ge(s["r_mm"], t + 1)
                    act.copy(L[0:r, t, :], G[t % 2][0:r, 0, 0:20]).then_inc(s["r_L"], 1)
                else:
                    if stage == 0 and t < MB:
                        act.wait_ge(s["big_done"], 2 * KB)
                    if stage == 1 and t == 0:
                        act.wait_ge(s["big_done"], use(at[("out", KB - 1)]) + 1)
                    evac_fwd(f, t, t * P, r)

            def norm_step(i):
                j, stage, t = nseq[i], i // TILES, i % TILES
                r = rows[t]
                same = [x for x in norm_seq if x // TILES == stage]
                p = same.index(i)
                if p == 0:
                    square(i)
                act.wait_ge(s["ms_done"], j + 1)
                act.activation(ssum[0:r, j, 2:3], ssum[0:r, j, 1:2], ACT.Sqrt).then_inc(s["rt_done"], 1)
                if p > 0:
                    late(same[p - 1])
                if p + 1 < len(same):
                    square(same[p + 1])
                else:
                    late(i)

            for what, i in order:
                if what == "mem":
                    evac_fwd(i, i, i * P, P)
                    if i == 0:
                        split_hi(0)
                elif what == "block":
                    if i + 1 < NBLK:
                        split_hi(i + 1)
                    evacuate(i)
                elif what == "norm":
                    if i // TILES == 2 and i % TILES == 0:
                        act.wait_ge(s["masks_rdy"], 1)
                    norm_step(i)
                elif what == "memout":
                    for n in range(2 * MB):
                        act.wait_ge(s["mem_tm_tr"], n + 1)
                        act.copy(mtm[n // MB][:, n % MB, :].rearrange("p (a n) -> p a n", a=2), back).then_inc(s["mem_tm_ev"], 1)
                elif what == "convstate":
                    if i == 0:
                        act.wait_ge(s["st_tr"], 1)
                        act.copy(stT[:, :, :], T[:, 1, 0:CB * 2 * DB].rearrange("p (k n) -> p k n", k=CB)).then_inc(s["st_ev"], 1)
                    act.wait_ge(s["us_tr"], i + 1)
                    act.copy(csrow[:, i * P:(i + 1) * P], T[0:2 + DB, 0, i * P:(i + 1) * P]).then_inc(s["us_ev"], 1)
                elif what == "gate":
                    act.wait_ge(s["const_in"], N_CONST)
                    for b in range(QB):
                        u = use_z(b)
                        act.wait_ge(s["big_done"], u + 1)
                        act.activation(chunks(zT[:, b, :]), G[u % 2][:, :, 0:CH], ACT.Identity,
                                       bias=gateb[:, b:b + 1]).then_inc(free[u % 2], 1)
                    for b in range(QB):
                        act.wait_ge(s["z_abs"], b + 1)
                        link(act.activation(tmp[b][:, 0:COLS], tmp[b][:, 0:COLS], ACT.Exp, scale=-1.0))
                        act.activation(tmp[b][:, 0:COLS], tmp[b][:, 0:COLS], ACT.Ln, bias=1.0).then_inc(s["z_ln"], 1)
                elif what == "prep":
                    b = i
                    act.wait_ge(s["la_done"], QB)
                    inv = 1.0 / 16.0
                    if b == 0:
                        for k in range(QB):
                            act.activation(adec[:, k, :], zT[:, k, SEQ:COLS], ACT.Exp, scale=inv).then_inc(s["p_x"], 1)
                    act.activation(dec[:, b, :].rearrange("p (n o) -> p n o", o=1), zT[:, b, 0:SEQ].rearrange("p (n c) -> p n c", c=CHUNK)[:, :, CHUNK - 1:CHUNK],
                                   ACT.Exp, scale=inv).then_inc(s["p_x"], 1)
                    if b >= 1:
                        act.wait_ge(s["p_m"], 4 * b)
                    act.activation(tmp[0][:, 0:SEQ], zT[:, b, 0:SEQ], ACT.Exp, scale=inv).then_inc(s["p_e"], 1)
                    act.wait_ge(s["p_d2"], b + 1)
                    act.activation(tmp[3][:, 0:SEQ], tmp[3][:, 0:SEQ], ACT.Exp, scale=inv).then_inc(s["p_e"], 1)
                    act.wait_ge(s["p_d1"], b + 1)
                    act.activation(tmp[2][:, 0:SEQ], tmp[1][:, 0:SEQ], ACT.Exp, scale=inv).then_inc(s["p_e"], 1)
                    act.wait_ge(s["p_e"], 4 * b + 3)
                    act.activation(tmp[1][:, 0:SEQ], tmp[1][:, 0:SEQ], ACT.Exp, scale=-inv).then_inc(s["p_e"], 1)
                elif what == "vT":
                    act.wait_ge(s["v_tr"], i + 1)
                    act.copy(vtm[:, 0:NT, i * P:(i + 1) * P], T[:, :, :].rearrange("p a (t n) -> p (a t) n", n=P)).then_inc(s["vt_ev"], 1)
                    if i == VB - 1:
                        act.wait_ge(s["v_tr"], VB + 1)
                        act.copy(vtm[0:DB, NT, :], T[0:DB, 0, :]).then_inc(s["vt_ev"], 1)
                elif what == "gla":
                    t = i
                    if t == 0:
                        act.wait_ge(s["prep_done"], 1)
                    act.wait_ge(s["a_kd"], t + 1)
                    act.copy(kdt[t % 2][:, :], spare(t)[:, 0, 0:QB * P]).then_inc(s["a_kdt"], 1)
                    act.wait_ge(s["a_o"], t + 1)
                    act.copy(feat[:, 0:VB, t * P:(t + 1) * P].rearrange("p (k q) n -> p q k n", q=2), lower4).then_inc(s["a_oev"], 1)
                    act.activation(gsq.rearrange("p (q n) -> p q n", q=2), T[:, :, 0:QB * P], ACT.Square).then_inc(s["a_sq"], 1)
                    act.wait_ge(s["a_ms"], t + 1)
                    if t >= 1:
                        act.wait_ge(s["a_norm"], t)
                    act.activation(grt, spare(t)[:, 0, :], ACT.Sqrt, scale=1.0 / DV, bias=epsb[:, 0:1]).then_inc(s["a_rt"], 1)
                elif what == "glasample":
                    act.wait_ge(s["gs_o"], 1)
                    n = HEADS * DB
                    act.copy(feat[:, 0:VB, SEQ:COLS].rearrange("p (k q) b -> p q k b", q=2),
                             T[:, :, 0:QB * DB].rearrange("p q (k b) -> p q k b", k=QB)).then_inc(s["gs_oev"], 1)
                    act.activation(gsq[:, 0:n].rearrange("p (q n) -> p q n", q=2), T[:, :, 0:QB * DB], ACT.Square).then_inc(s["gs_sq"], 1)
                    act.wait_ge(s["gs_ms"], 1)
                    act.wait_ge(s["a_norm"], NT)
                    act.activation(grt[:, 0:n], spare(NT - 1)[:, 0, 0:n], ACT.Sqrt, scale=1.0 / DV, bias=epsb[:, 0:1]).then_inc(s["gs_rt"], 1)
                elif what == "ysplit":
                    act.wait_ge(s["yg_done"], 1)
                    act.wait_ge(s["big_done"], use(at[("g", VB - 1)]) + 1)
                    for k in range(VB):
                        act.copy(act_hi[:, CB + k, :], feat[:, k, :]).then_inc(s["ys_hi"], 1)
                    act.wait_ge(s["yc_in"], 16)
                    for k in range(CB):
                        act.copy(act_hi[:, k, :], feat[:, VB + k, :]).then_inc(s["ys_hi"], 1)
                elif what == "sq":
                    act.wait_ge(s["q_tr"], 1)
                    act.wait_ge(s["gs_out"], 16 * 2 * QB)
                    act.copy(qs.rearrange("p (a n) -> p a n", a=2), back[0:DB]).then_inc(s["q_ev"], 1)
                elif what == "smax":
                    act.wait_ge(s["q_mx"], 1)
                    act.activation(sps[:, :], back[0:DB * MH, 0, 0:MEM], ACT.Exp, scale=DH ** -0.5, bias=sst[:, 1:2],
                                   accum_out=sst[:, 2:3]).then_inc(s["q_ex"], 1)
                elif what == "sprob":
                    act.wait_ge(s["q_t3"], 1)
                    act.copy(pTs[:, :, :], back[:, 1, 0:MB * DB * MH].rearrange("p (m e) -> p m e", m=MB)).then_inc(s["q_pT"], 1)
                elif what == "sout":
                    act.wait_ge(s["q_o"], DB)
                    act.copy(act_hi[:, :, SEQ:COLS], G[0][:, 0, 0:KB * DB].rearrange("p (k b) -> p k b", k=KB)).then_inc(s["q_ohi"], 1)
                elif what == "att":
                    def probs(t):
                        act.wait_ge(s["s_mx"], t + 1)
                        if t >= 2:
                            act.wait_ge(s["s_tr"], t - 1)
                        pair = (T[:, :, :], back)[t % 2]
                        for h in range(MH):
                            ins = act.activation(pr[t % 2][:, h, :], pair[:, h // 2, (h % 2) * MEM:(h % 2 + 1) * MEM], ACT.Exp,
                                                 scale=DH ** -0.5, bias=smx[:, t % 2, 1, h:h + 1],
                                                 accum_out=smx[:, t % 2, 2, h:h + 1])
                        ins.then_inc(s["s_e"], 1)
                    if i == 0:
                        probs(0)
                    if i + 1 < NT:
                        probs(i + 1)
                    act.wait_ge(s["s_tr"], i + 1)
                    if i == NT // 2:
                        act.wait_ge(s["s_pv"], KB)
                    c0 = (i % (NT // 2)) * P
                    act.copy(pT[:, :, c0:c0 + P], G[0][:, 1:3, :].rearrange("p a (e n) -> p (a e) n", n=P)).then_inc(s["s_pT"], 1)
                elif what == "pv":
                    for k in range(KB):
                        act.wait_ge(s["s_pv"], i * KB + k + 1)
                        act.copy(act_hi[:, k, i * HT:(i + 1) * HT], G[k % 2][:, 0, :]).then_inc(s["s_pvhi"], 1)
            act_moe(act)

        @block.vector
        def _(dve):
            link = links["dve"] = chain(dve, s["d_ch"])
            v = nc.vector

            def split_lo(n):
                width = blocks[n][2]
                dve.wait_ge(s["hi_done"], n + 1)
                v.tensor_tensor(w_lo[:, n % 2, :, 0:width], raw[:, n % RAW, :, 0:width], w_hi[:, n % 2, :, 0:width],
                                ALU.subtract).then_inc(s["split_done"], 1)

            def read_out(n):
                kind, b = kinds[n]
                u = use(n)
                if kind == "ch":
                    ucc = use(n - 1)
                    dve.wait_ge(s["big_done"], u + 1)
                    dve.wait_ge(free[ucc % 2], ucc // 2 + 1)
                    if b >= 1:
                        dve.wait_ge(s["us_tr"], b)
                    else:
                        link(v.memset(tmp[1][:, 0:2], 0.0))
                    v.tensor_tensor(chunks(tmp[1][:, 2:2 + COLS]), G[u % 2][:, :, 0:CH], chunks(tmp[0][:, 0:COLS]),
                                    ALU.mult).then_inc(free[u % 2], 1)
                    wait_read(dve, n)
                    if b == 0:
                        dve.wait_ge(s["const_in"], N_CONST)
                    else:
                        dve.wait_ge(s["y_sp"], 16 * b)
                    y, uu = tmp[2], tmp[1]
                    link(v.tensor_scalar(y[:, 0:SEQ], uu[:, 0:SEQ], cw[:, b, 0:1], None, ALU.mult))
                    link(v.scalar_tensor_tensor(y[:, 0:SEQ], uu[:, 1:1 + SEQ], cw[:, b, 1:2], y[:, 0:SEQ], ALU.mult, ALU.add))
                    link(v.scalar_tensor_tensor(y[:, 0:SEQ], uu[:, 2:2 + SEQ], cw[:, b, 2:3], y[:, 0:SEQ], ALU.mult, ALU.add))
                    if b == 0:
                        dve.wait_ge(s["st_ev"], 1)
                    st = stT[:, b, :].rearrange("p (b j) -> p b j", j=2)
                    ys = y[:, SEQ:COLS].rearrange("p (b o) -> p b o", o=1)
                    link(v.tensor_scalar(ys, st[:, :, 0:1], cw[:, b, 0:1], None, ALU.mult))
                    link(v.scalar_tensor_tensor(ys, st[:, :, 1:2], cw[:, b, 1:2], ys, ALU.mult, ALU.add))
                    link(v.scalar_tensor_tensor(y[:, SEQ:COLS], uu[:, 2 + SEQ:2 + COLS], cw[:, b, 2:3], y[:, SEQ:COLS], ALU.mult, ALU.add))
                elif kind == "cb":
                    dve.wait_ge(s["big_done"], u + 1)
                    v.tensor_tensor(chunks(tmp[2][:, 0:COLS]), G[u % 2][:, :, 0:CH], chunks(tmp[2][:, 0:COLS]), ALU.mult).then_inc(free[u % 2], 1)

            def evac_lo(f, col0, r):
                dve.wait_ge(s["nhi_done"], f + 1)
                v.tensor_tensor(act_lo[:, :, col0:col0 + r], fwd[f % 2].rearrange("p a (k n) -> p (a k) n", n=P)[:, :, 0:r],
                                act_hi[:, :, col0:col0 + r], ALU.subtract).then_inc(s["nlo_done"], 1)

            def late(i):
                j, stage, t = nseq[i], i // TILES, i % TILES
                if stage < 2:
                    evac_lo(MB + j, t * P, rows[t])

            def residual(i):
                j, stage, t = nseq[i], i // TILES, i % TILES
                if stage == 0:
                    return
                r = rows[t]
                dve.wait_ge(s["back_done"], (stage - 1) * TILES + t + 1)
                dve.wait_ge(x_in[j % 2], 16 * (j // 2 + 1))
                x3 = xb[j % 2][0:r, :].rearrange("p (a n) -> p a n", a=2)
                v.tensor_tensor(x3, back[0:r], x3, ALU.add).then_inc(s["res_done"], 1)

            def norm_step(i):
                j, stage, t = nseq[i], i // TILES, i % TILES
                r = rows[t]
                same = [x for x in norm_seq if x // TILES == stage]
                p = same.index(i)
                if p == 0:
                    residual(i)
                    dve.wait_ge(s["gain_in"], 16 * (stage + 1))
                dve.wait_ge(s["sq_done"], j + 1)
                v.tensor_scalar(ssum[0:r, j, 1:2], ssum[0:r, j, 0:1], 1.0 / D, EPS, ALU.mult, ALU.add).then_inc(s["ms_done"], 1)
                if p + 1 < len(same):
                    residual(same[p + 1])
                dve.wait_ge(s["rt_done"], j + 1)
                link(v.reciprocal(ssum[0:r, j, 3:4], ssum[0:r, j, 2:3]))
                v.scalar_tensor_tensor(hb[j % 2][0:r, :], xb[j % 2][0:r, :], ssum[0:r, j, 3:4], gain[0:r, :],
                                       ALU.mult, ALU.mult).then_inc(s["h_done"], 1)
                if p > 0:
                    late(same[p - 1])
                if p + 1 == len(same):
                    late(i)

            def bcast(ap, shape):
                return ap.to_broadcast(shape)

            link(v.memset(epsb[:, :], EPS))
            for what, i in order:
                if what == "mem":
                    evac_lo(i, i * P, P)
                    if i == 0:
                        split_lo(0)
                elif what == "block":
                    if i + 1 < NBLK:
                        split_lo(i + 1)
                    read_out(i)
                elif what == "norm":
                    norm_step(i)
                elif what == "gate":
                    dve.wait_ge(s["masks_rdy"], 1)
                    for b in range(QB):
                        u = use_z(b)
                        dve.wait_ge(free[u % 2], u // 2 + 1)
                        v.scalar_tensor_tensor(tmp[b][:, 0:COLS], zT[:, b, :], -1.0, zT[:, b, :], ALU.mult, ALU.max).then_inc(s["z_abs"], 1)
                    for b in range(QB):
                        dve.wait_ge(s["z_ln"], b + 1)
                        link(v.scalar_tensor_tensor(zT[:, b, :], zT[:, b, :], 0.0, tmp[b][:, 0:COLS], ALU.min, ALU.subtract))
                        v.tensor_tensor_scan(zT[:, b, 0:SEQ], smask[:, :], zT[:, b, 0:SEQ], 0.0, ALU.mult, ALU.add).then_inc(s["la_done"], 1)
                elif what == "prep":
                    b = i
                    dve.wait_ge(s["la_done"], QB)
                    if b >= 1:
                        dve.wait_ge(s["p_e"], 4 * b)
                        dve.wait_ge(s["p_m"], 4 * b)
                    z3 = zT[:, b, 0:SEQ].rearrange("p (n c) -> p n c", c=CHUNK)
                    def c3(ap):
                        return ap[:, 0:SEQ].rearrange("p (n c) -> p n c", c=CHUNK)
                    v.tensor_tensor(c3(tmp[3]), bcast(z3[:, :, CHUNK - 1:CHUNK], [P, NCK, CHUNK]), z3, ALU.subtract).then_inc(s["p_d2"], 1)
                    v.tensor_tensor(c3(tmp[1]), z3, bcast(z3[:, :, CHUNK // 2:CHUNK // 2 + 1], [P, NCK, CHUNK]), ALU.subtract).then_inc(s["p_d1"], 1)
                    dve.wait_ge(s["p_e"], 4 * b + 1)
                    v.tensor_tensor(qe[:, b, :], qT[:, b, 0:SEQ], tmp[0][:, 0:SEQ], ALU.mult).then_inc(s["p_m"], 1)
                    dve.wait_ge(s["p_e"], 4 * b + 2)
                    dve.wait_ge(s["p_x"], QB + b + 1)
                    dve.wait_ge(s["p_d1"], b + 1)
                    dve.wait_ge(free[use(at[("k", b)]) % 2], use(at[("k", b)]) // 2 + 1)
                    v.tensor_tensor(zT[:, b, 0:SEQ], kT[:, b, 0:SEQ], tmp[3][:, 0:SEQ], ALU.mult).then_inc(s["p_m"], 1)
                    dve.wait_ge(s["p_e"], 4 * b + 3)
                    dve.wait_ge(s["p_m"], 4 * b + 1)
                    v.tensor_tensor(qT[:, b, 0:SEQ], qT[:, b, 0:SEQ], tmp[2][:, 0:SEQ], ALU.mult).then_inc(s["p_m"], 1)
                    dve.wait_ge(s["p_e"], 4 * b + 4)
                    dve.wait_ge(s["p_m"], 4 * b + 2)
                    v.tensor_tensor(kT[:, b, 0:SEQ], kT[:, b, 0:SEQ], tmp[1][:, 0:SEQ], ALU.mult).then_inc(s["p_m"], 1)
                    if b == QB - 1:
                        dve.wait_ge(s["p_m"], 4 * QB)
                        for a in Am:
                            link(v.memset(a, 0.0))
                        v.memset(S[:, 0, :, :], 0.0).then_inc(s["prep_done"], 1)
                elif what == "gla":
                    t = i
                    dve.wait_ge(s["a_mm"], t + 1)
                    v.copy_predicated(Am[t % 2], bcast(cmask[:, :].bitcast(I32).unsqueeze(1).unsqueeze(1), [P, 2, QB, P]),
                                      lower4).then_inc(s["a_cp"], 1)
                    dve.wait_ge(s["a_ds"], t + 1)
                    if t >= 2:
                        dve.wait_ge(s["a_o"], t - 1)
                    for c in range(2):
                        n = 2 * t + c
                        for k in range(QB):
                            ins = v.scalar_tensor_tensor(S[:, (n + 1) % 4, k, :], S[:, n % 4, k, :], dec[:, k, n:n + 1],
                                                         spare(t)[:, 1 + c, k * DV:(k + 1) * DV], ALU.mult, ALU.add)
                            if c == 0 or k == 0:
                                link(ins)
                            else:
                                ins.then_inc(s["a_S"], 1)
                    dve.wait_ge(s["a_S"], t + 1)
                    dve.wait_ge(s["a_rt"], t + 1)
                    link(v.reciprocal(grt[:, :], grt[:, :]))
                    o3 = feat[:, 0:VB, t * P:(t + 1) * P].rearrange("p (k q) n -> p q k n", q=2)
                    v.tensor_tensor(o3, o3, grt[:, :].rearrange("p (q k n) -> p q k n", q=2, k=QB), ALU.mult).then_inc(s["a_norm"], 1)
                elif what == "glasample":
                    dve.wait_ge(s["a_o"], NT)
                    v.tensor_copy(sel_g, bcast(ident[0:DB, 0:DB].unsqueeze(2), [DB, DB, P])).then_inc(s["gs_a"], 1)
                    for b in range(DB):
                        dve.wait_ge(s["gs_bc"], b + 1)
                        for half in range(2):
                            r = slice(half * DK, (half + 1) * DK)
                            ins = v.tensor_tensor(KV[r, :, b, :],
                                                  T[r, b % 2, :].rearrange("p (k h v) -> p k h v", k=QB, h=2)[:, :, half, :],
                                                  bcast(kT[r, :, SEQ + b:SEQ + b + 1], [DK, QB, DV]), ALU.mult)
                            if half == 0:
                                link(ins)
                        ins.then_inc(s["gs_kv"], 1)
                    dve.wait_ge(s["gs_kv"], DB)
                    dve.wait_ge(s["gs_in"], 16 * QB)
                    for k in range(QB):
                        link(v.tensor_tensor(S0[:, k], S0[:, k], bcast(adec[:, k, :].unsqueeze(2), [P, DB, DV]), ALU.mult))
                    for k in range(QB):
                        ins = v.tensor_tensor(S0[:, k], S0[:, k], KV[:, k], ALU.add)
                        if k < QB - 1:
                            link(ins)
                    ins.then_inc(s["gs_sn"], 1)
                    dve.wait_ge(s["gs_rt"], 1)
                    n = HEADS * DB
                    link(v.reciprocal(grt[:, 0:n], grt[:, 0:n]))
                    o3 = feat[:, 0:VB, SEQ:COLS].rearrange("p (k q) b -> p q k b", q=2)
                    dve.wait_ge(s["gs_oev"], 1)
                    link(v.tensor_tensor(o3, o3, grt[:, 0:n].rearrange("p (q k b) -> p q k b", q=2, k=QB), ALU.mult))
                    for h in range(VB):
                        u = use(at[("g", h)])
                        dve.wait_ge(free[u % 2], u // 2 + 1)
                        ins = v.scalar_tensor_tensor(feat[:, h, :], feat[:, h, :], glag[:, h:h + 1], feat[:, VB + h, :], ALU.mult, ALU.mult)
                        if h < VB - 1:
                            link(ins)
                    ins.then_inc(s["yg_done"], 1)
                elif what == "ysplit":
                    for k in range(KB):
                        dve.wait_ge(s["ys_hi"], k + 1)
                        d, src = (CB + k, k) if k < VB else (k - VB, k)
                        v.tensor_tensor(act_lo[:, d, :], feat[:, src, :], act_hi[:, d, :], ALU.subtract).then_inc(s["ys_lo"], 1)
                elif what == "sq":
                    v.tensor_copy(sel_a, bcast(ident[0:DB, 0:DB].unsqueeze(2), [DB, DB, P])).then_inc(s["q_ev"], 1)
                elif what == "smax":
                    dve.wait_ge(s["q_t2"], 1)
                    link(v.reduce_max(sst[:, 0:1], back[0:DB * MH, 0, 0:MEM], AX.X))
                    v.tensor_scalar(sst[:, 1:2], sst[:, 0:1], -(DH ** -0.5), None, ALU.mult).then_inc(s["q_mx"], 1)
                    dve.wait_ge(s["q_ex"], 1)
                    link(v.reciprocal(sst[:, 3:4], sst[:, 2:3]))
                    v.tensor_scalar(sps[:, :], sps[:, :], sst[:, 3:4], None, ALU.mult).then_inc(s["q_pn"], 1)
                elif what == "sout":
                    dve.wait_ge(s["q_ohi"], 1)
                    v.tensor_tensor(act_lo[:, :, SEQ:COLS], G[0][:, 0, 0:KB * DB].rearrange("p (k b) -> p k b", k=KB),
                                    act_hi[:, :, SEQ:COLS], ALU.subtract).then_inc(s["q_olo"], 1)
                elif what == "att":
                    def key_scores(b):
                        if b >= 1:
                            dve.wait_ge(s["q_sc"], 2 * b)
                        dve.wait_ge(s[f"kc_in{b % 2}"], 16 * (b // 2 + 1))
                        for c in range(2):
                            dve.wait_ge(s["q_bc"], 2 * b + c + 1)
                            if c == 1:
                                dve.wait_ge(s["q_sc"], 2 * b + 1)
                            for m in range(MB):
                                for j in range(2):
                                    h = 2 * c + j
                                    ins = v.tensor_tensor_reduce(out=kprod, in0=cache[b % 2][:, m, h * DH:(h + 1) * DH],
                                                                 in1=G[c][:, 0, j * DH:(j + 1) * DH], scale=1.0, scalar=0.0,
                                                                 op0=ALU.mult, op1=ALU.add,
                                                                 accum_out=ksc[:, m, b * MH + h:b * MH + h + 1])
                                    if not (m == MB - 1 and j == 1):
                                        link(ins)
                            ins.then_inc(s["q_sc"], 1)

                    def maxima(t):
                        dve.wait_ge(s["s_mm"], t + 1)
                        pair = (T[:, :, :], back)[t % 2]
                        link(v.reduce_max(smx[:, t % 2, 0, :], pair.rearrange("p a (h m) -> p (a h) m", m=MEM), AX.X))
                        v.tensor_scalar(smx[:, t % 2, 1, :], smx[:, t % 2, 0, :], -(DH ** -0.5), None, ALU.mult).then_inc(s["s_mx"], 1)
                    if i == 0:
                        maxima(0)
                    if i + 1 < NT:
                        maxima(i + 1)
                    dve.wait_ge(s["s_e"], i + 1)
                    link(v.reciprocal(smx[:, i % 2, 3, :], smx[:, i % 2, 2, :]))
                    v.tensor_tensor(pr[i % 2], pr[i % 2], bcast(smx[:, i % 2, 3, :].unsqueeze(2), [P, MH, MEM]), ALU.mult).then_inc(s["s_p"], 1)
                    if i < NT // 2:
                        for b in range(i * PER, (i + 1) * PER):
                            key_scores(b)
                elif what == "pv":
                    for k in range(KB):
                        dve.wait_ge(s["s_pvhi"], i * KB + k + 1)
                        v.tensor_tensor(act_lo[:, k, i * HT:(i + 1) * HT], G[k % 2][:, 0, :], act_hi[:, k, i * HT:(i + 1) * HT],
                                        ALU.subtract).then_inc(s["s_pvlo"], 1)
            dve_moe(dve)


_INS = ['x_prompt', 'x_sample', 'state_conv', 'state_gla', 'cache_mem_k', 'cache_mem_v', 'mem_prompt', 'norm_mix', 'w_in',
        'conv_w', 'gla_gate_up', 'gla_gate_b', 'gla_out_norm', 'w_out', 'norm_mem', 'w_q', 'w_k', 'w_v', 'w_o', 'norm_ffn',
        'router_group', 'router_group_b', 'router_expert', 'router_expert_b', 'w_gate', 'w_up', 'w_down', 'norm_final']
_OUTS = [(1, 1024, 1024), (8, 1, 1024), (1, 1, 2, 512), (1, 1, 4, 64, 128), (1, 1, 256, 4, 256), (1, 1, 256, 4, 256),
         (1, 8, 2, 512), (1, 8, 4, 64, 128)]


def kernel(**inputs):
    import numpy as _np
    import concourse.bacc as _bacc
    from concourse import mybir as _mybir
    from concourse.bass_utils import run_bass_kernel_spmd as _run

    nc = _bacc.Bacc("TRN2", target_bir_lowering=False, num_devices=1)
    arrays, args = {}, []
    for name in _INS:
        a = _np.ascontiguousarray(inputs[name])
        arrays[f"in_{name}_dram"] = a
        args.append(nc.dram_tensor(f"in_{name}_dram", a.shape, _mybir.dt.from_np(a.dtype), kind="ExternalInput").ap())
    for i, shape in enumerate(_OUTS):
        args.append(nc.dram_tensor(f"out_{i}_dram", shape, _mybir.dt.float32, kind="ExternalOutput").ap())
    build(nc, *args)
    r = _run(nc, [arrays], core_ids=[0])
    return tuple(r.results[0][f"out_{i}_dram"] for i in range(len(_OUTS)))
```

```python
from contextlib import ExitStack

import concourse.bass as bass
from concourse import mybir

F32 = mybir.dt.float32
F32R = mybir.dt.float32r
BF16 = mybir.dt.bfloat16
I32 = mybir.dt.int32
U32 = mybir.dt.uint32
ALU = mybir.AluOpType
ACT = mybir.ActivationFunctionType
AX = mybir.AxisListType

P = 128


def build(nc, x_prompt, x_sample, state_conv, state_gla, cache_mem_k, cache_mem_v, mem_prompt,
          norm_mix, w_in, conv_w, gla_gate_up, gla_gate_b, gla_out_norm, w_out,
          norm_mem, w_q, w_k, w_v, w_o, norm_ffn, router_group, router_group_b,
          router_expert, router_expert_b, w_gate, w_up, w_down, norm_final,
          y_prompt, y_sample, new_conv_p, new_gla_p, new_mk, new_mv, new_conv_s, new_gla_s):
    D = x_prompt.shape[2]
    KB = D // P
    SEQ = x_prompt.shape[1]
    DB = x_sample.shape[0]
    NT = SEQ // P
    TILES = NT + 1
    COLS = SEQ + DB
    NCH = 3
    CH = COLS // NCH
    CONV = conv_w.shape[2]
    CB = CONV // P
    HEADS, DK, DV = 4, 64, 128
    QB = HEADS * DK // P
    VB = HEADS * DV // P
    CHUNK = 64
    NCK = SEQ // CHUNK
    MEM = mem_prompt.shape[1]
    MB = MEM // P
    MH, DH = 4, D // 4
    NG, EG = 4, 4
    NE = NG * EG
    FF = w_gate.shape[3]
    EPS = 1e-6
    STEPS = 2 * COLS // P + NE
    LEAST = COLS // P
    PAD = 1 << 14
    WR = 3
    rows = [P] * NT + [DB]

    win = w_in[0]
    c_q, c_k = 3 * CONV, 3 * CONV + QB * P
    c_v, c_g = c_k + QB * P, c_k + QB * P + VB * P
    c_lr = c_g + VB * P
    blocks, kinds = [], []

    def add(kind, i, w, c0, n=P):
        blocks.append((w, c0, n))
        kinds.append((kind, i))

    for i in range(KB):
        add("memk", i, w_k[0], i * P)
    for i in range(KB):
        add("memv", i, w_v[0], i * P)
    add("lr", 0, win, c_lr, 16)
    for i in range(QB):
        add("q", i, win, c_q + i * P)
    for i in range(QB):
        add("k", i, win, c_k + i * P)
    for i in range(VB):
        add("v", i, win, c_v + i * P)
    for i in range(CB):
        add("cc", i, win, CONV + i * P)
        add("ch", i, win, 2 * CONV + i * P)
        add("cb", i, win, i * P)
    for i in range(VB):
        add("g", i, win, c_g + i * P)
    for i in range(KB):
        add("out", i, w_out[0], i * P)
    for i in range(KB):
        add("mq", i, w_q[0], i * P)
    for i in range(KB):
        add("o", i, w_o[0], i * P)
    NBLK = len(blocks)
    at = {k: n for n, k in enumerate(kinds)}
    Z0 = at[("q", 0)] + 1
    def use(n):
        return n if n < Z0 else n + QB
    def use_z(i):
        return Z0 + i
    grp, cnt = [], []
    for u in range(NBLK + QB):
        beside_gla = use(at[("cc", 0)]) <= u <= use(at[("g", VB - 1)])
        g = 0 if beside_gla else (1 - grp[-1] if grp else 0)
        cnt.append(grp.count(g))
        grp.append(g)

    order = [("mem", t) for t in range(MB)]
    early = [("norm", t) for t in range(2, TILES)]
    for n in range(2 * KB):
        order.append(("block", n))
        if n >= 2 and n % 2 == 0 and early:
            order.append(early.pop(0))
    order += early + [("memout", 0), ("norm", 0), ("norm", 1)]
    order.append(("st", 0))
    for n in range(2 * KB, at[("cc", 0)]):
        order.append(("block", n))
        k, i = kinds[n]
        if (k, i) == ("q", 0):
            order.append(("gate", 0))
        if (k, i) == ("k", QB - 1):
            order.append(("prep", 0))
            order.append(("prep", 1))
        if k == "v":
            order.append(("vT", i))
    steps = []
    for t in range(NT):
        steps += [[("ga", t), ("gk", t)], [("gd", t)], [("go", t)], [("gm", t)]]
    PARTS = ((0, 3), (3, 6), (6, KB))
    steps += [[]] * (len(PARTS) * 3 * CB - len(steps))
    steps += [[("us", 0)]] + [[("gsb", b)] for b in range(0, DB, 2)] + [[("gso", 0)], [("gsm", 0)]]
    assert 4 * NT <= len(PARTS) * 3 * CB and len(steps) <= len(PARTS) * (3 * CB + VB)
    for n in range(at[("cc", 0)], at[("g", VB - 1)] + 1):
        order.append(("begin", n))
        for part in PARTS:
            if steps:
                order += steps.pop(0)
            order.append(("part", (n, part)))
        order.append(("end", n))
    order.append(("ysplit", 0))
    for i in range(KB):
        order.append(("block", at[("out", i)]))
    order += [("norm", TILES + t) for t in range(TILES)]
    for i in range(KB):
        order.append(("block", at[("mq", i)]))
    order += [("sq", 0)]
    order += [("att", t) for t in range(NT // 2)]
    order += [("smax", 0), ("pv", 0), ("sprob", 0)]
    order += [("att", NT // 2 + t) for t in range(NT // 2)]
    order += [("sout", 0), ("pv", 1)]
    PER = DB // (NT // 2)
    for i in range(KB):
        order.append(("block", at[("o", i)]))
    order += [("norm", 2 * TILES + t) for t in range(TILES)]
    norm_seq = [i for k, i in order if k == "norm"]
    nseq = {i: j for j, i in enumerate(norm_seq)}

    ctx = ExitStack()
    with ctx:
        def sb(name, shape, dt=F32):
            return ctx.enter_context(nc.sbuf_tensor(name, shape, dt))

        def pb(name, shape, dt=F32):
            return ctx.enter_context(nc.psum_tensor(name, shape, dt))

        def sem(name):
            return ctx.enter_context(nc.semaphore(name))

        def dram(name, shape, dt=F32):
            return nc.dram_tensor(name, shape, dt, kind="Internal").ap()

        d_mkT = dram("d_mkT", [P, KB * MEM])
        d_x1 = dram("d_x1", [COLS, D])
        d_x2 = dram("d_x2", [COLS, D])
        d_h3 = dram("d_h3", [COLS, D])
        d_y = dram("d_y", [2 * COLS, D])

        act_hi = sb("act_hi", [P, KB, COLS], F32R)
        act_lo = sb("act_lo", [P, KB, COLS], F32R)
        w_hi = sb("w_hi", [P, 2, KB, P], F32R)
        w_lo = sb("w_lo", [P, 2, KB, P], F32R)
        RAW = 3
        sizes = dict(feat=KB * COLS, vtm=TILES * VB * P, qk=2 * QB * COLS, zb=QB * COLS, tmp=4 * (COLS + 2),
                     qe=QB * SEQ, raw=RAW * KB * P, S=4 * QB * DV)
        base, tot = {}, 0
        for k, n in sizes.items():
            base[k] = tot
            tot += n
        arena = sb("arena", [P, tot])

        def region(k, off=0, n=None, parts=P):
            n = sizes[k] - off if n is None else n
            assert off + n <= sizes[k], (k, off, n)
            return arena[0:parts, base[k] + off:base[k] + off + n]

        ident = sb("ident", [P, P])
        ones = sb("ones", [P, P])
        tri = sb("tri", [P, P])
        cmask = sb("cmask", [P, P])
        smask = sb("smask", [P, SEQ], BF16)
        cw = sb("cw", [P, CB, 3])
        gateb = sb("gateb", [P, QB])
        glag = sb("glag", [P, VB])
        gup = sb("gup", [16, QB * P])
        rw = sb("rw", [P, KB, 20])
        rb = sb("rb", [P, 20])
        stT = sb("stT", [P, CB, 2 * DB])
        epsb = sb("epsb", [P, 1])
        sst = sb("sst", [DB * MH, 4])
        smx = sb("smx", [P, 2, 4, MH])
        ksc = sb("ksc", [P, MB, DB * MH])
        sps = sb("sps", [DB * MH, MEM])
        ssum = sb("ssum", [P, 3 * TILES + TILES, 4])
        dec = sb("dec", [P, QB, NCK])
        adec = sb("adec", [P, QB, DB])
        L = sb("L", [P, TILES, 20])

        raw = region("raw").rearrange("p (s k n) -> p s k n", s=RAW, k=KB)
        feat = region("feat").rearrange("p (k n) -> p k n", k=KB)
        vtm = region("vtm").rearrange("p (t n) -> p t n", t=TILES)
        qT = region("qk", 0, QB * COLS).rearrange("p (k n) -> p k n", k=QB)
        kT = region("qk", QB * COLS).rearrange("p (k n) -> p k n", k=QB)
        zT = region("zb").rearrange("p (k n) -> p k n", k=QB)
        qe = region("qe").rearrange("p (k n) -> p k n", k=QB)
        S = region("S").rearrange("p (s k v) -> p s k v", s=4, k=QB)
        gain = region("qe", 0, D)
        TW = COLS + 2
        tmp = [region("tmp", i * TW, TW) for i in range(4)]
        xb = [region("tmp", i * TW, D) for i in range(2)]
        hb = [region("tmp", (2 + i) * TW, D) for i in range(2)]
        lrT = region("qk", 3 * COLS, COLS, 16)
        S0 = region("qe").rearrange("p (k b v) -> p k b v", k=QB, b=DB)
        KV = region("zb", 0, QB * DB * DV).rearrange("p (k b v) -> p k b v", k=QB, b=DB)
        sel_g = region("tmp", 0, DB * P, DB).rearrange("q (b p) -> q b p", b=DB)
        sel_a = region("qe", D, DB * P, DB).rearrange("q (b p) -> q b p", b=DB)
        qs = region("S", 0, D, DB)
        cache = [region("tmp", i * MB * D, MB * D).rearrange("p (m d) -> p m d", m=MB) for i in range(2)]
        mkT = region("vtm", 0, KB * MEM).rearrange("p (k m) -> p k m", k=KB)
        mv_sb = region("vtm", KB * MEM, MB * D).rearrange("p (m d) -> p m d", m=MB)
        kprod = region("vtm", KB * MEM + MB * D, DH)
        pTz = region("vtm", KB * MEM + MB * D, MB * DB * DB * MH).rearrange("p (m b e) -> p m b e", m=MB, b=DB)
        so = region("S", 0, D, DB * MH)
        HT = SEQ // 2
        Am = [region("tmp", 2 * TW + i * HEADS * P, HEADS * P).rearrange("p (q k n) -> p q k n", q=2, k=QB) for i in range(2)]
        gsq = region("tmp", 3 * TW, HEADS * P)
        grt = region("tmp", 3 * TW + HEADS * P, HEADS * P)
        kdt = [region("tmp", i * QB * P, QB * P) for i in range(2)]
        pT = region("qk", 0, MH * MB * HT).rearrange("p (e n) -> p e n", e=MH * MB)
        pr = [region("zb", i * MH * MEM, MH * MEM).rearrange("p (h m) -> p h m", h=MH) for i in range(2)]
        h3T = [region("zb", i * D, D).rearrange("p (k n) -> p k n", k=KB) for i in range(2)]

        G = [pb("G0", [P, 3, 512]), pb("G1", [P, 3, 512])]
        T = pb("T", [P, 2, 512])
        lower4 = T[:, :, 0:QB * P].rearrange("p q (k n) -> p q k n", k=QB)
        fwd = [T[:, :, :], G[0][:, 1:3, :]]
        back = G[1][:, 1:3, :]


        def own_head(h):
            return T[:, 0, 0:KB * DB * MH].rearrange("p (k b e) -> p k b e", k=KB, e=MH)[:, 2 * h:2 * h + 2, :, h]

        names = """const_in ident_rdy masks_rdy raw_in0 raw_in1 raw_in2 hi_done split_done big_done free0 free1
        x_in0 x_in1 gain_in h_done sq_done ms_done rt_done fwd_done nhi_done nlo_done x_out0 x_out1 h_out0 h_out1 back_done res_done
        mem_in mk_spill mem_tm_tr mem_tm_ev mem_out
        st_in st_tr st_ev u_used g_used us_tr us_ev cs_out z_abs z_ln la_done
        p_d1 p_d2 p_e p_m p_x prep_done v_tr vt_ev
        a_mm a_kd a_cp a_kdt a_ds a_S a_o a_sq a_ms a_rt a_norm
        gs_in gs_bc gs_kv gs_a gs_sn gs_o gs_sq gs_ms gs_rt so_ev so_tr gs_out yg_done ys_hi ys_lo
        mk_in mv_in s_mm s_mx s_e s_p s_tr s_pT s_pv s_pvhi s_pvlo
        kc_in0 kc_in1 vc_in0 vc_in1 q_tr q_ev q_bc q_sc q_t2 q_mx q_ex q_pn q_t3 q_pT q_o q_ohi q_olo
        r_mm r_L r_ge r_gexp r_d r_dexp r_M r_rank r_slot r_tab iota_rdy r_seq l_tr l_ids
        wt_in0 wt_in1 wt_in2 wt_rdy moe_done xg_in0 xg_in1 tx_done hT_rdy gu_done sg_done hid_done ht_done hidT_rdy y_rdy y_out0 y_out1 xg_z
        c_x0 c_x1 c_in0 c_in1 c_in2 c_in3 c_y c_sq c_ms c_rt c_h c_out0 c_out1 c_out2 a_ch d_ch g_ch""".split()
        s = {n: sem(n) for n in names}
        raw_in = [s["raw_in0"], s["raw_in1"], s["raw_in2"]]
        free = [s["free0"], s["free1"]]
        x_in = [s["x_in0"], s["x_in1"]]

        x_out = [s["x_out0"], s["x_out1"]]
        h_out = [s["h_out0"], s["h_out1"]]

        def wait_x_out(eng, j):
            eng.wait_ge(x_out[j % 2], 16 * len([i for i in range(TILES, j + 1) if i % 2 == j % 2]))

        def wait_h_out(eng, j):
            eng.wait_ge(h_out[j % 2], 16 * len([i for i in range(2 * TILES, j + 1) if i % 2 == j % 2]))

        X = G[1]

        def wait_read(eng, n):
            eng.wait_ge(free[grp[use(n)]], cnt[use(n)] + 1)

        def wait_free(eng, n):
            for g in range(2):
                eng.wait_ge(free[g], grp[:use(n) + 1].count(g))

        links = {}

        def chain(eng, sm):
            count = [0]

            def link(ins):
                count[0] += 1
                ins.then_inc(sm, 1)
                eng.wait_ge(sm, count[0])
            return link

        def chunks(ap):
            return ap.rearrange("p (c n) -> p c n", c=NCH)

        xrows = [x_prompt[0, t * P:(t + 1) * P, :] for t in range(NT)] + [x_sample[:, 0, :]]
        yrows = [y_prompt[0, t * P:(t + 1) * P, :] for t in range(NT)] + [y_sample[:, 0, :]]

        def drows(d, t):
            return d[t * P:t * P + rows[t], :]

        const_loads = [
            (gateb[:, :], gla_gate_b[0].rearrange("(k p) -> p k", p=P)),
            (glag[:, :], gla_out_norm[0].rearrange("(k p) -> p k", p=P)),
            (gup[:, :], gla_gate_up[0]),
            (rw[:, :, 0:NG], router_group[0].rearrange("(k p) g -> p k g", p=P)),
            (rb[:, 0:NG], router_group_b[0].partition_broadcast(P)),
            (rb[:, NG:NG + NE], router_expert_b[0].rearrange("g e -> (g e)").partition_broadcast(P)),
        ] + [(rw[:, :, NG + g * EG:NG + (g + 1) * EG], router_expert[0, g].rearrange("(k p) e -> p k e", p=P)) for g in range(NG)] + [
            (cw[:, :, j], conv_w[0, j].rearrange("(k p) -> p k", p=P)) for j in range(3)]
        N_CONST = 16 * len(const_loads)
        memx = region("vtm", 0, MB * D).rearrange("p (m d) -> p m d", m=MB)
        mkT_w = region("vtm", MB * D, KB * MEM).rearrange("p (k m) -> p k m", k=KB)
        mvT_w = region("qk", 0, KB * MEM).rearrange("p (k m) -> p k m", k=KB)
        mtm = [region("qk", KB * MEM, MB * D).rearrange("p (m d) -> p m d", m=MB),
               region("feat", 0, MB * D).rearrange("p (m d) -> p m d", m=MB)]
        strow = region("feat", MB * D, CONV, 2 * DB)
        csrow = region("tmp", 2 * TW, CONV, 2 + DB)
        uend = sb("uend", [P, CB, 2 + DB])
        gsil = sb("gsil", [P, VB, DB])

        WSZ = KB * 2 * FF + (FF // P) * D
        o = WR * WSZ
        def take(n):
            taken[0] += n
            return arena[:, taken[0] - n:taken[0]]
        taken = [o]
        xg = [take(D) for _ in range(2)]
        hT = [take(D).rearrange("p (k n) -> p k n", k=KB) for _ in range(2)]
        sg = [take(FF) for _ in range(2)]
        hid = [take(FF) for _ in range(2)]
        hidT = [take(FF).rearrange("p (k n) -> p k n", k=FF // P) for _ in range(2)]
        yb = [take(D) for _ in range(2)]
        NTE = TILES * NE
        def t3(ap, a):
            return ap.rearrange("p (a b) -> p a b", a=a)
        M = t3(take(NTE), TILES)
        OH1 = t3(take(NTE), TILES)
        OH2 = t3(take(NTE), TILES)
        prod = t3(take(NTE), TILES)
        slotA = t3(take(NTE), TILES)
        totE = take(NTE)
        incE = take(NTE)
        tmask = take(NTE)
        cmp_ = t3(take(STEPS * NE), STEPS)
        ohg, oh1, oh2 = (t3(take(TILES * NG), TILES) for _ in range(3))
        esel, e2, ww, ee = (t3(take(TILES * EG), TILES) for _ in range(4))
        cj = take(NG)
        valid, gmx, wmx, gsm, m1, m2, dlt, wt1, wt2, slf = (take(TILES) for _ in range(10))
        tcnt, tend, tbase, one16 = (take(NE) for _ in range(4))
        stepf, est, em3, ec = (take(STEPS) for _ in range(4))
        active, seq, ids, ends = (take(NE) for _ in range(4))
        lastseq = take(1)
        posf = take(P)
        entry = take(2 * TILES).rearrange("p (c t) -> p c t", c=2)
        slotpf, slotsf = take(2 * TILES), take(2 * TILES)
        assert taken[0] <= tot, (taken, tot)
        n = 2 * TILES
        at_pos = arena[:, o + 2 * D:o + 2 * D + n * P].rearrange("p (i n) -> p i n", i=n)
        at_step = arena[:, o + 2 * D + n * P:o + 2 * D + n * (P + STEPS)].rearrange("p (i n) -> p i n", i=n)
        assert n * (P + STEPS) <= 4 * D + 6 * FF
        slotp = sb("slotp", [P, 2, TILES], I32)
        slot = sb("slot", [P, 2, TILES], I32)
        rid = sb("rid", [P, TILES, 2], I32)
        stepi = sb("stepi", [P, STEPS], I32)
        tci = sb("tci", [P, NE], I32)
        tab_off = sb("tab_off", [P, STEPS], I32)
        tab_need = sb("tab_need", [P, STEPS], I32)
        tab_id = sb("tab_id", [P, NE], I32)
        tab_end = sb("tab_end", [P, NE], I32)
        tab_last = sb("tab_last", [P, 2], I32)
        tab_pairs = sb("tab_pairs", [P, 1], I32)
        posi = sb("posi", [P, P], I32)
        ridx = sb("ridx", [P, STEPS], I32)
        tidx = sb("tidx", [P, STEPS], I32)
        wcol = sb("wcol", [P, 2, TILES])
        cst = sb("cst", [P, TILES, 4])
        GU = [G[0][:, 0, :], G[1][:, 0, :]]
        XT = T
        HTp = G[0][:, 1, 0:FF].rearrange("p (k n) -> p k n", k=FF // P)
        Y = G[1][:, 1:3, :]
        X_FIRST = WSZ // D - 1
        assert NE % WR == 1 and TILES - X_FIRST <= WSZ // D and WSZ >= 3 * 2 * D
        cg = arena[:, WSZ:WSZ + D]
        x2 = [arena[:, WSZ + (t + 1) * D:WSZ + (t + 2) * D] for t in range(TILES)]
        cy = [arena[:, i:i + 2 * D].rearrange("p (r d) -> p r d", r=2) for i in (0, 2 * D, 4 * D, o)]
        co = [arena[:, o + (2 + i) * D:o + (3 + i) * D] for i in range(3)]
        wt_in = [s["wt_in0"], s["wt_in1"], s["wt_in2"]]

        def step_pairs(eng):
            return eng.value_load(tab_pairs[0:1, 0:1], min_val=0, max_val=STEPS // 2 - LEAST) + LEAST

        def sp_moe(sp):
            def expert_id(e):
                return bass.ds(sp.value_load(tab_id[0:1, e:e + 1], min_val=0, max_val=NE - 1), 1)

            def load_expert(e, x):
                wv = arena[:, (e % WR) * WSZ:(e % WR + 1) * WSZ]
                gu = wv[:, 0:KB * 2 * FF].rearrange("p (k a f) -> p k a f", k=KB, a=2)
                sp.dma_start(gu[:, :, 0, :], w_gate[0, x].rearrange("o (k p) f -> p (o k) f", p=P)).then_inc(wt_in[e % WR], 16)
                sp.dma_start(gu[:, :, 1, :], w_up[0, x].rearrange("o (k p) f -> p (o k) f", p=P)).then_inc(wt_in[e % WR], 16)
                sp.dma_start(wv[:, KB * 2 * FF:].rearrange("p (k d) -> p k d", k=FF // P),
                             w_down[0, x].rearrange("o (k p) d -> p (o k) d", p=P)).then_inc(wt_in[e % WR], 16)

            def arrived(e):
                sp.wait_ge(wt_in[e % WR], 48 * (e // WR + 1))
                sp.sem_inc(s["wt_rdy"], 1)

            sp.wait_ge(s["r_mm"], TILES)
            sp.wait_ge(s["r_L"], TILES)
            sp.wait_ge(s["r_seq"], 1)
            for e in range(WR):
                x = expert_id(e)
                if e == WR - 1:
                    sp.wait_ge(s["xg_in0"], 16)
                    sp.wait_ge(s["xg_in1"], 16)
                load_expert(e, x)
            sp.wait_ge(s["r_tab"], 1)
            arrived(0)
            for e in range(NE):
                if e + 1 < NE:
                    arrived(e + 1)
                if e + WR < NE:
                    end = sp.value_load(tab_end[0:1, e:e + 1], min_val=1, max_val=STEPS + 1)
                    x = expert_id(e + WR)
                    sp.wait_ge(s["moe_done"], end)
                    load_expert(e + WR, x)
            end = sp.value_load(tab_end[0:1, NE - 3:NE - 2], min_val=1, max_val=STEPS + 1)
            for t in (3 * TILES - 1, 3 * TILES - 2):
                wait_x_out(sp, t)
            sp.wait_ge(s["moe_done"], end)
            for t in range(X_FIRST):
                sp.dma_start(x2[t][0:rows[t], :], drows(d_x2, t)).then_inc(s["c_x0"], 16)
            sp.dma_start(cg, norm_final.partition_broadcast(P)).then_inc(s["c_x0"], 16)
            steps_done = sp.value_load(tab_last[0:1, 0:1], min_val=2 * LEAST + 1, max_val=STEPS + 1)
            rows_out = sp.value_load(tab_last[0:1, 1:2], min_val=16 * LEAST, max_val=8 * STEPS)
            sp.wait_ge(s["moe_done"], steps_done)
            sp.wait_ge(s["y_out0"], rows_out)
            sp.wait_ge(s["y_out1"], rows_out)
            def load_y(t):
                r = rows[t]
                if t >= 4:
                    sp.wait_ge(s["c_sq"], t - 3)
                sp.dma_start(cy[t % 4][0:r], d_y[2 * t * P:2 * (t * P + r), :].rearrange("(p r) d -> p r d", r=2)).then_inc(s[f"c_in{t % 4}"], 16)

            for t in range(4):
                load_y(t)
            for t in range(X_FIRST, TILES):
                sp.dma_start(x2[t][0:rows[t], :], drows(d_x2, t)).then_inc(s["c_x1"], 16)
            for t in range(TILES):
                if t + 4 < TILES:
                    load_y(t + 4)
                sp.wait_ge(s["c_h"], t + 1)
                sp.dma_start(yrows[t], co[t % 3][0:rows[t], :]).then_inc(s[f"c_out{t % 3}"], 16)
            for i in range(3):
                sp.wait_ge(s[f"c_out{i}"], 16 * len(range(i, TILES, 3)))

        def pool_moe(pool):
            pool.iota(stepi[:, :], pattern=[[1, STEPS]], base=0, channel_multiplier=0)
            pool.iota(posi[:, :], pattern=[[1, P]], base=0, channel_multiplier=0)
            pool.iota(rid[:, :, :], pattern=[[2 * P, TILES], [1, 2]], base=0, channel_multiplier=2).then_inc(s["iota_rdy"], 1)
            pool.wait_ge(s["l_ids"], 1)
            wait_h_out(pool, 3 * TILES - 1)
            wait_h_out(pool, 3 * TILES - 2)
            pool.wait_ge(s["xg_z"], 1)

            def gather(t):
                if t >= 2:
                    pool.wait_ge(s["tx_done"], t - 1)
                pool.indirect_dma_start(out=xg[t % 2], out_offset=None, in_=d_h3,
                                        in_offset=bass.IndirectOffsetOnAxis(ap=tidx[:, t:t + 1].bitcast(U32), axis=0),
                                        bounds_check=COLS - 1, oob_is_err=False).then_inc(s[f"xg_in{t % 2}"], 16)

            def scatter(t):
                pool.wait_ge(s["y_rdy"], t + 1)
                pool.indirect_dma_start(out=d_y, out_offset=bass.IndirectOffsetOnAxis(ap=ridx[:, t:t + 1].bitcast(U32), axis=0),
                                        in_=yb[t % 2], in_offset=None, bounds_check=2 * COLS - 1,
                                        oob_is_err=False).then_inc(s[f"y_out{t % 2}"], 16)
            pairs = step_pairs(pool)
            gather(0)
            gather(1)
            gather(2)
            gather(3)
            for i in range(STEPS // 2):
                with pool.If(pairs > i):
                    scatter(2 * i)
                if 2 * i + 4 < STEPS:
                    with pool.If(pairs > i + 2):
                        gather(2 * i + 4)
                with pool.If(pairs > i):
                    scatter(2 * i + 1)
                if 2 * i + 4 < STEPS:
                    with pool.If(pairs > i + 2):
                        gather(2 * i + 5)

        def pe_moe(pe):
            pe.wait_ge(s["r_M"], 1)
            pe.matmul(T[:, 0, 0:NTE], tri[:, :], M.rearrange("p a b -> p (a b)"), start=True, stop=True)
            pe.matmul(T[:, 1, 0:NTE], ones[:, :], M.rearrange("p a b -> p (a b)"), start=True, stop=True).then_inc(s["r_rank"], 1)
            pe.wait_ge(s["r_slot"], 1)
            for i in range(2 * TILES):
                ins = pe.matmul(G[0][:, 2, 0:STEPS], at_pos[:, i, :], at_step[:, i, :], start=(i == 0), stop=(i == 2 * TILES - 1))
            ins.then_inc(s["l_tr"], 1)
            pe.wait_ge(s["r_tab"], 1)
            pe.nop().then_inc(s["moe_done"], 1)

            def transpose_rows(b, n_in, hT_used):
                pe.wait_ge(s[f"xg_in{b}"], n_in)
                pe.wait_ge(s["hT_rdy"], hT_used)
                for k in range(KB):
                    ins = pe.transpose(XT[:, k // 4, (k % 4) * P:(k % 4 + 1) * P], xg[b][:, k * P:(k + 1) * P], ident[:, :])
                ins.then_inc(s["tx_done"], 1)

            def gate_up(b, step, rdy):
                off = pe.value_load(tab_off[0:1, step], min_val=0, max_val=(WR - 1) * WSZ)
                need = pe.value_load(tab_need[0:1, step], min_val=1, max_val=NE)
                pe.wait_ge(s["wt_rdy"], need)
                pe.wait_ge(s["hT_rdy"], rdy)
                for k in range(KB):
                    ins = pe.matmul(GU[b], hT[b][:, k, :], arena[:, bass.ds(off + k * 2 * FF, 2 * FF)],
                                    start=(k == 0), stop=(k == KB - 1))
                ins.then_inc(s["gu_done"], 1)

            def hid_transpose(b, n):
                pe.wait_ge(s["hid_done"], n)
                for k in range(FF // P):
                    ins = pe.transpose(HTp[:, k, :], hid[b][:, k * P:(k + 1) * P], ident[:, :])
                ins.then_inc(s["ht_done"], 1)

            def down(b, step, n, y_used):
                off = pe.value_load(tab_off[0:1, step], min_val=0, max_val=(WR - 1) * WSZ)
                pe.wait_ge(s["hidT_rdy"], n)
                if y_used is not None:
                    pe.wait_ge(s["y_rdy"], y_used)
                for c in range(D // 512):
                    for k in range(FF // P):
                        ins = pe.matmul(Y[:, c, :], hidT[b][:, k, :],
                                        arena[:, bass.ds(off + KB * 2 * FF + k * D + c * 512, 512)],
                                        start=(k == 0), stop=(k == FF // P - 1))
                ins.then_inc(s["moe_done"], 1)

            pe.wait_ge(s["xg_in0"], 16)
            for k in range(KB):
                ins = pe.transpose(XT[:, k // 4, (k % 4) * P:(k % 4 + 1) * P], xg[0][:, k * P:(k + 1) * P], ident[:, :])
            ins.then_inc(s["tx_done"], 1)
            gate_up(0, slice(0, 1), 1)
            transpose_rows(1, 16, 1)
            hid_transpose(0, 1)
            for t in (1, 2):
                gate_up(t % 2, slice(t, t + 1), t + 1)
                transpose_rows(1 - t % 2, 32, t + 1)
                down(1 - t % 2, slice(t - 1, t), t, t - 1 if t > 1 else None)
                hid_transpose(t % 2, t + 1)
            pairs = step_pairs(pe)
            with pe.Fori(1, STEPS // 2 - 1) as it:
                with pe.If(it < pairs - 1):
                    for b in (1, 0):
                        t = 2 * it + (2 - b)
                        gate_up(b, bass.ds(t, 1), t + 1)
                        transpose_rows(1 - b, 16 * (it + 2), t + 1)
                        down(1 - b, bass.ds(t - 1, 1), t, t - 1)
                        hid_transpose(b, t + 1)
            t = 2 * pairs - 1
            gate_up(1, bass.ds(t, 1), t + 1)
            down(0, bass.ds(t - 1, 1), t, t - 1)
            hid_transpose(1, t + 1)
            down(1, bass.ds(t, 1), t + 1, t)

        def act_moe(act):
            act.wait_ge(s["r_ge"], 1)
            act.activation(ee, ee, ACT.Exp).then_inc(s["r_gexp"], 1)
            act.wait_ge(s["r_d"], 1)
            act.activation(dlt, dlt, ACT.Exp).then_inc(s["r_dexp"], 1)

            def rows_in(b, n):
                act.wait_ge(s["tx_done"], n)
                act.copy(hT[b], XT[:, :, :].rearrange("p a (k n) -> p (a k) n", n=P)).then_inc(s["hT_rdy"], 1)

            def gate(b, n):
                act.wait_ge(s["gu_done"], n)
                act.activation(sg[b], GU[b][:, 0:FF], ACT.Silu).then_inc(s["sg_done"], 1)

            def hidden(b, n):
                act.wait_ge(s["ht_done"], n)
                act.copy(hidT[b], HTp).then_inc(s["hidT_rdy"], 1)

            rows_in(0, 1)
            act.wait_ge(s["r_tab"], 1)
            pairs = step_pairs(act)
            with act.Fori(0, STEPS // 2 - 1) as it:
                with act.If(it < pairs - 1):
                    for b in (0, 1):
                        t = 2 * it + b
                        gate(b, t + 1)
                        rows_in(1 - b, t + 2)
                        hidden(b, t + 1)
            last = 2 * pairs
            gate(0, last - 1)
            rows_in(1, last)
            hidden(0, last - 1)
            gate(1, last)
            hidden(1, last)
            for t in range(TILES):
                r = rows[t]
                act.wait_ge(s["c_y"], t + 1)
                act.activation(cy[t % 4][0:r, 0, :], x2[t][0:r, :], ACT.Square, accum_out=cst[0:r, t, 0:1]).then_inc(s["c_sq"], 1)
                act.wait_ge(s["c_ms"], t + 1)
                act.activation(cst[0:r, t, 2:3], cst[0:r, t, 1:2], ACT.Sqrt).then_inc(s["c_rt"], 1)

        def dve_moe(dve):
            link = links["dve"]
            v = nc.vector
            def bc(ap, shape):
                return ap.to_broadcast(shape)
            dve.wait_ge(s["iota_rdy"], 1)
            for j in range(NG):
                link(v.memset(cj[:, j:j + 1], float(NG - j)))
            link(v.memset(valid, 1.0))
            link(v.memset(valid[:, NT:TILES], 0.0))
            link(v.memset(valid[0:DB, NT:TILES], 1.0))
            link(v.memset(tmask, 1.0))
            link(v.memset(t3(tmask, NE)[:, :, 0:1], 0.0))
            link(v.memset(one16, 1.0))
            link(v.tensor_copy(stepf, stepi[:, :]))
            link(v.tensor_copy(posf, posi[:, :]))
            link(v.tensor_copy(entry, rid[:, :, :].rearrange("p t c -> p c t")))
            link(v.tensor_scalar(entry, entry, -float(PAD), None, ALU.add))
            link(v.tensor_tensor(entry, entry, bc(valid.unsqueeze(1), [P, 2, TILES]), ALU.mult))
            dve.wait_ge(s["r_L"], TILES)
            link(v.tensor_tensor(L[:, :, :], L[:, :, :], bc(rb[:, :].unsqueeze(1), [P, TILES, 20]), ALU.add))
            gl = L[:, :, 0:NG]
            el = L[:, :, NG:20].rearrange("p t (g e) -> p t g e", g=NG)

            def first_max(vals, mx, oh):
                link(v.reduce_max(mx, vals, AX.X))
                link(v.tensor_tensor(oh, vals, bc(mx.unsqueeze(2), [P, TILES, NG]), ALU.is_equal))
                link(v.tensor_tensor(ww, oh, bc(cj.unsqueeze(1), [P, TILES, NG]), ALU.mult))
                link(v.reduce_max(wmx, ww, AX.X))
                link(v.tensor_tensor(oh, ww, bc(wmx.unsqueeze(2), [P, TILES, NG]), ALU.is_equal))

            first_max(gl, gmx, ohg)
            v.tensor_tensor(ee, gl, bc(gmx.unsqueeze(2), [P, TILES, NG]), ALU.subtract).then_inc(s["r_ge"], 1)
            p4 = prod.rearrange("p t (g e) -> p t g e", g=NG)
            for g in range(NG):
                link(v.tensor_tensor(p4[:, :, g, :], el[:, :, g, :], bc(ohg[:, :, g:g + 1], [P, TILES, EG]), ALU.mult))
            link(v.reduce_sum(esel, p4.rearrange("p t g e -> p t e g"), AX.X))
            first_max(esel, m1, oh1)
            link(v.scalar_tensor_tensor(e2, oh1, -1e30, esel, ALU.mult, ALU.add))
            first_max(e2, m2, oh2)
            v.tensor_tensor(dlt, m2, m1, ALU.subtract).then_inc(s["r_d"], 1)
            for oh, OH in ((oh1, OH1), (oh2, OH2)):
                o4 = OH.rearrange("p t (g e) -> p t g e", g=NG)
                for g in range(NG):
                    link(v.tensor_tensor(o4[:, :, g, :], oh, bc(ohg[:, :, g:g + 1], [P, TILES, EG]), ALU.mult))
                link(v.tensor_tensor(OH, OH, bc(valid.unsqueeze(2), [P, TILES, NE]), ALU.mult))
            v.tensor_tensor(M, OH1, OH2, ALU.add).then_inc(s["r_M"], 1)
            dve.wait_ge(s["r_gexp"], 1)
            link(v.reduce_sum(gsm, ee, AX.X))
            dve.wait_ge(s["r_dexp"], 1)
            link(v.tensor_scalar(wt1, dlt, 1.0, None, ALU.add))
            link(v.tensor_tensor(wt1, wt1, gsm, ALU.mult))
            link(v.reciprocal(wcol[:, 0, :], wt1))
            link(v.tensor_tensor(wcol[:, 1, :], wcol[:, 0, :], dlt, ALU.mult))
            dve.wait_ge(s["r_rank"], 1)
            link(v.tensor_copy(t3(totE, NE), T[:, 1, 0:NTE].rearrange("p (t e) -> p e t", t=TILES)))
            link(v.tensor_tensor_scan(incE, tmask, totE, 0.0, ALU.mult, ALU.add))
            counts = t3(incE, NE)[:, :, TILES - 1:TILES].rearrange("p e o -> p (e o)")
            link(v.tensor_scalar(tci[:, :], counts, float(P - 1), None, ALU.add))
            link(v.tensor_single_scalar(tci[:, :], tci[:, :], 7, ALU.logical_shift_right))
            link(v.tensor_copy(tcnt, tci[:, :]))
            link(v.tensor_tensor_scan(tend, one16, tcnt, 0.0, ALU.mult, ALU.add))
            link(v.tensor_tensor(tbase, tend, tcnt, ALU.subtract))
            link(v.tensor_scalar(tbase, tbase, float(P), None, ALU.mult))
            iota16 = stepf[:, 0:NE]
            pick = cmp_[:, 0:NE, :]
            picked = cmp_[:, NE:2 * NE, :]
            link(v.tensor_scalar(active, tcnt, 1.0, None, ALU.min))
            link(v.tensor_tensor_scan(seq, one16, active, 0.0, ALU.mult, ALU.add))
            link(v.tensor_scalar(lastseq, seq[:, NE - 1:NE], -1.0, None, ALU.add))
            link(v.tensor_tensor(seq, seq, active, ALU.subtract))
            link(v.tensor_tensor(pick, bc(seq.unsqueeze(1), [P, NE, NE]), bc(iota16.unsqueeze(2), [P, NE, NE]), ALU.is_equal))
            link(v.tensor_tensor(pick, pick, bc(active.unsqueeze(1), [P, NE, NE]), ALU.mult))
            link(v.tensor_tensor(picked, pick, bc(iota16.unsqueeze(1), [P, NE, NE]), ALU.mult))
            link(v.reduce_sum(ids, picked, AX.X))
            link(v.tensor_copy(tab_id[:, :], ids))
            link(v.tensor_tensor(picked, pick, bc(tend.unsqueeze(1), [P, NE, NE]), ALU.mult))
            link(v.reduce_sum(ends, picked, AX.X))
            link(v.reduce_sum(ids, pick, AX.X))
            link(v.tensor_scalar(ids, ids, -1.0, 1.0, ALU.mult, ALU.add))
            link(v.scalar_tensor_tensor(ends, ids, tend[:, NE - 1:NE], ends, ALU.mult, ALU.add))
            v.tensor_scalar(tab_end[:, :], ends, 1.0, None, ALU.add).then_inc(s["r_seq"], 1)
            link(v.tensor_tensor(incE, incE, totE, ALU.subtract))
            link(v.tensor_tensor(slotA, T[:, 0, 0:NTE].rearrange("p (t e) -> p t e", t=TILES),
                                 incE.rearrange("p (e t) -> p t e", t=TILES), ALU.add))
            link(v.tensor_tensor(slotA, slotA, bc(tbase.unsqueeze(1), [P, TILES, NE]), ALU.add))
            for c, OH in enumerate((OH1, OH2)):
                link(v.tensor_tensor(prod, slotA, OH, ALU.mult))
                link(v.reduce_sum(slf, prod, AX.X))
                link(v.tensor_copy(slot[:, c, :], slf))
            link(v.tensor_single_scalar(slotp[:, :, :], slot[:, :, :], P - 1, ALU.bitwise_and))
            link(v.tensor_single_scalar(slot[:, :, :], slot[:, :, :], 7, ALU.logical_shift_right))
            link(v.tensor_copy(slotpf, slotp[:, :, :].rearrange("p c t -> p (c t)")))
            link(v.tensor_copy(slotsf, slot[:, :, :].rearrange("p c t -> p (c t)")))
            n = 2 * TILES
            wait_h_out(dve, 3 * TILES - 1)
            wait_h_out(dve, 3 * TILES - 2)
            link(v.tensor_tensor(at_step, bc(slotsf.unsqueeze(2), [P, n, STEPS]), bc(stepf.unsqueeze(1), [P, n, STEPS]), ALU.is_equal))
            link(v.tensor_tensor(at_step, at_step, bc(entry.rearrange("p c t -> p (c t)").unsqueeze(2), [P, n, STEPS]), ALU.mult))
            v.tensor_tensor(at_pos, bc(slotpf.unsqueeze(2), [P, n, P]), bc(posf.unsqueeze(1), [P, n, P]), ALU.is_equal).then_inc(s["r_slot"], 1)
            link(v.tensor_tensor(cmp_, bc(tend.unsqueeze(1), [P, STEPS, NE]), bc(stepf.unsqueeze(2), [P, STEPS, NE]), ALU.is_le))
            link(v.tensor_tensor(cmp_, cmp_, bc(active.unsqueeze(1), [P, STEPS, NE]), ALU.mult))
            link(v.reduce_sum(est, cmp_, AX.X))
            link(v.tensor_scalar(est, est, lastseq, None, ALU.min))
            link(v.tensor_scalar(tab_need[:, :], est, 1.0, None, ALU.add))
            link(v.tensor_copy(em3, est))
            for j in range(WR, NE, WR):
                link(v.tensor_scalar(ec, est, float(j), -float(WR), ALU.is_ge, ALU.mult))
                link(v.tensor_tensor(em3, em3, ec, ALU.add))
            link(v.tensor_scalar(tab_off[:, :], em3, float(WSZ), None, ALU.mult))
            link(v.tensor_scalar(tab_pairs[:, :], tend[:, NE - 1:NE], 1.0, None, ALU.add))
            link(v.tensor_single_scalar(tab_pairs[:, :], tab_pairs[:, :], 1, ALU.logical_shift_right))
            link(v.tensor_scalar(tab_last[:, 0:1], tab_pairs[:, :], 2.0, 1.0, ALU.mult, ALU.add))
            link(v.tensor_scalar(tab_last[:, 1:2], tab_pairs[:, :], 16.0, None, ALU.mult))
            v.tensor_scalar(tab_pairs[:, :], tab_pairs[:, :], -float(LEAST), None, ALU.add).then_inc(s["r_tab"], 1)
            dve.wait_ge(s["r_tab"], 1)
            link(v.memset(xg[0], 0.0))
            v.memset(xg[1], 0.0).then_inc(s["xg_z"], 1)
            dve.wait_ge(s["l_tr"], 1)
            link(v.tensor_scalar(ridx[:, :], G[0][:, 2, 0:STEPS], float(PAD), None, ALU.add))
            v.tensor_single_scalar(tidx[:, :], ridx[:, :], 1, ALU.logical_shift_right).then_inc(s["l_ids"], 1)

            def product(b, n, used):
                dve.wait_ge(s["sg_done"], n)
                if used is not None:
                    dve.wait_ge(s["ht_done"], used)
                v.tensor_tensor(hid[b], GU[b][:, FF:2 * FF], sg[b], ALU.mult).then_inc(s["hid_done"], 1)

            def out_rows(b, n, stored):
                dve.wait_ge(s["moe_done"], n)
                if stored is not None:
                    dve.wait_ge(s[f"y_out{b}"], stored)
                v.tensor_copy(yb[b].rearrange("p (a n) -> p a n", a=2), Y).then_inc(s["y_rdy"], 1)

            product(0, 1, None)
            product(1, 2, None)
            out_rows(0, 2, None)
            product(0, 3, 1)
            out_rows(1, 3, None)
            pairs = step_pairs(dve)
            with dve.Fori(1, STEPS // 2 - 1) as it:
                with dve.If(it < pairs - 1):
                    for b in (1, 0):
                        t = 2 * it + (2 - b)
                        product(b, t + 1, t - 1)
                        out_rows(1 - b, t + 1, 16 * it)
            last = 2 * pairs
            product(1, last, last - 2)
            out_rows(0, last, 16 * (pairs - 1))
            out_rows(1, last + 1, 16 * (pairs - 1))
            def choice(t, c):
                r = rows[t]
                if c == 0 and t == X_FIRST:
                    dve.wait_ge(s["c_x1"], 16 * (TILES - X_FIRST))
                if c == 0:
                    dve.wait_ge(s[f"c_in{t % 4}"], 16 * (t // 4 + 1))
                x = x2[t][0:r, :]
                ins = v.scalar_tensor_tensor(x, cy[t % 4][0:r, c, :], wcol[0:r, c, t:t + 1],
                                             x, ALU.mult, ALU.add)
                if c == 0:
                    link(ins)
                else:
                    ins.then_inc(s["c_y"], 1)
            dve.wait_ge(s["c_x0"], 16 * (X_FIRST + 1))
            choice(0, 0)
            choice(0, 1)
            for t in range(TILES):
                r = rows[t]
                if t + 1 < TILES:
                    choice(t + 1, 0)
                dve.wait_ge(s["c_sq"], t + 1)
                v.tensor_scalar(cst[0:r, t, 1:2], cst[0:r, t, 0:1], 1.0 / D, EPS, ALU.mult, ALU.add).then_inc(s["c_ms"], 1)
                if t + 1 < TILES:
                    choice(t + 1, 1)
                dve.wait_ge(s["c_rt"], t + 1)
                link(v.reciprocal(cst[0:r, t, 3:4], cst[0:r, t, 2:3]))
                if t >= 3:
                    dve.wait_ge(s[f"c_out{t % 3}"], 16 * (t // 3))
                v.scalar_tensor_tensor(co[t % 3][0:r, :], x2[t][0:r, :], cst[0:r, t, 3:4], cg[0:r, :], ALU.mult, ALU.mult).then_inc(s["c_h"], 1)

        block = ctx.enter_context(nc.Block())

        @block.sync
        def _(sp):

            def load_block(n):
                w, c0, width = blocks[n]
                if n >= RAW:
                    sp.wait_ge(s["split_done"], n - RAW + 1)
                sp.dma_start(raw[:, n % RAW, :, 0:width],
                             w[:, c0:c0 + width].rearrange("(k p) n -> p k n", p=P)).then_inc(raw_in[n % RAW], 16)

            def load_x(i):
                j, stage, t = nseq[i], i // TILES, i % TILES
                if j >= 2:
                    sp.wait_ge(s["h_done"], j - 1)
                if stage == 0:
                    src = xrows[t]
                elif stage == 1:
                    src = xrows[t]
                    if t >= 2:
                        wait_x_out(sp, j - 2)
                else:
                    src = drows(d_x1, t)
                    if t == 0:
                        wait_x_out(sp, 2 * TILES - 1)
                        wait_x_out(sp, 2 * TILES - 2)
                    if t >= 2:
                        wait_x_out(sp, j - 2)
                sp.dma_start(xb[j % 2][0:rows[t], :], src).then_inc(x_in[j % 2], 16)

            for m in range(MB):
                sp.dma_start(memx[:, m, :], mem_prompt[0, m * P:(m + 1) * P, :]).then_inc(s["mem_in"], 16)
            for n in range(RAW):
                load_block(n)
            sp.dma_start(gain, norm_mix[0].partition_broadcast(P)).then_inc(s["gain_in"], 16)
            sp.dma_start(strow, state_conv[0].rearrange("b j c -> (b j) c")).then_inc(s["st_in"], 16)
            for i in norm_seq[0:2]:
                load_x(i)
            for dst, src in const_loads:
                sp.dma_start(dst, src, allow_slow_non_contiguous=True).then_inc(s["const_in"], 16)
            sp.dma_start(new_conv_s[0, :, 0, :], state_conv[0, :, 1, :]).then_inc(s["cs_out"], 16)

            nb = RAW
            for what, i in order:
                if what in ("block", "begin"):
                    if nb < NBLK:
                        load_block(nb)
                        nb += 1
                elif what == "norm":
                    j, stage, t = nseq[i], i // TILES, i % TILES
                    if stage == 1:
                        sp.wait_ge(s["res_done"], t + 1)
                        sp.dma_start(drows(d_x1, t), xb[j % 2][0:rows[t], :]).then_inc(x_out[j % 2], 16)
                    if stage == 2:
                        sp.wait_ge(s["res_done"], TILES + t + 1)
                        sp.dma_start(drows(d_x2, t), xb[j % 2][0:rows[t], :]).then_inc(x_out[j % 2], 16)
                        sp.wait_ge(s["h_done"], j + 1)
                        sp.dma_start(drows(d_h3, t), hb[j % 2][0:rows[t], :]).then_inc(h_out[j % 2], 16)
                    if j + 2 < len(norm_seq) and norm_seq[j + 2] // TILES == stage:
                        load_x(norm_seq[j + 2])
                elif what == "memout":
                    sp.wait_ge(s["mem_tm_ev"], 2 * MB)
                    for o, (dst, r) in enumerate(((new_mk, mtm[0]), (new_mv, mtm[1]))):
                        for m in range(MB):
                            sp.dma_start(dst[0, 0, m * P:(m + 1) * P].rearrange("m h d -> m (h d)"),
                                         r[:, m, :]).then_inc(s["mem_out"], 16)
                    sp.dma_start(d_mkT, region("vtm", MB * D, KB * MEM)).then_inc(s["mk_spill"], 16)
                elif what == "us":
                    sp.wait_ge(s["a_o"], NT)
                    for k in range(QB):
                        sp.dma_start(S0[:, k, :, :], state_gla[0, :, 2 * k:2 * k + 2].rearrange("b h d v -> (h d) b v")).then_inc(s["gs_in"], 16)
                    sp.wait_ge(s["a_S"], NT)
                    for k in range(QB):
                        sp.dma_start(new_gla_p[0, 0, 2 * k:2 * k + 2].rearrange("h d v -> (h d) v"), S[:, NCK % 4, k, :]).then_inc(s["gs_out"], 16)
                    sp.wait_ge(s["us_ev"], 1)
                    sp.dma_start(new_conv_p[0, 0], csrow[0:2, :]).then_inc(s["cs_out"], 16)
                    sp.dma_start(new_conv_s[0, :, 1, :], csrow[2:2 + DB, :]).then_inc(s["cs_out"], 16)
                elif what == "gsm":
                    sp.wait_ge(s["gs_sn"], 1)
                    for k in range(QB):
                        sp.dma_start(new_gla_s[0, :, 2 * k:2 * k + 2].rearrange("b h d v -> (h d) b v"), S0[:, k, :, :]).then_inc(s["gs_out"], 16)
                elif what == "ysplit":
                    sp.wait_ge(s["gs_o"], 1)
                    sp.wait_ge(s["gs_out"], 16 * 2 * QB)
                    sp.dma_start(gain, norm_mem[0].partition_broadcast(P)).then_inc(s["gain_in"], 16)
                    sp.wait_ge(s["yg_done"], 1)
                    load_x(norm_seq[TILES])
                    load_x(norm_seq[TILES + 1])
                elif what == "sq":
                    sp.wait_ge(s["gs_bc"], DB)
                    sp.wait_ge(s["mk_spill"], 16)
                    sp.wait_ge(s["mem_out"], 16 * 2 * MB)
                    sp.dma_start(region("vtm", 0, KB * MEM), d_mkT).then_inc(s["mk_in"], 16)
                    for m in range(MB):
                        sp.dma_start(mv_sb[:, m, :], new_mv[0, 0, m * P:(m + 1) * P].rearrange("m h d -> m (h d)")).then_inc(s["mv_in"], 16)
                    sp.wait_ge(s["h_done"], 2 * TILES)
                    wait_x_out(sp, 2 * TILES - 1)
                    wait_x_out(sp, 2 * TILES - 2)
                    sp.wait_ge(s["fwd_done"], MB + 2 * TILES)
                    for b in range(DB):
                        if b >= 2:
                            sp.wait_ge(s["q_sc"], 2 * b - 2)
                        sp.dma_start(cache[b % 2], cache_mem_k[0, b].rearrange("(m p) h d -> p m (h d)", p=P)).then_inc(s[f"kc_in{b % 2}"], 16)
                    for b in range(DB):
                        sp.wait_ge(s["q_sc"], 2 * DB - (2 if b == 0 else 0))
                        if b >= 2:
                            sp.wait_ge(s["q_o"], b - 1)
                        sp.dma_start(cache[b % 2], cache_mem_v[0, b].rearrange("(m p) h d -> p m (h d)", p=P)).then_inc(s[f"vc_in{b % 2}"], 16)
                elif what == "pv" and i == 1:
                    sp.wait_ge(s["q_o"], DB)
                    sp.wait_ge(s["h_done"], 2 * TILES)
                    sp.wait_ge(s["q_bc"], 2 * DB)
                    sp.dma_start(gain, norm_ffn[0].partition_broadcast(P)).then_inc(s["gain_in"], 16)
                    load_x(norm_seq[2 * TILES])
                    load_x(norm_seq[2 * TILES + 1])
            sp_moe(sp)
            sp.wait_ge(s["cs_out"], 16 * 3)
            sp.wait_ge(s["gs_out"], 16 * 2 * QB)
            sp.wait_ge(s["mem_out"], 16 * 2 * MB)
            wait_x_out(sp, 2 * TILES - 1)
            wait_x_out(sp, 2 * TILES - 2)
            wait_h_out(sp, 3 * TILES - 1)
            wait_h_out(sp, 3 * TILES - 2)
            sp.wait_ge(s["mk_spill"], 16)

        @block.gpsimd
        def _(pool):
            link = chain(pool, s["g_ch"])
            link(pool.memset(ident[:, :], 0.0))
            pool.affine_select(out=ident[:, :], in_=ident[:, :], compare_op=ALU.not_equal, fill=1.0, base=0,
                               pattern=[[-1, P]], channel_multiplier=1).then_inc(s["ident_rdy"], 1)
            link(pool.memset(ones[:, :], 1.0))
            link(pool.memset(tri[:, :], 1.0))
            link(pool.memset(cmask[:, :], 1.0))
            link(pool.affine_select(out=tri[:, :], in_=tri[:, :], compare_op=ALU.is_gt, fill=0.0, base=0,
                                    pattern=[[1, P]], channel_multiplier=-1))
            link(pool.affine_select(out=cmask[:, :], in_=cmask[:, :], compare_op=ALU.is_ge, fill=0.0, base=0,
                                    pattern=[[1, P]], channel_multiplier=-1))
            link(pool.memset(cmask[0:CHUNK, CHUNK:P], 0.0))
            link(pool.memset(smask[:, :], 1.0))
            link(pool.memset(smask[:, :].rearrange("p (n c) -> p n c", c=CHUNK)[:, :, 0:1], 0.0))
            pool.memset(L[:, :, :], 0.0).then_inc(s["masks_rdy"], 1)
            pool_moe(pool)

        @block.tensor
        def _(pe):
            def mm3(out, a_hi, a_lo, b_hi, b_lo, first, last):
                pe.matmul(out, a_hi, b_hi, start=first, stop=False)
                pe.matmul(out, a_hi, b_lo, start=False, stop=False)
                return pe.matmul(out, a_lo, b_hi, start=False, stop=last)

            def stream(n, part=(0, KB)):
                kind, b = kinds[n]
                u, slot, width = use(n), n % 2, blocks[n][2]
                if part[0] == 0:
                    pe.wait_ge(s["split_done"], n + 1)
                    if cnt[u] > 0:
                        pe.wait_ge(free[grp[u]], cnt[u])
                spans = [(0, MEM)] if kind in ("memk", "memv") else [(c * CH, CH) for c in range(NCH)]
                ins = None
                for k in range(*part):
                    if (kind, b) == ("out", 0):
                        pe.wait_ge(s["ys_lo"], k + 1)
                    for c, (c0, cn) in enumerate(spans):
                        ins = mm3(G[grp[u]][0:width, c, 0:cn], w_hi[:, slot, k, 0:width], w_lo[:, slot, k, 0:width],
                                  act_hi[:, k, c0:c0 + cn], act_lo[:, k, c0:c0 + cn], k == 0, k == KB - 1)
                if part[1] == KB:
                    ins.then_inc(s["big_done"], 1)

            def forward(f, src, r):
                if f >= 2:
                    pe.wait_ge(s["nlo_done"], f - 1)
                for k in range(KB):
                    ins = pe.transpose(fwd[f % 2][:, k // 4, (k % 4) * P:(k % 4) * P + r],
                                       src[0:r, k * P:(k + 1) * P], ident[0:r, 0:r])
                ins.then_inc(s["fwd_done"], 1)

            def backward(t):
                r = rows[t]
                for k in range(KB):
                    ins = pe.transpose(back[0:r, k // 4, (k % 4) * P:(k % 4) * P + P],
                                       feat[:, k, t * P:t * P + r], ident[:, :])
                ins.then_inc(s["back_done"], 1)

            def router(t):
                j = nseq[2 * TILES + t]
                pe.wait_ge(s["nlo_done"], MB + j + 1)
                if t == 0:
                    pe.wait_ge(s["const_in"], N_CONST)
                if t >= 2:
                    pe.wait_ge(s["r_L"], t - 1)
                for k in range(KB):
                    ins = pe.matmul(G[t % 2][0:rows[t], 0, 0:20], h3T[j % 2][:, k, 0:rows[t]], rw[:, k, :],
                                    start=(k == 0), stop=(k == KB - 1))
                ins.then_inc(s["r_mm"], 1)

            pe.wait_ge(s["ident_rdy"], 1)
            for what, i in order:
                if what == "mem":
                    if i == 0:
                        pe.wait_ge(s["mem_in"], 16 * MB)
                    forward(i, memx[:, i, :], P)
                elif what == "block":
                    kind, b = kinds[i]
                    if i == 0:
                        pe.wait_ge(s["nlo_done"], MB)
                    if (kind, b) == ("lr", 0):
                        pe.wait_ge(s["mem_tm_ev"], 2 * MB)
                    if (kind, b) == ("out", 1 if grp[use(at[("out", 0)])] == 0 else 0):
                        pe.wait_ge(s["gs_rt"], 1)
                    if (kind, b) == ("mq", 0):
                        pe.wait_ge(s["nlo_done"], MB + 2 * TILES)
                    if (kind, b) == ("o", 0):
                        pe.wait_ge(s["s_pvlo"], 2 * KB)
                        pe.wait_ge(s["q_olo"], 1)
                    stream(i)
                elif what == "part":
                    stream(i[0], i[1])
                elif what == "memout":
                    wait_free(pe, 2 * KB - 1)
                    for o, src in enumerate((mkT_w, mvT_w)):
                        for m in range(MB):
                            if o * MB + m >= 1:
                                pe.wait_ge(s["mem_tm_ev"], o * MB + m)
                            for k in range(KB):
                                ins = pe.transpose(back[:, k // 4, (k % 4) * P:(k % 4 + 1) * P],
                                                   src[:, k, m * P:(m + 1) * P], ident[:, :])
                            ins.then_inc(s["mem_tm_tr"], 1)
                elif what == "norm":
                    j, stage, t = nseq[i], i // TILES, i % TILES
                    if stage >= 1:
                        if t == 0:
                            wait_free(pe, at[("out" if stage == 1 else "o", KB - 1)])
                            backward(0)
                        if t + 1 < TILES:
                            pe.wait_ge(s["res_done"], (stage - 1) * TILES + t + 1)
                            backward(t + 1)
                    pe.wait_ge(s["h_done"], j + 1)
                    forward(MB + j, hb[j % 2], rows[t])
                    if stage == 2:
                        if t >= 1:
                            router(t - 1)
                        if t == TILES - 1:
                            router(t)
                elif what == "st":
                    pe.wait_ge(s["nlo_done"], MB + TILES)
                    pe.wait_ge(s["st_in"], 16)
                    for k in range(CB):
                        ins = pe.transpose(T[:, 1, k * 2 * DB:(k + 1) * 2 * DB], strow[:, k * P:(k + 1) * P],
                                           ident[0:2 * DB, 0:2 * DB])
                    ins.then_inc(s["st_tr"], 1)
                elif what == "us":
                    pe.wait_ge(s["u_used"], CB)
                    pe.wait_ge(s["a_sq"], NT)
                    for k in range(CB):
                        ins = pe.transpose(T[0:2 + DB, 0, k * P:(k + 1) * P], uend[:, k, :], ident[:, :])
                    ins.then_inc(s["us_tr"], 1)
                elif what == "gate":
                    wait_read(pe, at[("lr", 0)])
                    pe.wait_ge(s["const_in"], N_CONST)
                    for b in range(QB):
                        u = use_z(b)
                        pe.wait_ge(free[grp[u]], cnt[u])
                        for c in range(NCH):
                            ins = pe.matmul(G[grp[u]][:, c, 0:CH], gup[:, b * P:(b + 1) * P],
                                            lrT[:, c * CH:(c + 1) * CH], start=True, stop=True)
                        ins.then_inc(s["big_done"], 1)
                elif what == "vT":
                    wait_free(pe, at[("v", i)])
                    if i == 0:
                        pe.wait_ge(s["st_ev"], 1)
                    else:
                        pe.wait_ge(s["vt_ev"], i)
                    for t in range(NT):
                        ins = pe.transpose(T[:, t // 4, (t % 4) * P:(t % 4 + 1) * P],
                                           feat[:, i, t * P:(t + 1) * P], ident[:, :])
                    ins.then_inc(s["v_tr"], 1)
                    if i == VB - 1:
                        pe.wait_ge(s["vt_ev"], VB)
                        for k in range(VB):
                            ins = pe.transpose(T[0:DB, 0, k * P:(k + 1) * P], feat[:, k, SEQ:COLS], ident[:, :])
                        ins.then_inc(s["v_tr"], 1)
                elif what == "ga":
                    t = i
                    if t == 0:
                        pe.wait_ge(s["prep_done"], 1)
                        pe.wait_ge(s["vt_ev"], VB + 1)
                        pe.wait_ge(s["masks_rdy"], 1)
                    else:
                        pe.wait_ge(s["a_sq"], t)
                    c0 = t * P
                    for q in range(2):
                        for k in range(QB):
                            ins = pe.matmul(T[:, q, k * P:(k + 1) * P], kT[q * DK:(q + 1) * DK, k, c0:c0 + P],
                                            qT[q * DK:(q + 1) * DK, k, c0:c0 + P], start=True, stop=True)
                    ins.then_inc(s["a_mm"], 1)
                elif what == "gk":
                    t = i
                    if t == 0:
                        wait_free(pe, at[("v", VB - 1)])
                    else:
                        pe.wait_ge(s["a_rt"], t)
                    for k in range(QB):
                        ins = pe.transpose(X[:, 0, k * P:(k + 1) * P], zT[:, k, t * P:(t + 1) * P], ident[:, :])
                    ins.then_inc(s["a_kd"], 1)
                elif what == "gd":
                    t = i
                    pe.wait_ge(s["a_kdt"], t + 1)
                    for c in range(2):
                        for h in range(HEADS):
                            r0, k = (h % 2) * DK, h // 2
                            ins = pe.matmul(X[r0:r0 + DK, 1 + c, k * DV:(k + 1) * DV],
                                            kdt[t % 2][c * CHUNK:(c + 1) * CHUNK, h * DK:(h + 1) * DK],
                                            vtm[c * CHUNK:(c + 1) * CHUNK, t, h * DV:(h + 1) * DV],
                                            start=True, stop=True)
                    ins.then_inc(s["a_ds"], 1)
                elif what == "go":
                    t, c0 = i, i * P
                    pe.wait_ge(s["a_cp"], t + 1)
                    pe.wait_ge(s["a_S"], t + 1)
                    for q in range(2):
                        for k in range(QB):
                            h = 2 * k + q
                            pe.matmul(T[:, q, k * P:(k + 1) * P], vtm[:, t, h * DV:(h + 1) * DV], Am[t % 2][:, q, k, :],
                                      start=True, stop=False)
                            for c in range(2):
                                a0 = k * P + c * CHUNK
                                ins = pe.matmul(T[:, q, a0:a0 + CHUNK], S[q * DK:(q + 1) * DK, (2 * t + c) % 4, k, :],
                                                qe[q * DK:(q + 1) * DK, k, c0 + c * CHUNK:c0 + (c + 1) * CHUNK],
                                                start=False, stop=(c == 1))
                    ins.then_inc(s["a_o"], 1)
                elif what == "gm":
                    pe.wait_ge(s["a_sq"], i + 1)
                    pe.matmul(X[:, 0, :], ones[:, :], gsq[:, :], start=True, stop=True).then_inc(s["a_ms"], 1)
                elif what == "gsb":
                    if i == 0:
                        pe.wait_ge(s["gs_a"], 1)
                        pe.wait_ge(s["us_ev"], 1)
                    for b in (i, i + 1):
                        if b >= 2:
                            pe.wait_ge(s["gs_kv"], b - 1)
                        pe.matmul(T[:, b % 2, :], sel_g[:, b, :], vtm[0:DB, NT, :], start=True,
                                  stop=True).then_inc(s["gs_bc"], 1)
                elif what == "gso":
                    pe.wait_ge(s["gs_sn"], 1)
                    for q in range(2):
                        for k in range(QB):
                            for b in range(DB):
                                ins = pe.matmul(T[:, q, k * DB + b:k * DB + b + 1], S0[q * DK:(q + 1) * DK, k, b, :],
                                                qT[q * DK:(q + 1) * DK, k, SEQ + b:SEQ + b + 1], start=True, stop=True)
                    ins.then_inc(s["gs_o"], 1)
                elif what == "gsm":
                    pe.wait_ge(s["gs_sq"], 1)
                    pe.wait_ge(s["a_rt"], NT)
                    pe.matmul(X[:, 0, 0:HEADS * DB], ones[:, :], gsq[:, 0:HEADS * DB], start=True,
                              stop=True).then_inc(s["gs_ms"], 1)
                elif what == "sq":
                    wait_free(pe, at[("mq", KB - 1)])
                    for k in range(KB):
                        ins = pe.transpose(back[0:DB, k // 4, (k % 4) * P:(k % 4 + 1) * P], feat[:, k, SEQ:COLS], ident[:, :])
                    ins.then_inc(s["q_tr"], 1)
                    pe.wait_ge(s["q_ev"], 2)
                elif what == "smax":
                    pe.wait_ge(s["q_sc"], 2 * DB)
                    pe.wait_ge(s["s_e"], NT // 2)
                    for m in range(MB):
                        ins = pe.transpose(back[0:DB * MH, 0, m * P:(m + 1) * P], ksc[:, m, :], ident[:, :])
                    ins.then_inc(s["q_t2"], 1)
                elif what == "sprob":
                    pe.wait_ge(s["q_pn"], 1)
                    for m in range(MB):
                        ins = pe.transpose(back[:, 1, m * DB * MH:(m + 1) * DB * MH], sps[:, m * P:(m + 1) * P],
                                           ident[0:DB * MH, 0:DB * MH])
                    ins.then_inc(s["q_t3"], 1)
                    pe.wait_ge(s["q_pT"], 1)
                elif what == "sout":
                    pe.wait_ge(s["so_ev"], 1)
                    pe.wait_ge(s["s_e"], NT)
                    for k in range(KB):
                        ins = pe.transpose(T[:, 0, k * DB * MH:(k + 1) * DB * MH], so[:, k * P:(k + 1) * P],
                                           ident[0:DB * MH, 0:DB * MH])
                    ins.then_inc(s["so_tr"], 1)
                elif what == "att":
                    def key_rows(b):
                        for c in range(2):
                            if b >= 1:
                                pe.wait_ge(s["q_sc"], 2 * b - 1 + c)
                            pe.matmul(G[c][:, 0, :], sel_a[:, b, :], qs[:, c * 512:(c + 1) * 512], start=True,
                                      stop=True).then_inc(s["q_bc"], 1)

                    def values(b):
                        if b == 0:
                            pe.wait_ge(s["s_pvlo"], KB)
                        pe.wait_ge(s[f"vc_in{b % 2}"], 16 * (b // 2 + 1))
                        for c in range(2):
                            for m in range(MB):
                                ins = pe.matmul(G[c][0:DB * MH, 0, :], pTz[:, m, b, :], cache[b % 2][:, m, c * 512:(c + 1) * 512],
                                                start=(b == 0 and m == 0), stop=(b == DB - 1 and m == MB - 1))
                        ins.then_inc(s["q_o"], 1)

                    beside = key_rows if i < NT // 2 else values
                    b0 = i % (NT // 2) * PER

                    def scores(t):
                        if t == 0:
                            pe.wait_ge(s["mk_in"], 16)
                        if t >= 2:
                            pe.wait_ge(s["s_e"], t - 1)
                        pair = (T[:, :, :], back)[t % 2]
                        for h in range(MH):
                            for kk in range(DH // P):
                                k = h * (DH // P) + kk
                                ins = pe.matmul(pair[:, h // 2, (h % 2) * MEM:(h % 2 + 1) * MEM],
                                                feat[:, k, t * P:(t + 1) * P], mkT[:, k, :],
                                                start=(kk == 0), stop=(kk == DH // P - 1))
                        ins.then_inc(s["s_mm"], 1)
                    if i == 0:
                        scores(0)
                    if i + 1 < NT:
                        scores(i + 1)
                    for b in range(b0, b0 + PER // 2):
                        beside(b)
                    pe.wait_ge(s["s_p"], i + 1)
                    if i >= 1:
                        pe.wait_ge(s["s_pT"], i)
                    for e in range(MH * MB):
                        ins = pe.transpose(G[0][:, 1 + e // 4, (e % 4) * P:(e % 4 + 1) * P],
                                           pr[i % 2][:, e // MB, (e % MB) * P:(e % MB + 1) * P], ident[:, :])
                    ins.then_inc(s["s_tr"], 1)
                    for b in range(b0 + PER // 2, b0 + PER):
                        beside(b)
                elif what == "pv":
                    if i == 0:
                        pe.wait_ge(s["mv_in"], 16 * MB)
                    pe.wait_ge(s["s_pT"], (i + 1) * (NT // 2))
                    for k in range(KB):
                        n = i * KB + k
                        if n >= 2:
                            pe.wait_ge(s["s_pvlo"], n - 1)
                        for m in range(MB):
                            ins = pe.matmul(G[k % 2][:, 0, :], mv_sb[:, m, k * P:(k + 1) * P],
                                            pT[:, (k * P // DH) * MB + m, :], start=(m == 0), stop=(m == MB - 1))
                        ins.then_inc(s["s_pv"], 1)
            pe_moe(pe)

        @block.scalar
        def _(act):
            link = chain(act, s["a_ch"])

            def split_hi(n):
                width = blocks[n][2]
                act.wait_ge(raw_in[n % RAW], 16 * (n // RAW + 1))
                if n >= 2:
                    act.wait_ge(s["big_done"], use(n - 2) + 1)
                act.copy(w_hi[:, n % 2, :, 0:width], raw[:, n % RAW, :, 0:width]).then_inc(s["hi_done"], 1)

            def evacuate(n):
                kind, b = kinds[n]
                u = use(n)
                if kind in ("ch", "cb"):
                    return
                act.wait_ge(s["big_done"], u + 1)
                src, dst, scale, fn = G[grp[u]][:, :, 0:CH], None, 1.0, None
                if kind == "memk":
                    src, dst = G[grp[u]][:, 0, 0:MEM], mkT_w[:, b, :]
                elif kind == "memv":
                    src, dst = G[grp[u]][:, 0, 0:MEM], mvT_w[:, b, :]
                elif kind == "cc":
                    if b >= 1:
                        act.wait_ge(s["u_used"], b)
                    else:
                        act.wait_ge(s["prep_done"], 1)
                    dst = chunks(tmp[1][:, 2:2 + COLS])
                elif kind == "lr":
                    act.wait_ge(s["mem_out"], 16 * 2 * MB)
                    src, dst = G[grp[u]][0:16, :, 0:CH], chunks(lrT)
                elif kind == "q":
                    dst, scale = chunks(qT[:, b, :]), DK ** -0.5
                elif kind == "k":
                    dst = chunks(kT[:, b, :])
                elif kind == "v":
                    if b == 0:
                        act.wait_ge(s["mk_spill"], 16)
                    dst = chunks(feat[:, b, :])
                elif kind == "g":
                    if b >= 1:
                        act.wait_ge(s["g_used"], b)
                    else:
                        act.wait_ge(s["u_used"], CB)
                    dst, fn = chunks(tmp[1][:, 0:COLS]), ACT.Silu
                elif kind == "out":
                    if b == 0:
                        act.wait_ge(s["ys_lo"], KB)
                    dst = chunks(feat[:, b, :])
                else:
                    dst = chunks(feat[:, b, :])
                if fn is not None:
                    ins = act.activation(dst, src, fn)
                elif scale != 1.0:
                    ins = act.activation(dst, src, ACT.Copy, scale=scale)
                else:
                    ins = act.copy(dst, src)
                ins.then_inc(free[grp[u]], 1)

            def evac_fwd(f, t, col0, r):
                act.wait_ge(s["fwd_done"], f + 1)
                act.copy(act_hi[:, :, col0:col0 + r], fwd[f % 2].rearrange("p a (k n) -> p (a k) n", n=P)[:, :, 0:r]).then_inc(s["nhi_done"], 1)

            def square(i):
                j, stage, t = nseq[i], i // TILES, i % TILES
                r = rows[t]
                if stage == 0:
                    act.wait_ge(x_in[j % 2], 16 * (j // 2 + 1))
                else:
                    act.wait_ge(s["res_done"], (stage - 1) * TILES + t + 1)
                if stage == 1 and t == 0:
                    act.wait_ge(s["cs_out"], 16 * 3)
                if j >= 2:
                    act.wait_ge(s["fwd_done"], MB + j - 1)
                if stage == 2 and t >= 2:
                    wait_h_out(act, j - 2)
                act.activation(hb[j % 2][0:r, :], xb[j % 2][0:r, :], ACT.Square,
                               accum_out=ssum[0:r, j, 0:1]).then_inc(s["sq_done"], 1)

            def late(i):
                j, stage, t = nseq[i], i // TILES, i % TILES
                f, r = MB + j, rows[t]
                if stage == 2:
                    act.wait_ge(s["fwd_done"], f + 1)
                    if t >= 2:
                        act.wait_ge(s["r_mm"], t - 1)
                    act.copy(h3T[j % 2][:, :, 0:r], fwd[f % 2].rearrange("p a (k n) -> p (a k) n", n=P)[:, :, 0:r]).then_inc(s["nlo_done"], 1)
                    for u in ([t - 2] if t >= 2 else []) + ([TILES - 2, TILES - 1] if t == TILES - 1 else []):
                        act.wait_ge(s["r_mm"], u + 1)
                        act.copy(L[0:rows[u], u, :], G[u % 2][0:rows[u], 0, 0:20]).then_inc(s["r_L"], 1)
                else:
                    if stage == 0 and t < MB:
                        act.wait_ge(s["big_done"], 2 * KB)
                    if stage == 1 and t == 0:
                        act.wait_ge(s["big_done"], use(at[("out", KB - 1)]) + 1)
                    evac_fwd(f, t, t * P, r)

            def norm_step(i):
                j, stage, t = nseq[i], i // TILES, i % TILES
                r = rows[t]
                same = [x for x in norm_seq if x // TILES == stage]
                p = same.index(i)
                for x in ([i] if p == 0 else []) + same[p + 1:p + 2]:
                    square(x)
                    jx, rx = nseq[x], rows[x % TILES]
                    act.wait_ge(s["ms_done"], jx + 1)
                    act.activation(ssum[0:rx, jx, 2:3], ssum[0:rx, jx, 1:2], ACT.Sqrt).then_inc(s["rt_done"], 1)
                late(i)

            for what, i in order:
                if what == "mem":
                    evac_fwd(i, i, i * P, P)
                    if i == 0:
                        split_hi(0)
                elif what in ("block", "begin", "end"):
                    if what != "end" and i + 1 < NBLK:
                        split_hi(i + 1)
                    if what != "begin":
                        evacuate(i)
                elif what == "norm":
                    if i // TILES == 2 and i % TILES == 0:
                        act.wait_ge(s["masks_rdy"], 1)
                    norm_step(i)
                elif what == "memout":
                    for n in range(2 * MB):
                        act.wait_ge(s["mem_tm_tr"], n + 1)
                        act.copy(mtm[n // MB][:, n % MB, :].rearrange("p (a n) -> p a n", a=2), back).then_inc(s["mem_tm_ev"], 1)
                elif what == "st":
                    act.wait_ge(s["st_tr"], 1)
                    act.copy(stT[:, :, :], T[:, 1, 0:CB * 2 * DB].rearrange("p (k n) -> p k n", k=CB)).then_inc(s["st_ev"], 1)
                elif what == "us":
                    act.wait_ge(s["us_tr"], 1)
                    act.wait_ge(s["a_o"], NT)
                    act.copy(csrow[:, :], T[0:2 + DB, 0, :]).then_inc(s["us_ev"], 1)
                elif what == "gate":
                    act.wait_ge(s["const_in"], N_CONST)
                    for b in range(QB):
                        u = use_z(b)
                        act.wait_ge(s["big_done"], u + 1)
                        act.activation(chunks(zT[:, b, :]), G[grp[u]][:, :, 0:CH], ACT.Identity,
                                       bias=gateb[:, b:b + 1]).then_inc(free[grp[u]], 1)
                    for b in range(QB):
                        act.wait_ge(s["z_abs"], b + 1)
                        link(act.activation(tmp[b][:, 0:COLS], tmp[b][:, 0:COLS], ACT.Exp, scale=-1.0))
                        act.activation(tmp[b][:, 0:COLS], tmp[b][:, 0:COLS], ACT.Ln, bias=1.0).then_inc(s["z_ln"], 1)
                elif what == "prep":
                    b = i
                    act.wait_ge(s["la_done"], QB)
                    inv = 1.0 / 16.0
                    if b == 0:
                        for k in range(QB):
                            act.activation(adec[:, k, :], zT[:, k, SEQ:COLS], ACT.Exp, scale=inv).then_inc(s["p_x"], 1)
                    act.activation(dec[:, b, :].rearrange("p (n o) -> p n o", o=1), zT[:, b, 0:SEQ].rearrange("p (n c) -> p n c", c=CHUNK)[:, :, CHUNK - 1:CHUNK],
                                   ACT.Exp, scale=inv).then_inc(s["p_x"], 1)
                    if b >= 1:
                        act.wait_ge(s["p_m"], 4 * b)
                    act.activation(tmp[0][:, 0:SEQ], zT[:, b, 0:SEQ], ACT.Exp, scale=inv).then_inc(s["p_e"], 1)
                    act.wait_ge(s["p_d2"], b + 1)
                    act.activation(tmp[3][:, 0:SEQ], tmp[3][:, 0:SEQ], ACT.Exp, scale=inv).then_inc(s["p_e"], 1)
                    act.wait_ge(s["p_d1"], b + 1)
                    act.activation(tmp[2][:, 0:SEQ], tmp[1][:, 0:SEQ], ACT.Exp, scale=inv).then_inc(s["p_e"], 1)
                    act.wait_ge(s["p_e"], 4 * b + 3)
                    act.activation(tmp[1][:, 0:SEQ], tmp[1][:, 0:SEQ], ACT.Exp, scale=-inv).then_inc(s["p_e"], 1)
                elif what == "vT":
                    act.wait_ge(s["v_tr"], i + 1)
                    act.copy(vtm[:, 0:NT, i * P:(i + 1) * P], T[:, :, :].rearrange("p a (t n) -> p (a t) n", n=P)).then_inc(s["vt_ev"], 1)
                    if i == VB - 1:
                        act.wait_ge(s["v_tr"], VB + 1)
                        act.copy(vtm[0:DB, NT, :], T[0:DB, 0, :]).then_inc(s["vt_ev"], 1)
                elif what == "gk":
                    if i == 0:
                        act.wait_ge(s["prep_done"], 1)
                    act.wait_ge(s["a_kd"], i + 1)
                    act.copy(kdt[i % 2][:, :], X[:, 0, 0:QB * P]).then_inc(s["a_kdt"], 1)
                elif what == "go":
                    t = i
                    act.wait_ge(s["a_o"], t + 1)
                    act.copy(feat[:, 0:VB, t * P:(t + 1) * P].rearrange("p (k q) n -> p q k n", q=2), lower4)
                    act.activation(gsq.rearrange("p (q n) -> p q n", q=2), T[:, :, 0:QB * P], ACT.Square).then_inc(s["a_sq"], 1)
                elif what == "gm":
                    act.wait_ge(s["a_ms"], i + 1)
                    if i >= 1:
                        act.wait_ge(s["a_norm"], i)
                    act.activation(grt, X[:, 0, :], ACT.Sqrt, scale=1.0 / DV, bias=epsb[:, 0:1]).then_inc(s["a_rt"], 1)
                elif what == "gso":
                    act.wait_ge(s["gs_o"], 1)
                    n = HEADS * DB
                    act.copy(feat[:, 0:VB, SEQ:COLS].rearrange("p (k q) b -> p q k b", q=2),
                             T[:, :, 0:QB * DB].rearrange("p q (k b) -> p q k b", k=QB))
                    act.activation(gsq[:, 0:n].rearrange("p (q n) -> p q n", q=2), T[:, :, 0:QB * DB], ACT.Square).then_inc(s["gs_sq"], 1)
                elif what == "gsm":
                    n = HEADS * DB
                    act.wait_ge(s["gs_ms"], 1)
                    act.wait_ge(s["a_norm"], NT)
                    act.activation(grt[:, 0:n], X[:, 0, 0:n], ACT.Sqrt, scale=1.0 / DV, bias=epsb[:, 0:1]).then_inc(s["gs_rt"], 1)
                elif what == "ysplit":
                    act.wait_ge(s["big_done"], use(at[("g", VB - 1)]) + 1)
                    wait_read(act, at[("cb", CB - 1)])
                    for k in range(KB):
                        if k == CB:
                            act.wait_ge(s["g_used"], VB)
                            act.wait_ge(s["yg_done"], 1)
                        act.copy(act_hi[:, k, :], feat[:, (k + CB) % KB, :]).then_inc(s["ys_hi"], 1)
                elif what == "sq":
                    act.wait_ge(s["q_tr"], 1)
                    act.wait_ge(s["gs_out"], 16 * 2 * QB)
                    act.copy(qs.rearrange("p (a n) -> p a n", a=2), back[0:DB]).then_inc(s["q_ev"], 1)
                elif what == "smax":
                    act.wait_ge(s["q_mx"], 1)
                    act.activation(sps[:, :], back[0:DB * MH, 0, 0:MEM], ACT.Exp, scale=DH ** -0.5, bias=sst[:, 1:2],
                                   accum_out=sst[:, 2:3]).then_inc(s["q_ex"], 1)
                elif what == "sprob":
                    act.wait_ge(s["q_t3"], 1)
                    for b in range(DB):
                        ins = act.copy(pTz[:, :, b, b * MH:(b + 1) * MH],
                                       back[:, 1, 0:MB * DB * MH].rearrange("p (m e) -> p m e", m=MB)[:, :, b * MH:(b + 1) * MH])
                    ins.then_inc(s["q_pT"], 1)
                elif what == "sout":
                    act.wait_ge(s["q_o"], DB)
                    act.copy(so[:, 0:512], G[0][0:DB * MH, 0, :])
                    act.copy(so[:, 512:D], G[1][0:DB * MH, 0, :]).then_inc(s["so_ev"], 1)
                    act.wait_ge(s["so_tr"], 1)
                    for h in range(MH):
                        ins = act.copy(act_hi[:, 2 * h:2 * h + 2, SEQ:COLS], own_head(h))
                    ins.then_inc(s["q_ohi"], 1)
                elif what == "att":
                    def probs(t):
                        act.wait_ge(s["s_mx"], t + 1)
                        if t >= 2:
                            act.wait_ge(s["s_tr"], t - 1)
                        pair = (T[:, :, :], back)[t % 2]
                        for h in range(MH):
                            ins = act.activation(pr[t % 2][:, h, :], pair[:, h // 2, (h % 2) * MEM:(h % 2 + 1) * MEM], ACT.Exp,
                                                 scale=DH ** -0.5, bias=smx[:, t % 2, 1, h:h + 1],
                                                 accum_out=smx[:, t % 2, 2, h:h + 1])
                        ins.then_inc(s["s_e"], 1)
                    if i == 0:
                        probs(0)
                    if i + 1 < NT:
                        probs(i + 1)
                    act.wait_ge(s["s_tr"], i + 1)
                    if i == NT // 2:
                        act.wait_ge(s["s_pv"], KB)
                    c0 = (i % (NT // 2)) * P
                    act.copy(pT[:, :, c0:c0 + P], G[0][:, 1:3, :].rearrange("p a (e n) -> p (a e) n", n=P)).then_inc(s["s_pT"], 1)
                elif what == "pv":
                    for k in range(KB):
                        act.wait_ge(s["s_pv"], i * KB + k + 1)
                        act.copy(act_hi[:, k, i * HT:(i + 1) * HT], G[k % 2][:, 0, :]).then_inc(s["s_pvhi"], 1)
            act_moe(act)

        @block.vector
        def _(dve):
            link = links["dve"] = chain(dve, s["d_ch"])
            v = nc.vector

            def split_lo(n):
                width = blocks[n][2]
                dve.wait_ge(s["hi_done"], n + 1)
                v.tensor_tensor(w_lo[:, n % 2, :, 0:width], raw[:, n % RAW, :, 0:width], w_hi[:, n % 2, :, 0:width],
                                ALU.subtract).then_inc(s["split_done"], 1)

            def read_out(n):
                kind, b = kinds[n]
                u = use(n)
                if kind == "ch":
                    uu, y = tmp[1], feat[:, VB + b, :]
                    dve.wait_ge(s["big_done"], u + 1)
                    wait_read(dve, n - 1)
                    if b == 0:
                        dve.wait_ge(s["const_in"], N_CONST)
                        dve.wait_ge(s["st_ev"], 1)
                        link(v.memset(uu[:, 0:2], 0.0))
                    uc = chunks(uu[:, 2:2 + COLS])
                    v.tensor_tensor(uc, G[grp[u]][:, :, 0:CH], uc, ALU.mult).then_inc(free[grp[u]], 1)
                    wait_read(dve, n)
                    link(v.tensor_copy(uend[:, b, :], uu[:, SEQ:SEQ + 2 + DB]))
                    link(v.tensor_scalar(y[:, 0:SEQ], uu[:, 0:SEQ], cw[:, b, 0:1], None, ALU.mult))
                    link(v.scalar_tensor_tensor(y[:, 0:SEQ], uu[:, 1:1 + SEQ], cw[:, b, 1:2], y[:, 0:SEQ], ALU.mult, ALU.add))
                    link(v.scalar_tensor_tensor(y[:, 0:SEQ], uu[:, 2:2 + SEQ], cw[:, b, 2:3], y[:, 0:SEQ], ALU.mult, ALU.add))
                    st = stT[:, b, :].rearrange("p (b j) -> p b j", j=2)
                    ys = y[:, SEQ:COLS].rearrange("p (b o) -> p b o", o=1)
                    link(v.tensor_scalar(ys, st[:, :, 0:1], cw[:, b, 0:1], None, ALU.mult))
                    link(v.scalar_tensor_tensor(ys, st[:, :, 1:2], cw[:, b, 1:2], ys, ALU.mult, ALU.add))
                    v.scalar_tensor_tensor(y[:, SEQ:COLS], uu[:, 2 + SEQ:2 + COLS], cw[:, b, 2:3], y[:, SEQ:COLS], ALU.mult,
                                           ALU.add).then_inc(s["u_used"], 1)
                elif kind == "cb":
                    y = chunks(feat[:, VB + b, :])
                    dve.wait_ge(s["big_done"], u + 1)
                    dve.wait_ge(s["u_used"], b + 1)
                    v.tensor_tensor(y, G[grp[u]][:, :, 0:CH], y, ALU.mult).then_inc(free[grp[u]], 1)
                elif kind == "g":
                    wait_read(dve, n)
                    if b == 0:
                        dve.wait_ge(s["a_norm"], NT)
                    link(v.tensor_copy(gsil[:, b, :], tmp[1][:, SEQ:COLS]))
                    v.scalar_tensor_tensor(feat[:, b, 0:SEQ], feat[:, b, 0:SEQ], glag[:, b:b + 1], tmp[1][:, 0:SEQ],
                                           ALU.mult, ALU.mult).then_inc(s["g_used"], 1)

            def evac_lo(f, col0, r):
                dve.wait_ge(s["nhi_done"], f + 1)
                v.tensor_tensor(act_lo[:, :, col0:col0 + r], fwd[f % 2].rearrange("p a (k n) -> p (a k) n", n=P)[:, :, 0:r],
                                act_hi[:, :, col0:col0 + r], ALU.subtract).then_inc(s["nlo_done"], 1)

            def late(i):
                j, stage, t = nseq[i], i // TILES, i % TILES
                if stage < 2:
                    evac_lo(MB + j, t * P, rows[t])

            def residual(i):
                j, stage, t = nseq[i], i // TILES, i % TILES
                if stage == 0:
                    return
                r = rows[t]
                dve.wait_ge(s["back_done"], (stage - 1) * TILES + t + 1)
                dve.wait_ge(x_in[j % 2], 16 * (j // 2 + 1))
                x3 = xb[j % 2][0:r, :].rearrange("p (a n) -> p a n", a=2)
                out = xb[j % 2][0:r, :].rearrange("p (a n) -> p a n", a=2)
                v.tensor_tensor(out, back[0:r], x3, ALU.add).then_inc(s["res_done"], 1)

            def norm_step(i):
                j, stage, t = nseq[i], i // TILES, i % TILES
                r = rows[t]
                same = [x for x in norm_seq if x // TILES == stage]
                p = same.index(i)

                def mean_square(x):
                    jx, rx = nseq[x], rows[x % TILES]
                    dve.wait_ge(s["sq_done"], jx + 1)
                    v.tensor_scalar(ssum[0:rx, jx, 1:2], ssum[0:rx, jx, 0:1], 1.0 / D, EPS, ALU.mult, ALU.add).then_inc(s["ms_done"], 1)

                if p == 0:
                    residual(i)
                    dve.wait_ge(s["gain_in"], 16 * (stage + 1))
                    mean_square(i)
                dve.wait_ge(s["rt_done"], j + 1)
                link(v.reciprocal(ssum[0:r, j, 3:4], ssum[0:r, j, 2:3]))
                v.scalar_tensor_tensor(hb[j % 2][0:r, :], xb[j % 2][0:r, :], ssum[0:r, j, 3:4], gain[0:r, :],
                                       ALU.mult, ALU.mult).then_inc(s["h_done"], 1)
                if p + 1 < len(same):
                    residual(same[p + 1])
                if p > 0:
                    late(same[p - 1])
                if p + 1 < len(same):
                    mean_square(same[p + 1])
                else:
                    late(i)

            def bcast(ap, shape):
                return ap.to_broadcast(shape)

            link(v.memset(epsb[:, :], EPS))
            for what, i in order:
                if what == "mem":
                    evac_lo(i, i * P, P)
                    if i == 0:
                        split_lo(0)
                elif what in ("block", "begin", "end"):
                    if what != "end" and i + 1 < NBLK:
                        split_lo(i + 1)
                    if what != "begin":
                        read_out(i)
                elif what == "norm":
                    norm_step(i)
                elif what == "gate":
                    dve.wait_ge(s["masks_rdy"], 1)
                    for b in range(QB):
                        u = use_z(b)
                        dve.wait_ge(free[grp[u]], cnt[u] + 1)
                        v.scalar_tensor_tensor(tmp[b][:, 0:COLS], zT[:, b, :], -1.0, zT[:, b, :], ALU.mult, ALU.max).then_inc(s["z_abs"], 1)
                    for b in range(QB):
                        dve.wait_ge(s["z_ln"], b + 1)
                        link(v.scalar_tensor_tensor(zT[:, b, :], zT[:, b, :], 0.0, tmp[b][:, 0:COLS], ALU.min, ALU.subtract))
                        v.tensor_tensor_scan(zT[:, b, 0:SEQ], smask[:, :], zT[:, b, 0:SEQ], 0.0, ALU.mult, ALU.add).then_inc(s["la_done"], 1)
                elif what == "prep":
                    b = i
                    dve.wait_ge(s["la_done"], QB)
                    if b >= 1:
                        dve.wait_ge(s["p_e"], 4 * b)
                        dve.wait_ge(s["p_m"], 4 * b)
                    z3 = zT[:, b, 0:SEQ].rearrange("p (n c) -> p n c", c=CHUNK)
                    def c3(ap):
                        return ap[:, 0:SEQ].rearrange("p (n c) -> p n c", c=CHUNK)
                    v.tensor_tensor(c3(tmp[3]), bcast(z3[:, :, CHUNK - 1:CHUNK], [P, NCK, CHUNK]), z3, ALU.subtract).then_inc(s["p_d2"], 1)
                    v.tensor_tensor(c3(tmp[1]), z3, bcast(z3[:, :, CHUNK // 2:CHUNK // 2 + 1], [P, NCK, CHUNK]), ALU.subtract).then_inc(s["p_d1"], 1)
                    dve.wait_ge(s["p_e"], 4 * b + 1)
                    v.tensor_tensor(qe[:, b, :], qT[:, b, 0:SEQ], tmp[0][:, 0:SEQ], ALU.mult).then_inc(s["p_m"], 1)
                    dve.wait_ge(s["p_e"], 4 * b + 2)
                    dve.wait_ge(s["p_x"], QB + b + 1)
                    dve.wait_ge(s["p_d1"], b + 1)
                    dve.wait_ge(free[grp[use(at[("k", b)])]], cnt[use(at[("k", b)])] + 1)
                    v.tensor_tensor(zT[:, b, 0:SEQ], kT[:, b, 0:SEQ], tmp[3][:, 0:SEQ], ALU.mult).then_inc(s["p_m"], 1)
                    dve.wait_ge(s["p_e"], 4 * b + 3)
                    dve.wait_ge(s["p_m"], 4 * b + 1)
                    v.tensor_tensor(qT[:, b, 0:SEQ], qT[:, b, 0:SEQ], tmp[2][:, 0:SEQ], ALU.mult).then_inc(s["p_m"], 1)
                    dve.wait_ge(s["p_e"], 4 * b + 4)
                    dve.wait_ge(s["p_m"], 4 * b + 2)
                    v.tensor_tensor(kT[:, b, 0:SEQ], kT[:, b, 0:SEQ], tmp[1][:, 0:SEQ], ALU.mult).then_inc(s["p_m"], 1)
                    if b == QB - 1:
                        dve.wait_ge(s["p_m"], 4 * QB)
                        for a in Am:
                            link(v.memset(a, 0.0))
                        v.memset(S[:, 0, :, :], 0.0).then_inc(s["prep_done"], 1)
                elif what == "ga":
                    dve.wait_ge(s["a_mm"], i + 1)
                    v.copy_predicated(Am[i % 2], bcast(cmask[:, :].bitcast(I32).unsqueeze(1).unsqueeze(1), [P, 2, QB, P]),
                                      lower4).then_inc(s["a_cp"], 1)
                elif what == "gd":
                    t = i
                    dve.wait_ge(s["a_ds"], t + 1)
                    if t >= 2:
                        dve.wait_ge(s["a_o"], t - 1)
                    for c in range(2):
                        n = 2 * t + c
                        for k in range(QB):
                            ins = v.scalar_tensor_tensor(S[:, (n + 1) % 4, k, :], S[:, n % 4, k, :], dec[:, k, n:n + 1],
                                                         X[:, 1 + c, k * DV:(k + 1) * DV], ALU.mult, ALU.add)
                            if c == 0 or k == 0:
                                link(ins)
                            else:
                                ins.then_inc(s["a_S"], 1)
                    dve.wait_ge(s["a_S"], t + 1)
                elif what == "gm":
                    t = i
                    dve.wait_ge(s["a_rt"], t + 1)
                    link(v.reciprocal(grt[:, :], grt[:, :]))
                    o3 = feat[:, 0:VB, t * P:(t + 1) * P].rearrange("p (k q) n -> p q k n", q=2)
                    v.tensor_tensor(o3, o3, grt[:, :].rearrange("p (q k n) -> p q k n", q=2, k=QB), ALU.mult).then_inc(s["a_norm"], 1)
                elif what == "us":
                    dve.wait_ge(s["a_ds"], NT)
                    v.tensor_copy(sel_g, bcast(ident[0:DB, 0:DB].unsqueeze(2), [DB, DB, P])).then_inc(s["gs_a"], 1)
                elif what == "gsb":
                    for b in (i, i + 1):
                        dve.wait_ge(s["gs_bc"], b + 1)
                        for half in range(2):
                            r = slice(half * DK, (half + 1) * DK)
                            ins = v.tensor_tensor(KV[r, :, b, :],
                                                  T[r, b % 2, :].rearrange("p (k h v) -> p k h v", k=QB, h=2)[:, :, half, :],
                                                  bcast(kT[r, :, SEQ + b:SEQ + b + 1], [DK, QB, DV]), ALU.mult)
                            if half == 0:
                                link(ins)
                        ins.then_inc(s["gs_kv"], 1)
                    if i == DB - 2:
                        dve.wait_ge(s["gs_kv"], DB)
                        dve.wait_ge(s["gs_in"], 16 * QB)
                        for k in range(QB):
                            link(v.tensor_tensor(S0[:, k], S0[:, k], bcast(adec[:, k, :].unsqueeze(2), [P, DB, DV]), ALU.mult))
                        for k in range(QB):
                            ins = v.tensor_tensor(S0[:, k], S0[:, k], KV[:, k], ALU.add)
                            if k < QB - 1:
                                link(ins)
                        ins.then_inc(s["gs_sn"], 1)
                elif what == "gsm":
                    dve.wait_ge(s["gs_rt"], 1)
                    n = HEADS * DB
                    link(v.reciprocal(grt[:, 0:n], grt[:, 0:n]))
                    o3 = feat[:, 0:VB, SEQ:COLS].rearrange("p (k q) b -> p q k b", q=2)
                    link(v.tensor_tensor(o3, o3, grt[:, 0:n].rearrange("p (q k b) -> p q k b", q=2, k=QB), ALU.mult))
                elif what == "ysplit":
                    dve.wait_ge(s["g_used"], VB)
                    for h in range(VB):
                        ins = v.scalar_tensor_tensor(feat[:, h, SEQ:COLS], feat[:, h, SEQ:COLS], glag[:, h:h + 1], gsil[:, h, :],
                                                     ALU.mult, ALU.mult)
                        if h < VB - 1:
                            link(ins)
                    ins.then_inc(s["yg_done"], 1)
                    for k in range(KB):
                        dve.wait_ge(s["ys_hi"], k + 1)
                        v.tensor_tensor(act_lo[:, k, :], feat[:, (k + CB) % KB, :], act_hi[:, k, :], ALU.subtract).then_inc(s["ys_lo"], 1)
                elif what == "sq":
                    v.tensor_copy(sel_a, bcast(ident[0:DB, 0:DB].unsqueeze(2), [DB, DB, P])).then_inc(s["q_ev"], 1)
                elif what == "smax":
                    dve.wait_ge(s["q_sc"], 2 * DB)
                    link(v.memset(pTz, 0.0))
                    dve.wait_ge(s["q_t2"], 1)
                    link(v.reduce_max(sst[:, 0:1], back[0:DB * MH, 0, 0:MEM], AX.X))
                    v.tensor_scalar(sst[:, 1:2], sst[:, 0:1], -(DH ** -0.5), None, ALU.mult).then_inc(s["q_mx"], 1)
                    dve.wait_ge(s["q_ex"], 1)
                    link(v.reciprocal(sst[:, 3:4], sst[:, 2:3]))
                    v.tensor_scalar(sps[:, :], sps[:, :], sst[:, 3:4], None, ALU.mult).then_inc(s["q_pn"], 1)
                elif what == "sout":
                    dve.wait_ge(s["q_ohi"], 1)
                    for h in range(MH):
                        ins = v.tensor_tensor(act_lo[:, 2 * h:2 * h + 2, SEQ:COLS], own_head(h), act_hi[:, 2 * h:2 * h + 2, SEQ:COLS],
                                              ALU.subtract)
                    ins.then_inc(s["q_olo"], 1)
                elif what == "att":
                    def key_scores(b):
                        if b >= 1:
                            dve.wait_ge(s["q_sc"], 2 * b)
                        dve.wait_ge(s[f"kc_in{b % 2}"], 16 * (b // 2 + 1))
                        for c in range(2):
                            dve.wait_ge(s["q_bc"], 2 * b + c + 1)
                            if c == 1:
                                dve.wait_ge(s["q_sc"], 2 * b + 1)
                            for m in range(MB):
                                for j in range(2):
                                    h = 2 * c + j
                                    ins = v.tensor_tensor_reduce(out=kprod, in0=cache[b % 2][:, m, h * DH:(h + 1) * DH],
                                                                 in1=G[c][:, 0, j * DH:(j + 1) * DH], scale=1.0, scalar=0.0,
                                                                 op0=ALU.mult, op1=ALU.add,
                                                                 accum_out=ksc[:, m, b * MH + h:b * MH + h + 1])
                                    if not (m == MB - 1 and j == 1):
                                        link(ins)
                            ins.then_inc(s["q_sc"], 1)

                    def maxima(t):
                        dve.wait_ge(s["s_mm"], t + 1)
                        pair = (T[:, :, :], back)[t % 2]
                        link(v.reduce_max(smx[:, t % 2, 0, :], pair.rearrange("p a (h m) -> p (a h) m", m=MEM), AX.X))
                        v.tensor_scalar(smx[:, t % 2, 1, :], smx[:, t % 2, 0, :], -(DH ** -0.5), None, ALU.mult).then_inc(s["s_mx"], 1)
                    if i == 0:
                        maxima(0)
                    if i + 1 < NT:
                        maxima(i + 1)
                    dve.wait_ge(s["s_e"], i + 1)
                    link(v.reciprocal(smx[:, i % 2, 3, :], smx[:, i % 2, 2, :]))
                    v.tensor_tensor(pr[i % 2], pr[i % 2], bcast(smx[:, i % 2, 3, :].unsqueeze(2), [P, MH, MEM]), ALU.mult).then_inc(s["s_p"], 1)
                    if i < NT // 2:
                        for b in range(i * PER, (i + 1) * PER):
                            key_scores(b)
                elif what == "pv":
                    for k in range(KB):
                        dve.wait_ge(s["s_pvhi"], i * KB + k + 1)
                        v.tensor_tensor(act_lo[:, k, i * HT:(i + 1) * HT], G[k % 2][:, 0, :], act_hi[:, k, i * HT:(i + 1) * HT],
                                        ALU.subtract).then_inc(s["s_pvlo"], 1)
            dve_moe(dve)


_INS = ['x_prompt', 'x_sample', 'state_conv', 'state_gla', 'cache_mem_k', 'cache_mem_v', 'mem_prompt', 'norm_mix', 'w_in',
        'conv_w', 'gla_gate_up', 'gla_gate_b', 'gla_out_norm', 'w_out', 'norm_mem', 'w_q', 'w_k', 'w_v', 'w_o', 'norm_ffn',
        'router_group', 'router_group_b', 'router_expert', 'router_expert_b', 'w_gate', 'w_up', 'w_down', 'norm_final']
_OUTS = [(1, 1024, 1024), (8, 1, 1024), (1, 1, 2, 512), (1, 1, 4, 64, 128), (1, 1, 256, 4, 256), (1, 1, 256, 4, 256),
         (1, 8, 2, 512), (1, 8, 4, 64, 128)]


def kernel(**inputs):
    import numpy as _np
    import concourse.bacc as _bacc
    from concourse import mybir as _mybir
    from concourse.bass_utils import run_bass_kernel_spmd as _run

    nc = _bacc.Bacc("TRN2", target_bir_lowering=False, num_devices=1)
    arrays, args = {}, []
    for name in _INS:
        a = _np.ascontiguousarray(inputs[name])
        arrays[f"in_{name}_dram"] = a
        args.append(nc.dram_tensor(f"in_{name}_dram", a.shape, _mybir.dt.from_np(a.dtype), kind="ExternalInput").ap())
    for i, shape in enumerate(_OUTS):
        args.append(nc.dram_tensor(f"out_{i}_dram", shape, _mybir.dt.float32, kind="ExternalOutput").ap())
    build(nc, *args)
    r = _run(nc, [arrays], core_ids=[0])
    return tuple(r.results[0][f"out_{i}_dram"] for i in range(len(_OUTS)))
```
